# Optimizing a Trainium2 kernel written in Bass

```python
import jax
import jax.numpy as jnp
from jax import lax
import numpy as np
import jax, jax.numpy as jnp

D_MODEL = 1024
BATCH = 1
SEQ = 256
DEPTH = 1

HQ_A = 8
HKV_A = 2
DH_A = 64
WINDOW = 128
BLOCK_A = 128
H_B = 4
DK_B = 128
DV_B = 256
GK_RANK = 16
GATE_NORMALIZER = 16.0
CHUNK_B = 64
SUB_B = 16
D_FF = 2816
CONV_W = 3
EPS = 1e-6

QA_W = HQ_A * DH_A
KVA_W = HKV_A * DH_A
QKB_W = H_B * DK_B
VB_W = H_B * DV_B
SPLITS = (QA_W, KVA_W, KVA_W, QKB_W, QKB_W, VB_W, VB_W, GK_RANK, D_MODEL, D_MODEL)
IN_W = QA_W + 2 * KVA_W + 2 * QKB_W + 2 * VB_W + GK_RANK + 2 * D_MODEL


def rmsnorm(x, g):
    xf = x.astype(jnp.float32)
    y = xf * lax.rsqrt(jnp.mean(xf * xf, axis=-1, keepdims=True) + EPS)
    return (y * g.astype(jnp.float32)).astype(x.dtype)

def split_cols(z):
    idx = []
    acc = 0
    for w in SPLITS[:-1]:
        acc += w
        idx.append(acc)
    return jnp.split(z, idx, axis=-1)

def sliding_window_sink_attention(q, k, v, sinks):
    B, S = q.shape[0], q.shape[1]
    nb = S // BLOCK_A
    G = HQ_A // HKV_A
    qb = q.reshape(B, nb, BLOCK_A, HKV_A, G, DH_A)
    kb = k.reshape(B, nb, BLOCK_A, HKV_A, DH_A)
    vb = v.reshape(B, nb, BLOCK_A, HKV_A, DH_A)
    shift = lambda t: jnp.concatenate([jnp.zeros_like(t[:, :1]), t[:, :-1]], axis=1)
    kk = jnp.concatenate([shift(kb), kb], axis=2)
    vv = jnp.concatenate([shift(vb), vb], axis=2)
    s = jnp.einsum("bnqhgd,bnkhd->bnhgqk", qb, kk).astype(jnp.float32) * (DH_A ** -0.5)
    qpos = jnp.arange(BLOCK_A)[:, None]
    kpos = jnp.arange(2 * BLOCK_A)[None, :] - BLOCK_A
    band = (kpos <= qpos) & (kpos > qpos - WINDOW)
    kabs = (jnp.arange(nb) * BLOCK_A)[:, None, None] + kpos[None]
    mask = band[None] & (kabs >= 0)
    s = jnp.where(mask[None, :, None, None], s, -jnp.inf)
    sink = sinks.astype(jnp.float32).reshape(HKV_A, G)[None, None, :, :, None, None]
    m = jnp.maximum(jnp.max(s, axis=-1, keepdims=True), sink)
    p = jnp.exp(s - m)
    p = p / (jnp.sum(p, axis=-1, keepdims=True) + jnp.exp(sink - m))
    o = jnp.einsum("bnhgqk,bnkhd->bnqhgd", p.astype(v.dtype), vv)
    return o.reshape(B, S, QA_W)

def gla_chunked(q, k, v, gk):
    out_dtype = v.dtype
    f32 = jnp.float32
    B, S = q.shape[0], q.shape[1]
    N = S // CHUNK_B
    NS = CHUNK_B // SUB_B
    to_chunks = lambda t: t.astype(f32).reshape(B, N, CHUNK_B, H_B, t.shape[-1]).transpose(0, 3, 1, 2, 4)
    q = to_chunks(q) * (DK_B ** -0.5)
    k = to_chunks(k)
    v = to_chunks(v)
    b = jnp.cumsum(to_chunks(gk), axis=3)
    b_last = b[:, :, :, -1:]
    kv = jnp.einsum("bhncd,bhnce->bhnde", k * jnp.exp(b_last - b), v)
    decay = jnp.exp(b_last[:, :, :, 0])

    def step(state, inp):
        kv_n, d_n = inp
        return d_n[..., None] * state + kv_n, state

    _, s_prev = lax.scan(step, jnp.zeros((B, H_B, DK_B, DV_B), f32),
                         (jnp.moveaxis(kv, 2, 0), jnp.moveaxis(decay, 2, 0)))
    s_prev = jnp.moveaxis(s_prev, 0, 2)
    o_inter = jnp.einsum("bhncd,bhnde->bhnce", q * jnp.exp(b), s_prev)
    sub = lambda t: t.reshape(B, H_B, N, NS, SUB_B, t.shape[-1])
    qs, ks, bs = sub(q), sub(k), sub(b)
    r = bs[:, :, :, :, -1]
    lower = jnp.arange(NS)[:, None] > jnp.arange(NS)[None, :]
    dq = jnp.where(lower[:, :, None, None], bs[:, :, :, :, None] - r[:, :, :, None, :, None], 0.0)
    q_ref = qs[:, :, :, :, None] * jnp.exp(dq)
    k_ref = ks * jnp.exp(r[:, :, :, :, None] - bs)
    a_off = jnp.einsum("bhnijtd,bhnjsd->bhnijts", q_ref, k_ref)
    a_off = jnp.where(lower[:, :, None, None], a_off, 0.0)
    tri = jnp.arange(SUB_B)[:, None] >= jnp.arange(SUB_B)[None, :]
    dd = jnp.where(tri[:, :, None], bs[..., :, None, :] - bs[..., None, :, :], 0.0)
    a_diag = jnp.einsum("bhnitsd,bhnisd->bhnits", qs[..., :, None, :] * jnp.exp(dd), ks)
    a_diag = jnp.where(tri, a_diag, 0.0)
    a_blocks = a_off + jnp.eye(NS, dtype=f32)[:, :, None, None] * a_diag[:, :, :, :, None]
    a_intra = a_blocks.transpose(0, 1, 2, 3, 5, 4, 6).reshape(B, H_B, N, CHUNK_B, CHUNK_B)
    o = o_inter + jnp.einsum("bhnts,bhnse->bhnte", a_intra, v)
    return o.transpose(0, 2, 3, 1, 4).reshape(B, S, H_B, DV_B).astype(out_dtype)

def causal_dwconv(a, w, bias):
    y = lax.conv_general_dilated(a, w[:, None, :].astype(a.dtype), window_strides=(1,),
                                 padding=[(CONV_W - 1, 0)], dimension_numbers=("NWC", "WIO", "NWC"),
                                 feature_group_count=a.shape[-1])
    return y + bias

def first_inputs(seed: int = 0) -> dict:
    key = jax.random.key(seed)
    ks = jax.random.split(key, 17)
    nrm = lambda k, shape, scale: jax.random.normal(k, shape, jnp.float32) * scale
    return {
        "x": nrm(ks[0], (BATCH, SEQ, D_MODEL), 1.0),
        "ln_mix_g": 1.0 + nrm(ks[1], (DEPTH, D_MODEL), 0.05),
        "w_in": nrm(ks[2], (DEPTH, D_MODEL, IN_W), D_MODEL ** -0.5),
        "q_norm_g": 1.0 + nrm(ks[3], (DEPTH, DH_A), 0.05),
        "k_norm_g": 1.0 + nrm(ks[4], (DEPTH, DH_A), 0.05),
        "sinks": nrm(ks[5], (DEPTH, HQ_A), 1.0),
        "w_gk_up": nrm(ks[6], (DEPTH, GK_RANK, QKB_W), GK_RANK ** -0.5),
        "b_gk": nrm(ks[7], (DEPTH, QKB_W), 0.1),
        "gla_norm_g": 1.0 + nrm(ks[8], (DEPTH, DV_B), 0.05),
        "w_branch_a": nrm(ks[9], (DEPTH, QA_W, D_MODEL), QA_W ** -0.5),
        "w_branch_b": nrm(ks[10], (DEPTH, VB_W, D_MODEL), VB_W ** -0.5),
        "w_out": nrm(ks[11], (DEPTH, D_MODEL, D_MODEL), D_MODEL ** -0.5),
        "ln_ffn_g": 1.0 + nrm(ks[12], (DEPTH, D_MODEL), 0.05),
        "w_ffn_in": nrm(ks[13], (DEPTH, D_MODEL, 2 * D_FF), D_MODEL ** -0.5),
        "conv_w": nrm(ks[14], (DEPTH, CONV_W, D_FF), CONV_W ** -0.5),
        "conv_b": nrm(ks[15], (DEPTH, D_FF), 0.02),
        "w_ffn_out": nrm(ks[16], (DEPTH, D_FF, D_MODEL), D_FF ** -0.5),
    }

def first_block(x, ln_mix_g, w_in, q_norm_g, k_norm_g, sinks, w_gk_up, b_gk, gla_norm_g,
              w_branch_a, w_branch_b, w_out, ln_ffn_g, w_ffn_in, conv_w, conv_b, w_ffn_out):
    B, S = x.shape[0], x.shape[1]
    for l in range(DEPTH):
        h = rmsnorm(x, ln_mix_g[l])
        z = h @ w_in[l]
        qa, ka, va, qb, kb, vb, rb, gk_lr, ga, gb = split_cols(z)
        qa = rmsnorm(qa.reshape(B, S, HQ_A, DH_A), q_norm_g[l])
        ka = rmsnorm(ka.reshape(B, S, HKV_A, DH_A), k_norm_g[l])
        ya = sliding_window_sink_attention(qa, ka, va.reshape(B, S, HKV_A, DH_A), sinks[l])
        gk = jax.nn.log_sigmoid((gk_lr @ w_gk_up[l] + b_gk[l]).astype(jnp.float32)) / GATE_NORMALIZER
        yb = gla_chunked(qb.reshape(B, S, H_B, DK_B), kb.reshape(B, S, H_B, DK_B),
                         vb.reshape(B, S, H_B, DV_B), gk.reshape(B, S, H_B, DK_B))
        yb = rmsnorm(yb, gla_norm_g[l]) * jax.nn.silu(rb.reshape(B, S, H_B, DV_B))
        yb = yb.reshape(B, S, VB_W)
        merged = jax.nn.sigmoid(ga) * (ya @ w_branch_a[l]) + jax.nn.sigmoid(gb) * (yb @ w_branch_b[l])
        x = x + merged @ w_out[l]
        h = rmsnorm(x, ln_ffn_g[l])
        a, u = jnp.split(h @ w_ffn_in[l], 2, axis=-1)
        a = causal_dwconv(a, conv_w[l], conv_b[l])
        x = x + (jax.nn.silu(a) * u) @ w_ffn_out[l]
    return x


DEPTH_2 = 2

N_EVEN = (DEPTH_2 + 1) // 2
N_ODD = DEPTH_2 // 2

POOL_WINDOWS = (2, 4, 8, 16)
POOL_GROUPS = len(POOL_WINDOWS)
POOL_GROUP_DIM = D_MODEL // POOL_GROUPS

SSM_EXPAND = 2
SSM_D_INNER = SSM_EXPAND * D_MODEL
SSM_HEAD_DIM = 64
SSM_N_HEADS = SSM_D_INNER // SSM_HEAD_DIM
SSM_N_GROUPS = 8
SSM_HEADS_PER_GROUP = SSM_N_HEADS // SSM_N_GROUPS
SSM_D_STATE = 128
SSM_CONV = 4
SSM_CHUNK = 128
SSM_BC_DIM = SSM_N_GROUPS * SSM_D_STATE
SSM_CONV_DIM = SSM_D_INNER + 2 * SSM_BC_DIM
SSM_IN_DIM = SSM_D_INNER + SSM_CONV_DIM + SSM_N_HEADS

D_FF_DENSE = 2816
N_EXPERTS = 8
TOP_K = 2
D_FF_EXPERT = 3584

NORM_EPS = 1e-6
SSM_NORM_EPS = 1e-5
DT_MIN = 1e-3
DT_MAX = 1e-1


def rmsnorm_2(x, w, eps=NORM_EPS):
    xf = x.astype(jnp.float32)
    y = xf * lax.rsqrt(jnp.mean(xf * xf, axis=-1, keepdims=True) + eps)
    return (y * w.astype(jnp.float32)).astype(x.dtype)

def swiglu(t, w_gate, w_up, w_down):
    return jnp.matmul(jax.nn.silu(jnp.matmul(t, w_gate)) * jnp.matmul(t, w_up), w_down)

def pool_mixer(h, w_grp, scale):
    b, l, d = h.shape
    hf = h.astype(jnp.float32).reshape(b, l, POOL_GROUPS, POOL_GROUP_DIM)
    cs0 = jnp.pad(jnp.cumsum(hf, axis=1), ((0, 0), (1, 0), (0, 0), (0, 0)))
    pos = jnp.arange(l)
    outs = []
    for g, w in enumerate(POOL_WINDOWS):
        upper = cs0[:, 1:, g]
        lower = jnp.pad(cs0[:, :l + 1 - w, g], ((0, 0), (w - 1, 0), (0, 0)))
        count = jnp.minimum(pos + 1, w).astype(jnp.float32)[None, :, None]
        outs.append((upper - lower) / count - hf[:, :, g])
    p = jnp.stack(outs, axis=2)
    y = jnp.einsum('blgc,gce->blge', p, w_grp.astype(jnp.float32)).reshape(b, l, d)
    return (y * scale.astype(jnp.float32)).astype(h.dtype)

def ssd_scan(xs, dt, a, bm, cm):
    b, l = xs.shape[:2]
    nc = l // SSM_CHUNK

    def to_chunks(t):
        return jnp.moveaxis(t.reshape(b, nc, SSM_CHUNK, *t.shape[2:]), 1, 0)

    causal = jnp.tril(jnp.ones((SSM_CHUNK, SSM_CHUNK), dtype=bool))[None, :, :, None, None]

    def step(state, inp):
        x_c, dt_c, b_c, c_c = inp
        acs = jnp.cumsum(dt_c * a, axis=1)
        seg = acs[:, :, None] - acs[:, None, :]
        decay = jnp.exp(jnp.where(causal, seg, -jnp.inf))
        cb = jnp.einsum('bign,bjgn->bijg', c_c, b_c)
        w = cb[..., None] * decay * dt_c[:, None]
        y_diag = jnp.einsum('bijgr,bjgrp->bigrp', w, x_c)
        y_off = jnp.einsum('bign,bgrpn->bigrp', c_c, state) * jnp.exp(acs)[..., None]
        to_end = jnp.exp(acs[:, -1:] - acs) * dt_c
        new_state = (state * jnp.exp(acs[:, -1])[..., None, None]
                     + jnp.einsum('bjgn,bjgr,bjgrp->bgrpn', b_c, to_end, x_c))
        return new_state, y_diag + y_off

    state0 = jnp.zeros((b, SSM_N_GROUPS, SSM_HEADS_PER_GROUP, SSM_HEAD_DIM, SSM_D_STATE), jnp.float32)
    _, y = lax.scan(step, state0, (to_chunks(xs), to_chunks(dt), to_chunks(bm), to_chunks(cm)))
    return jnp.moveaxis(y, 0, 1).reshape(xs.shape)

def ssd_mixer(h, w_in, conv_w, conv_b, dt_bias, a_log, d_skip, gate_norm_w, w_out):
    b, l, _ = h.shape
    f32 = jnp.float32
    zxbcdt = jnp.einsum('bld,de->ble', h, w_in).astype(f32)
    z = zxbcdt[..., :SSM_D_INNER]
    xbc = zxbcdt[..., SSM_D_INNER:SSM_D_INNER + SSM_CONV_DIM]
    dt = zxbcdt[..., SSM_D_INNER + SSM_CONV_DIM:]
    xbc = lax.conv_general_dilated(
        xbc, conv_w.astype(f32)[:, None, :], window_strides=(1,),
        padding=[(SSM_CONV - 1, 0)], dimension_numbers=('NWC', 'WIO', 'NWC'),
        feature_group_count=SSM_CONV_DIM) + conv_b.astype(f32)
    xbc = jax.nn.silu(xbc)
    xs = xbc[..., :SSM_D_INNER].reshape(b, l, SSM_N_GROUPS, SSM_HEADS_PER_GROUP, SSM_HEAD_DIM)
    bm = xbc[..., SSM_D_INNER:SSM_D_INNER + SSM_BC_DIM].reshape(b, l, SSM_N_GROUPS, SSM_D_STATE)
    cm = xbc[..., SSM_D_INNER + SSM_BC_DIM:].reshape(b, l, SSM_N_GROUPS, SSM_D_STATE)
    dt = jax.nn.softplus(dt + dt_bias.astype(f32)).reshape(b, l, SSM_N_GROUPS, SSM_HEADS_PER_GROUP)
    a = -jnp.exp(a_log.astype(f32)).reshape(SSM_N_GROUPS, SSM_HEADS_PER_GROUP)
    y = ssd_scan(xs, dt, a, bm, cm)
    y = y + d_skip.astype(f32).reshape(SSM_N_GROUPS, SSM_HEADS_PER_GROUP)[..., None] * xs
    y = y.reshape(b, l, SSM_D_INNER)
    y = rmsnorm_2(y * jax.nn.silu(z), gate_norm_w, SSM_NORM_EPS)
    return jnp.einsum('ble,ed->bld', y.astype(h.dtype), w_out).astype(h.dtype)

def moe_swiglu(h, w_router, w_gate, w_up, w_down):
    b, l, d = h.shape
    t = h.reshape(b * l, d)
    logits = jnp.matmul(t, w_router).astype(jnp.float32)
    top_val, top_idx = lax.top_k(logits, TOP_K)
    gates = jax.nn.softmax(top_val, axis=-1)
    combine = jnp.sum(jax.nn.one_hot(top_idx, N_EXPERTS, dtype=jnp.float32) * gates[..., None], axis=1)
    out = jnp.zeros((b * l, d), jnp.float32)
    for e in range(N_EXPERTS):
        y_e = swiglu(t, w_gate[e], w_up[e], w_down[e]).astype(jnp.float32)
        out = out + combine[:, e:e + 1] * y_e
    return out.reshape(b, l, d).astype(h.dtype)

def second_inputs(seed: int = 0) -> dict:
    key = jax.random.key(seed)
    ks = jax.random.split(key, 32)
    f32 = jnp.float32

    def nrm(k, shape, fan_in):
        return jax.random.normal(k, shape, f32) * (fan_in ** -0.5)

    def gain(k, shape):
        return 1.0 + 0.1 * jax.random.normal(k, shape, f32)

    dt0 = jnp.exp(jax.random.uniform(ks[14], (N_ODD, SSM_N_HEADS), f32)
                  * (np.log(DT_MAX) - np.log(DT_MIN)) + np.log(DT_MIN))
    dt_bias = dt0 + jnp.log(-jnp.expm1(-dt0))
    return {
        "x": jax.random.normal(ks[0], (BATCH, SEQ, D_MODEL), f32),
        "pool_norm_w": gain(ks[1], (N_EVEN, D_MODEL)),
        "pool_w": nrm(ks[2], (N_EVEN, POOL_GROUPS, POOL_GROUP_DIM, POOL_GROUP_DIM), POOL_GROUP_DIM),
        "pool_scale": 0.5 + 0.05 * jax.random.normal(ks[3], (N_EVEN, D_MODEL), f32),
        "dense_norm_w": gain(ks[4], (N_EVEN, D_MODEL)),
        "dense_w_gate": nrm(ks[5], (N_EVEN, D_MODEL, D_FF_DENSE), D_MODEL),
        "dense_w_up": nrm(ks[6], (N_EVEN, D_MODEL, D_FF_DENSE), D_MODEL),
        "dense_w_down": nrm(ks[7], (N_EVEN, D_FF_DENSE, D_MODEL), D_FF_DENSE),
        "ssd_norm_w": gain(ks[8], (N_ODD, D_MODEL)),
        "ssd_w_in": nrm(ks[9], (N_ODD, D_MODEL, SSM_IN_DIM), D_MODEL),
        "ssd_conv_w": 0.5 * jax.random.normal(ks[10], (N_ODD, SSM_CONV, SSM_CONV_DIM), f32),
        "ssd_conv_b": 0.02 * jax.random.normal(ks[11], (N_ODD, SSM_CONV_DIM), f32),
        "ssd_dt_bias": dt_bias,
        "ssd_a_log": jnp.log(jax.random.uniform(ks[12], (N_ODD, SSM_N_HEADS), f32, 1.0, 16.0)),
        "ssd_d": gain(ks[13], (N_ODD, SSM_N_HEADS)),
        "ssd_gate_norm_w": gain(ks[15], (N_ODD, SSM_D_INNER)),
        "ssd_w_out": nrm(ks[16], (N_ODD, SSM_D_INNER, D_MODEL), SSM_D_INNER),
        "moe_norm_w": gain(ks[17], (N_ODD, D_MODEL)),
        "moe_w_router": nrm(ks[18], (N_ODD, D_MODEL, N_EXPERTS), D_MODEL),
        "moe_w_gate": nrm(ks[19], (N_ODD, N_EXPERTS, D_MODEL, D_FF_EXPERT), D_MODEL),
        "moe_w_up": nrm(ks[20], (N_ODD, N_EXPERTS, D_MODEL, D_FF_EXPERT), D_MODEL),
        "moe_w_down": nrm(ks[21], (N_ODD, N_EXPERTS, D_FF_EXPERT, D_MODEL), D_FF_EXPERT),
        "final_norm_w": gain(ks[22], (D_MODEL,)),
    }

def second_block(x, pool_norm_w, pool_w, pool_scale, dense_norm_w, dense_w_gate, dense_w_up,
              dense_w_down, ssd_norm_w, ssd_w_in, ssd_conv_w, ssd_conv_b, ssd_dt_bias,
              ssd_a_log, ssd_d, ssd_gate_norm_w, ssd_w_out, moe_norm_w, moe_w_router,
              moe_w_gate, moe_w_up, moe_w_down, final_norm_w):
    for i in range(DEPTH_2):
        j = i // 2
        if i % 2 == 0:
            x = x + pool_mixer(rmsnorm_2(x, pool_norm_w[j]), pool_w[j], pool_scale[j])
            x = x + swiglu(rmsnorm_2(x, dense_norm_w[j]), dense_w_gate[j], dense_w_up[j],
                           dense_w_down[j]).astype(x.dtype)
        else:
            x = x + ssd_mixer(rmsnorm_2(x, ssd_norm_w[j]), ssd_w_in[j], ssd_conv_w[j], ssd_conv_b[j],
                              ssd_dt_bias[j], ssd_a_log[j], ssd_d[j], ssd_gate_norm_w[j], ssd_w_out[j])
            x = x + moe_swiglu(rmsnorm_2(x, moe_norm_w[j]), moe_w_router[j], moe_w_gate[j],
                               moe_w_up[j], moe_w_down[j])
    return rmsnorm_2(x, final_norm_w)


def setup_inputs(seed=0):
    out = dict(first_inputs(seed))
    for name, value in second_inputs(seed + 1).items():
        if name != "x":
            out[name + "_2"] = value
    return out


def reference(
    x, ln_mix_g, w_in, q_norm_g, k_norm_g, sinks, w_gk_up, b_gk, gla_norm_g, w_branch_a,
    w_branch_b, w_out, ln_ffn_g, w_ffn_in, conv_w, conv_b, w_ffn_out, pool_norm_w_2, pool_w_2,
    pool_scale_2, dense_norm_w_2, dense_w_gate_2, dense_w_up_2, dense_w_down_2, ssd_norm_w_2,
    ssd_w_in_2, ssd_conv_w_2, ssd_conv_b_2, ssd_dt_bias_2, ssd_a_log_2, ssd_d_2,
    ssd_gate_norm_w_2, ssd_w_out_2, moe_norm_w_2, moe_w_router_2, moe_w_gate_2, moe_w_up_2,
    moe_w_down_2, final_norm_w_2,
):
    x = first_block(
        x, ln_mix_g, w_in, q_norm_g, k_norm_g, sinks, w_gk_up, b_gk, gla_norm_g, w_branch_a,
        w_branch_b, w_out, ln_ffn_g, w_ffn_in, conv_w, conv_b, w_ffn_out,
    )
    return second_block(
        x, pool_norm_w_2, pool_w_2, pool_scale_2, dense_norm_w_2, dense_w_gate_2, dense_w_up_2,
        dense_w_down_2, ssd_norm_w_2, ssd_w_in_2, ssd_conv_w_2, ssd_conv_b_2, ssd_dt_bias_2,
        ssd_a_log_2, ssd_d_2, ssd_gate_norm_w_2, ssd_w_out_2, moe_norm_w_2, moe_w_router_2,
        moe_w_gate_2, moe_w_up_2, moe_w_down_2, final_norm_w_2,
    )


_drawn_inputs = setup_inputs


def setup_inputs(seed=0):
    import zlib

    import numpy as np

    out = dict(_drawn_inputs(seed))
    spreads = {}
    factors = {'q_norm_g': 2.897, 'k_norm_g': 3.176, 'sinks': 9.761, 'conv_b': 2.866}
    for name, (base, spread) in spreads.items():
        noise = np.random.default_rng([zlib.crc32(name.encode()), seed]).standard_normal(out[name].shape)
        drawn = base * np.exp(spread * noise) if base else spread * noise
        out[name] = jnp.asarray(drawn.astype(out[name].dtype))
    for name, factor in factors.items():
        out[name] = (out[name] * factor).astype(out[name].dtype)
    return out
```

```python
import concourse.bass as bass
from concourse import mybir
from contextlib import ExitStack

F32 = mybir.dt.float32
F32R = mybir.dt.float32r
BF16 = mybir.dt.bfloat16
I32 = mybir.dt.int32
ALU = mybir.AluOpType
ACT = mybir.ActivationFunctionType
AX = mybir.AxisListType

P = 128
S = 256
T = S // P
D = 1024
DC = D // P
EPS, SSM_EPS = 1e-6, 1e-5

QA, KVA, QKB, VB, GKR = 512, 128, 512, 1024, 16
DH, HKV, GQ = 64, 2, 4
HB, DKB, DVB = 4, 128, 256
GATE_NORM = 16.0
C_KA, C_VA, C_QB = QA, QA + KVA, QA + 2 * KVA
C_KB, C_VB = C_QB + QKB, C_QB + 2 * QKB
C_RB = C_VB + VB
C_GK = C_RB + VB
C_GA = C_GK + GKR
C_GB = C_GA + D
IN_W = C_GB + D
FF = 2816
FFC = FF // P
CONV_W = 3

DI, BC, NH, NG, HPG, HD = 2048, 1024, 32, 8, 4, 64
XBC = DI + 2 * BC
XBCC = XBC // P
SCONV = 4

NE, FE = 8, 3584
MAX_TASKS = NE + (2 * S - NE) // P

UC = 2048
RAW, SPL = 6, 3
WB = 512


def schedule():
    first, at = {}, 0
    for name, n in (("in", 24), ("wa", 2), ("wb", 4), ("wo", 4), ("ffn0", 33), ("pool", 1), ("ffn1", 33),
                    ("dt", 1), ("xbc", 16), ("z", 8), ("sout", 8), ("moe", 0)):
        first[name] = at
        at += n
    return first


UNIT = schedule()
MOE_UNITS = 42

TURNS = (("mix", 4), ("ya", 2), ("yb", 4), ("merged", 4), ("ffn0", 4), ("pooled", 0), ("ffn1", 4), ("ssd", 4),
         ("y", 8))
TURN = {}
_at = 0
for _name, _n in TURNS:
    TURN[_name] = _at
    _at += _n


def bcast(ap, axis, n):
    a = ap.unsqueeze(axis)
    shape = list(a.shape)
    shape[axis] = n
    return a.to_broadcast(shape)


def block_kernel(nc, I, out, stop="all"):
    ctx = ExitStack()
    with ctx:
        def sb(name, shape, dt=F32):
            return ctx.enter_context(nc.sbuf_tensor(name, shape, dt))

        def sem(name):
            return ctx.enter_context(nc.semaphore(name))

        def rows(w):
            return w.rearrange("(k p) n -> p k n", p=P)

        w_in_v = rows(I["w_in"][0])
        wa_v, wb_v, wo_v = rows(I["w_branch_a"][0]), rows(I["w_branch_b"][0]), rows(I["w_out"][0])
        ffn_in_v = rows(I["w_ffn_in"][0])
        ffn_gate_v = (ffn_in_v[:, :, 0:FF], rows(I["dense_w_gate_2"][0]))
        ffn_up_v = (ffn_in_v[:, :, FF:2 * FF], rows(I["dense_w_up_2"][0]))
        ffn_down_v = (rows(I["w_ffn_out"][0]), rows(I["dense_w_down_2"][0]))
        pool_v = I["pool_w_2"][0].rearrange("g (k p) n -> p (g k) n", p=P)
        ssd_in_v, ssd_out_v = rows(I["ssd_w_in_2"][0]), rows(I["ssd_w_out_2"][0])
        moe_gate_v = I["moe_w_gate_2"][0].rearrange("e (k p) n -> p e k n", p=P)
        moe_up_v = I["moe_w_up_2"][0].rearrange("e (k p) n -> p e k n", p=P)
        moe_down_v = I["moe_w_down_2"][0].rearrange("e (k p) n -> p e k n", p=P)
        x_v = I["x"][0].rearrange("(t p) d -> p t d", p=P)
        out_v = out[0].rearrange("(t p) d -> p t d", p=P)

        raw = sb("raw", [P, RAW, UC])
        w_hi = sb("w_hi", [P, SPL, UC], F32R)
        w_lo = sb("w_lo", [P, SPL, UC], F32R)
        a0_hi = sb("a0_hi", [P, DC, S], F32R)
        a0_lo = sb("a0_lo", [P, DC, S], F32R)
        a1_hi = sb("a1_hi", [P, DC, S], F32R)
        a1_lo = sb("a1_lo", [P, DC, S], F32R)
        x = sb("x_res", [P, T, D])
        arena = sb("arena", [P, 15496])
        vec = sb("vec", [P, 3 * P])
        cst = sb("cst", [P, 7 * P + 1])
        lmask = sb("lmask", [P, 7, P], BF16)
        rowv = sb("rowv", [P, 8 + 3 * NH])
        stat = sb("stat", [P, 64])
        sm = sb("sm", [P, 9, T * NH])
        taps = sb("taps", [P, SCONV + 1, 4])
        wr = sb("wr", [P, DC, NE])
        tasks = sb("tasks", [1, 16], I32)

        ident, upper, lower, ones = (cst[:, k * P:(k + 1) * P] for k in range(4))
        amask = cst[:, 4 * P:6 * P]
        iota_row, iota_col = cst[:, 6 * P:7 * P], cst[:, 7 * P:7 * P + 1]
        wgk = sm[0:GKR, 0:8, :].rearrange("p a b -> p (a b)")
        sinks, dt_bias, a_log, d_skip = rowv[:, 0:8], rowv[:, 8:40], rowv[:, 40:72], rowv[:, 72:104]
        ss, sd, rstd = stat[:, 0:2], stat[:, 2:4], stat[:, 4:6]

        def region(at, *dims):
            n = 1
            for d in dims:
                n *= d
            v = arena[:, at:at + n]
            if len(dims) == 2:
                v = v.rearrange("p (a b) -> p a b", a=dims[0])
            if len(dims) == 3:
                v = v.rearrange("p (a b c) -> p a b c", a=dims[0], b=dims[1])
            return v

        V_MIX, V_FFN, V_CB, V_CW, V_BGK, V_G2, V_QG, V_KG, VA_N = 0, 8, 16, 38, 104, 108, 110, 111, 112
        V_POOL, V_DENSE, V_SSD, V_MOE, V_GN, V_SCB = (P + n for n in (0, 8, 16, 24, 32, 48))
        VB_N = 80
        V_SCW = 2 * P

        TMP = 11808
        z = region(0, T, IN_W)
        h = region(TMP, T, D)
        junk = region(TMP + T * D, D)
        vrow = region(0, 3, P)

        ps = [ctx.enter_context(nc.psum_tensor(f"ps{b}", [P, 512], F32)) for b in range(8)]

        raw_full = [sem(f"raw_full{k}") for k in range(RAW)]
        hi_done, lo_done, unit_used = sem("hi_done"), sem("lo_done"), sem("unit_used")
        s_x, s_vrow, s_rowv, s_small = sem("s_x"), sem("s_vrow"), sem("s_rowv"), sem("s_small")
        s_const, s_out = sem("s_const"), sem("s_out")
        s_vecT, s_vec = sem("s_vecT"), sem("s_vec")
        x_new, sq_sum, h_ready = sem("x_new"), sem("sq_sum"), sem("h_ready")
        turned, turn_hi, turn_lo = sem("turned"), sem("turn_hi"), sem("turn_lo")
        z_act, z_dve = sem("z_act"), sem("z_dve")

        N_CONST = 10 + 4 * 7

        class Chain:

            def __init__(self, eng, name, rounds=0, per=0):
                self.eng, self.sem, self.n, self.base, self.per = eng, sem(name), 0, rounds, per

            def link(self, ins):
                self.n += 1
                ins.then_inc(self.sem, 1)
                self.eng.wait_ge(self.sem, self.base * self.per + self.n)

            def again(self, rounds, per):
                self.n, self.base, self.per = 0, rounds, per

            def close(self):
                assert self.n == self.per, (self.n, self.per)

        block = ctx.enter_context(nc.Block())

        PHASES = ["mix", "ffn0", "pool", "ffn1", "ssd", "all"]
        level = PHASES.index(stop)

        UPD = {"mix": 4, "ffn0": 8, "pool": 12, "ffn1": 16, "ssd": 20}

        def used(u, rounds=0):
            return RAW * rounds + u + 1

        def load(sp, u, src, rounds=0, part=None):
            if u >= RAW:
                sp.wait_ge(lo_done, RAW * rounds + u - RAW + 1)
            k, n = src.shape[-2], src.shape[-1]
            dst = raw[:, u % RAW, 0:k * n].rearrange("p (k n) -> p k n", k=k) if part is None else part
            return sp.dma_start(dst, src).then_inc(raw_full[u % RAW], 16)

        LAST = [UNIT["ffn0"], UNIT["pool"], UNIT["ffn1"], UNIT["dt"], UNIT["moe"], UNIT["moe"] + 1000][level]

        def split_hi(act, u, rounds=0):
            if u >= LAST:
                return
            act.wait_ge(raw_full[u % RAW], 16 * rounds + 16 * (u // RAW + 1))
            if u >= SPL:
                act.wait_ge(unit_used, RAW * rounds + u - SPL + 1)
            nc.scalar.activation(w_hi[:, u % SPL, :], raw[:, u % RAW, :], ACT.Copy).then_inc(hi_done, 1)

        def split_lo(dve, u, rounds=0):
            if u >= LAST:
                return
            dve.wait_ge(hi_done, RAW * rounds + u + 1)
            nc.vector.tensor_tensor(w_lo[:, u % SPL, :], raw[:, u % RAW, :], w_hi[:, u % SPL, :].bitcast(F32),
                                    ALU.subtract).then_inc(lo_done, 1)

        def mm3(o, lh, ll, rh, rl, start, stop):
            nc.tensor.matmul(o, lh, rh, start=start, stop=False, skip_group_check=True)
            nc.tensor.matmul(o, lh, rl, start=False, stop=False, skip_group_check=True)
            return nc.tensor.matmul(o, ll, rh, start=False, stop=stop, skip_group_check=True)

        def mm_rows(pe, u, banks, rounds=0, n=WB):
            for half in range(2):
                pe.wait_ge(lo_done, RAW * rounds + u + half + 1)
                slot = (u + half) % SPL
                for k in range(4):
                    kc = 4 * half + k
                    for t in range(T):
                        cols = slice(k * n, (k + 1) * n)
                        last = mm3(banks[t][:, 0:n], a0_hi[:, kc, t * P:(t + 1) * P], a0_lo[:, kc, t * P:(t + 1) * P],
                                   w_hi[:, slot, cols], w_lo[:, slot, cols], kc == 0, kc == DC - 1)
                last.then_inc(unit_used, 1)

        def mm_cols(pe, u, outs, rounds=0, n=WB):
            for half in range(2):
                pe.wait_ge(lo_done, RAW * rounds + u + half + 1)
                slot = (u + half) % SPL
                for k in range(4):
                    kc = 4 * half + k
                    for f in range(n // P):
                        cols = slice(k * n + f * P, k * n + (f + 1) * P)
                        last = mm3(outs[f], w_hi[:, slot, cols], w_lo[:, slot, cols], a0_hi[:, kc, :], a0_lo[:, kc, :],
                                   kc == 0 and f % 2 == 0, kc == DC - 1)
                last.then_inc(unit_used, 1)

        def mm_down(pe, u, src_hi, src_lo, banks, first, last_one, rounds=0, tiles=T, nk=2):
            pe.wait_ge(lo_done, RAW * rounds + u + 1)
            slot = u % SPL
            for k in range(nk):
                for t in range(tiles):
                    lh, ll = src_hi[:, k, t * P:(t + 1) * P], src_lo[:, k, t * P:(t + 1) * P]
                    for half in range(2):
                        cols = slice(k * D + half * 512, k * D + (half + 1) * 512)
                        mm = mm3(banks[2 * t + half][:, :], lh, ll, w_hi[:, slot, cols], w_lo[:, slot, cols],
                                 first and k == 0, last_one and k == nk - 1)
            mm.then_inc(unit_used, 1)

        def norm_stat(act, width, eps):
            nc.scalar.activation(sd, ss, ACT.Sqrt, scale=1.0 / width, bias=eps).then_inc(sq_sum, 1)

        NORMS = ["mix", "ffn0", "pool", "ffn1", "ssd", "moe", "final"]

        def norm_act(act, name, chain):
            n = NORMS.index(name)
            if name == "mix":
                act.wait_ge(s_x, 16)
            elif name != "final":
                act.wait_ge(x_new, 4 * n)
            for t in range(T):
                chain.link(nc.scalar.activation(junk, x[:, t, :], ACT.Square, accum_out=ss[:, t:t + 1]))
            norm_stat(act, D, EPS)

        def norm_dve(dve, name, chain):
            n = NORMS.index(name)
            dve.wait_ge(sq_sum, n + 1 + (1 if name in ("moe", "final") else 0))
            chain.link(nc.vector.reciprocal(rstd, sd))
            if name == "final":
                return
            nc.vector.tensor_scalar(h[:, 0, :], x[:, 0, :], rstd[:, 0:1], None, ALU.mult)
            nc.vector.tensor_scalar(h[:, 1, :], x[:, 1, :], rstd[:, 1:2], None, ALU.mult).then_inc(h_ready, 1)

        def turn_pe(pe, name, src, chunks):
            for b in range(chunks // 2):
                g = TURN[name] + b
                if b >= 4:
                    pe.wait_ge(turn_lo, g - 3)
                for c in (2 * b, 2 * b + 1):
                    for t in range(T):
                        at = (c % 2) * S + t * P
                        last = nc.tensor.transpose(ps[b % 4][:, at:at + P], src[:, t, c * P:(c + 1) * P], ident)
                last.then_inc(turned, 1)

        def turn_act(act, name, dst_hi, chunks, gain):
            for b in range(chunks // 2):
                act.wait_ge(turned, TURN[name] + b + 1)
                if gain is None:
                    last = nc.scalar.activation(dst_hi(2 * b, 2), ps[b % 4][:, :].rearrange("p (c s) -> p c s", c=2),
                                                ACT.Copy)
                else:
                    for c in (2 * b, 2 * b + 1):
                        g = gain(c)
                        last = nc.scalar.activation(dst_hi(c, 1), ps[b % 4][:, (c % 2) * S:(c % 2 + 1) * S], ACT.Copy,
                                                    scale=vec[:, g:g + 1])
                last.then_inc(turn_hi, 1)

        def turn_dve(dve, name, dst_hi, dst_lo, chunks, gain):
            for b in range(chunks // 2):
                dve.wait_ge(turn_hi, TURN[name] + b + 1)
                if gain is None:
                    last = nc.vector.tensor_tensor(dst_lo(2 * b, 2), ps[b % 4][:, :].rearrange("p (c s) -> p c s", c=2),
                                                   dst_hi(2 * b, 2).bitcast(F32), ALU.subtract)
                else:
                    for c in (2 * b, 2 * b + 1):
                        g = gain(c)
                        last = nc.vector.scalar_tensor_tensor(dst_lo(c, 1), ps[b % 4][:, (c % 2) * S:(c % 2 + 1) * S],
                                                              vec[:, g:g + 1], dst_hi(c, 1).bitcast(F32),
                                                              ALU.mult, ALU.subtract)
                last.then_inc(turn_lo, 1)

        def chunks_of(buf):
            def at(c, n):
                return buf[:, c, :] if n == 1 else buf[:, c:c + n, :]
            return at

        def chunks_two(b0, b1):
            def at(c, n):
                buf, c = (b0, c) if c < DC else (b1, c - DC)
                return buf[:, c, :] if n == 1 else buf[:, c:c + n, :]
            return at

        at_sq, at_qkT = region(TMP, T, 640), region(TMP, 5, S)
        at_qn = region(TMP + 1280, T, 640)
        at_s = region(TMP + 1280, 4, S)
        at_pT = region(TMP + 2304, 8, P)
        ya = z[:, :, 0:QA]
        def tiles(v):
            return v.rearrange("p t (h i) -> p t h i", h=HB)
        g_b, g_acc, g_e = tiles(z[:, :, C_QB:C_QB + 512]), tiles(z[:, :, C_KB:C_KB + 512]), tiles(z[:, :, 0:512])
        g_q, g_k = region(TMP, T, HB, P), region(TMP + 1024, T, HB, P)
        g_qe = region(TMP + 2048, T, HB, P)
        g_lrT = region(TMP + 3072, T, P)
        g_f = (g_e[:, 0], g_e[:, 1], g_qe[:, 0], g_qe[:, 1])
        LEVELS = 7

        def halves(v, lv):
            m = 64 >> lv
            pairs = v.rearrange("p h (b r) -> p (h b) r", r=2 * m)
            return pairs[:, :, 0:m], pairs[:, :, m:2 * m], pairs[:, :, m - 1:m].to_broadcast([P, HB * P // (2 * m), m])

        g_kdT = region(TMP + 2048, HB, P)
        g_s0 = region(TMP + 2560, HB, DVB)
        g_o = region(TMP, T, D)
        merged = z[:, :, C_QB:C_QB + D]
        f_acc, f_sg, f_p = region(0, 4, S), region(1024, 4, S), region(2048, 4, S)
        p_hT, p_w0, p_w1, p_out = region(3072, DC, S), region(5120, 2, S), region(5632, 2, S), region(6144, DC, S)
        p_inv, p_scale = region(9216, 16), region(8192, D)
        cv = region(0, XBCC, S)
        zs = region(0, T, DI)
        xs = region(8192, T, DI)
        s_b0 = region(12288, NG, P)
        s_ex, s_cb = (region(13312, HPG, P), region(13824, HPG, P)), region(14336, P)
        s_xd, s_xe, s_st = (region(14464, HPG, HD), region(14720, HPG, HD)), region(14976, HPG, HD), region(15232, HPG, HD)
        ssd_junk = region(13312, DI)
        (dt, dta, acs, eacs, tend, ea, dskip2, lgt, lg2) = (sm[:, k, :] for k in range(9))
        c_acc = region(13312, 4, S)

        def cv_at(b):
            return cv[:, 4 * b:4 * b + 4, :]

        def cv_dyn(i, b):
            return arena[:, bass.ds(i * (12 * S) + 4 * b * S, 4 * S)].rearrange("p (c s) -> p c s", c=4)

        def xt_dst(r):
            if r < 8:
                return xs[:, r // 4, (r % 4) * 512:(r % 4 + 1) * 512]
            return s_b0[:, 4 * (r - 8):4 * (r - 8) + 4, :].rearrange("p g n -> p (g n)")

        SCAT = (6, 7, 2, 3)
        m_hT = region(0, DC, S)
        m_p, m_pt = region(2048, T, P), region(2304, T, P)
        m_gt, m_gt2 = region(2560, S), region(2816, S)
        m_bc = region(3072, 4, S)
        m_sg, m_act, m_y = region(4096, 512), region(4608, 512), region(5120, D)
        m_rt = region(6144, 24, T * NE)
        fin_w = region(8192, D)
        fin_o = region(9216, T, D)

        at_ss, at_sd, at_n, at_T, at_c = (sem("at_" + k) for k in ("ss", "sd", "n", "T", "c"))
        at_sc, at_m, at_e, at_pt, at_pc, at_o, at_y = (sem("at_" + k) for k in ("sc", "m", "e", "pt", "pc", "o", "y"))
        gl_T, gl_c, gl_g, gl_y, gl_l, gl_b = (sem("gl_" + k) for k in ("T", "c", "g", "y", "l", "b"))
        gl_d, gl_e, gl_p, gl_a, gl_m = (sem("gl_" + k) for k in ("d", "e", "p", "a", "m"))
        gl_i, gl_x, gl_k, gl_kT, gl_kc, gl_s, gl_sc, gl_o, gl_ss, gl_sd, gl_r, gl_on, gl_yb = (
            sem("gl_" + k) for k in ("i", "x", "k", "kT", "kc", "s", "sc", "o", "ss", "sd", "r", "on", "yb"))
        br_g, br_a, br_m = sem("br_g"), sem("br_a"), sem("br_m")
        f_one, f_tap, f_conv, f_silu, f_mult, f_hi, f_lo, f_vec = (
            sem("f_" + k) for k in ("one", "tap", "conv", "silu", "mult", "hi", "lo", "vec"))

        pl_T, pl_c, pl_p, pl_hi, pl_lo = (sem("pl_" + k) for k in ("T", "c", "p", "hi", "lo"))
        fin_done = sem("fin_done")
        sd_y, sd_l, sd_dta, sd_acs, sd_te, sd_ex = (sem("sd_" + k) for k in ("y", "l", "dta", "acs", "te", "ex"))
        c_vec, c_tap, c_one, c_two, c_conv, c_silu = (sem("c_" + k) for k in ("vec", "tap", "one", "two", "conv", "silu"))
        xt_ps, xt_act, xt_dve, zs_done = sem("xt_ps"), sem("xt_act"), sem("xt_dve"), sem("zs_done")
        st_skip, st_xd, st_seg, st_ex, st_cb, st_w, st_y, st_s, st_sc, st_acc = (
            sem("st_" + k) for k in ("skip", "xd", "seg", "ex", "cb", "w", "y", "s", "sc", "acc"))
        sy_gated, sy_done = sem("sy_gated"), sem("sy_done")
        r_T, r_h, r_lg, r_m, r_e, r_g, r_rank, r_tab, r_diag, r_bc = (
            sem("r_" + k) for k in ("T", "h", "lg", "m", "e", "g", "rank", "tab", "diag", "bc"))
        m_pk, m_gt_done, m_gather, m_ahi, m_alo, m_silu, m_mult, m_tr, m_phi, m_plo, m_y_done, m_scat = (
            sem("m_" + k) for k in ("p", "gt", "gather", "ahi", "alo", "silu", "mult", "tr", "phi", "plo", "y", "scat"))
        up_tail = sem("up_tail")
        pool_in = sem("pool_in")

        @block.gpsimd
        def _(pool):
            n = [0]

            def link(ins):
                n[0] += 1
                ins.then_inc(s_const, 1)
                pool.wait_ge(s_const, n[0])

            link(nc.gpsimd.memset(cst[:, 0:3 * P], 0.0))
            link(nc.gpsimd.memset(ones, 1.0))
            link(nc.gpsimd.memset(amask, 0.0))
            link(nc.gpsimd.affine_select(out=ident, in_=ident, compare_op=ALU.not_equal, fill=1.0, base=0,
                                         pattern=[[-1, P]], channel_multiplier=1))
            link(nc.gpsimd.affine_select(out=upper, in_=upper, compare_op=ALU.is_gt, fill=1.0, base=0,
                                         pattern=[[-1, P]], channel_multiplier=1))
            link(nc.gpsimd.affine_select(out=lower, in_=lower, compare_op=ALU.is_ge, fill=1.0, base=0,
                                         pattern=[[1, P]], channel_multiplier=-1))
            link(nc.gpsimd.affine_select(out=amask[:, 0:P], in_=amask[:, 0:P], compare_op=ALU.is_gt, fill=-3e38, base=0,
                                         pattern=[[1, P]], channel_multiplier=-1))
            link(nc.gpsimd.affine_select(out=amask[:, P:S], in_=amask[:, P:S], compare_op=ALU.is_ge, fill=-3e38, base=0,
                                         pattern=[[-1, P]], channel_multiplier=1))
            link(nc.gpsimd.iota(iota_row, pattern=[[1, P]], base=0, channel_multiplier=0,
                                allow_small_or_imprecise_dtypes=True))
            link(nc.gpsimd.iota(iota_col, pattern=[[0, 1]], base=0, channel_multiplier=1,
                                allow_small_or_imprecise_dtypes=True))
            for lv in range(7):
                m = 64 >> lv
                link(nc.gpsimd.memset(lmask[:, lv, :], 0.0))
                right = lmask[:, lv, :].rearrange("p (b r) -> p b r", r=2 * m)[:, :, m:2 * m]
                link(nc.gpsimd.memset(right, 1.0))
                link(nc.gpsimd.affine_select(out=right, in_=right, compare_op=ALU.is_ge, fill=0.0, base=0,
                                             pattern=[[-2 * m, P // (2 * m)], [0, m]], channel_multiplier=1))
                link(nc.gpsimd.affine_select(out=right, in_=right, compare_op=ALU.is_ge, fill=0.0, base=m - 1,
                                             pattern=[[2 * m, P // (2 * m)], [0, m]], channel_multiplier=-1))
            pool.wait_ge(gl_b, 1)
            for n in range(T * LEVELS):
                if n >= 4:
                    pool.wait_ge(gl_a, n - 1)
                left, right, middle = halves(g_b[:, n % 2], n // 2)
                to_left, to_right, _ = halves(g_f[n % 4], n // 2)
                nc.gpsimd.tensor_tensor(to_left, middle, left, ALU.subtract)
                nc.gpsimd.tensor_tensor(to_right, right, middle, ALU.subtract).then_inc(gl_d, 1)
            pool.wait_ge(gl_a, T * LEVELS + 1)
            nc.gpsimd.tensor_tensor(g_e[:, 0], g_b[:, 0, :, P - 1:P].to_broadcast([P, HB, P]), g_b[:, 0],
                                    ALU.subtract).then_inc(gl_i, 1)
            if level >= PHASES.index("pool"):
                pool.wait_ge(x_new, UPD["ffn0"])
                pool.dma_start(p_scale, I["pool_scale_2"].to_broadcast([P, D])).then_inc(pool_in, 16)
            if level >= 4:
                pool.wait_ge(sd_dta, 1)
                pool.wait_ge(sd_ex, 1)
                pool.wait_ge(xt_act, 5)
                pool.wait_ge(xt_dve, 5)
                pool.wait_ge(s_rowv, 64)
                for k in range(2 * NG):
                    g, t = k // 2, k % 2
                    heads = slice(t * NH + HPG * g, t * NH + HPG * (g + 1))
                    xv = xs[:, t, g * 256:(g + 1) * 256].rearrange("p (r e) -> p r e", r=HPG)
                    if k >= 2:
                        pool.wait_ge(st_y, k - 1)
                    nc.gpsimd.tensor_tensor(s_xd[k % 2], xv, bcast(dt[:, heads], 2, HD), ALU.mult).then_inc(st_xd, 1)
                    pool.wait_ge(st_xd, 3 * g + (1 if t == 0 else 3))
                    if t == 0:
                        if g:
                            pool.wait_ge(st_s, g)
                        nc.gpsimd.tensor_tensor(s_xe, s_xd[0], bcast(tend[:, heads], 2, HD), ALU.mult).then_inc(st_xd, 1)
                    nc.gpsimd.tensor_tensor(xv, xv, bcast(d_skip[:, HPG * g:HPG * (g + 1)], 2, HD),
                                            ALU.mult).then_inc(st_skip, 1)
            if level >= PHASES.index("all"):
                pool.wait_ge(x_new, UPD["ssd"])
                pool.dma_start(fin_w, I["final_norm_w_2"].unsqueeze(0).to_broadcast([P, D])).then_inc(pool_in, 16)


        @block.sync
        def _(sp):
            sp.dma_start(x[:, :, :], x_v).then_inc(s_x, 16)

            def in_block(u, cols, n=WB, rounds=0):
                for half in range(2):
                    load(sp, u + half, w_in_v[:, 4 * half:4 * half + 4, cols], rounds)

            u0 = UNIT["in"]
            for b in range(3):
                in_block(u0 + 2 * b, slice(b * WB, (b + 1) * WB))
            with sp.Fori(1, 3) as i:
                for b in range(3):
                    for half in range(2):
                        u = u0 + 2 * b + half
                        sp.wait_ge(lo_done, RAW * i + u - RAW + 1)
                        sp.dma_start(raw[:, u % RAW, :].rearrange("p (k n) -> p k n", k=4),
                                     w_in_v[:, 4 * half:4 * half + 4, bass.ds((3 * i + b) * WB, WB)]
                                     ).then_inc(raw_full[u % RAW], 16)
            for b in range(9, 12):
                n = min(WB, IN_W - b * WB)
                in_block(u0 + 2 * b, slice(b * WB, b * WB + n), n)
            for name, src, n in (("wa", wa_v, 2), ("wb", wb_v, 4), ("wo", wo_v, 4)):
                for k in range(n):
                    load(sp, UNIT[name] + k, src[:, 2 * k:2 * k + 2, :])

            def ffn(f):
                u0 = UNIT[f"ffn{f}"]
                gate, up, down = ffn_gate_v[f], ffn_up_v[f], ffn_down_v[f]

                def two(u, src, cols, rounds=0):
                    for half in range(2):
                        load(sp, u + half, src[:, 4 * half:4 * half + 4, cols], rounds)

                two(u0, gate, slice(0, WB))
                two(u0 + 2, up, slice(0, WB))
                with sp.Fori(0, 4) as i:
                    two(u0 + 4, gate, bass.ds(i * WB + WB, WB), i)
                    for half in range(2):
                        load(sp, u0 + 6 + half, down[:, bass.ds(4 * i + 2 * half, 2), :], i)
                    two(u0 + 8, up, bass.ds(i * WB + WB, WB), i)
                views = [raw[:, (u0 + 28 + half) % RAW, :].rearrange("p (k n) -> p k n", k=4) for half in range(2)]
                for half in range(2):
                    sp.wait_ge(lo_done, u0 + 28 + half - RAW + 1)
                    sp.dma_start(views[half][:, :, 256:512], up[:, 4 * half:4 * half + 4, 5 * WB:FF]
                                 ).then_inc(up_tail, 16)
                sp.wait_ge(up_tail, 32 * (f + 1))
                for half in range(2):
                    load(sp, u0 + 28 + half, gate[:, 4 * half:4 * half + 4, 5 * WB:FF],
                         part=views[half][:, :, 0:256])
                for k in range(3):
                    load(sp, u0 + 30 + k, down[:, 16 + 2 * k:18 + 2 * k, :])

            if level >= 1:
                ffn(0)
            if level >= 2:
                load(sp, UNIT["pool"], pool_v)
            if level >= 3:
                ffn(1)
            if level >= 4:
                load(sp, UNIT["dt"], ssd_in_v[:, :, DI + XBC:DI + XBC + NH])
                u0 = UNIT["xbc"]
                with sp.Fori(0, 2) as i:
                    for b in range(3):
                        for half in range(2):
                            load(sp, u0 + 2 * b + half,
                                 ssd_in_v[:, 4 * half:4 * half + 4, bass.ds(i * 3 * WB + DI + b * WB, WB)], i)
                for b in range(6, 8):
                    for half in range(2):
                        load(sp, u0 + 2 * b + half,
                             ssd_in_v[:, 4 * half:4 * half + 4, DI + b * WB:DI + (b + 1) * WB])
                for b in range(4):
                    for half in range(2):
                        load(sp, UNIT["z"] + 2 * b + half,
                             ssd_in_v[:, 4 * half:4 * half + 4, b * WB:(b + 1) * WB])
                for k in range(8):
                    load(sp, UNIT["sout"] + k, ssd_out_v[:, 2 * k:2 * k + 2, :])
            if level >= 5:
                M0 = UNIT["moe"]
                sp.wait_ge(r_tab, 1)
                n_tasks = sp.value_load(tasks[0:1, 15:16], min_val=1, max_val=MAX_TASKS)

                def moe_load(u, src, rounds):
                    sp.wait_ge(lo_done, RAW * rounds + (M0 + u - RAW + 1))
                    sp.dma_start(raw[:, (M0 + u) % RAW, :].rearrange("p (k n) -> p k n", k=src.shape[-2]),
                                 src).then_inc(raw_full[(M0 + u) % RAW], 16)

                with sp.Fori(0, n_tasks) as i:
                    e = sp.value_load(tasks[0:1, bass.ds(i, 1)], min_val=0, max_val=NE - 1)

                    def two(u, src, cols, rounds):
                        for half in range(2):
                            moe_load(u + half, src[:, bass.ds(e, 1), 4 * half:4 * half + 4, cols]
                                     .rearrange("p a k n -> p (a k) n"), rounds)

                    def down(u, k0, rounds):
                        for half in range(2):
                            moe_load(u + half, moe_down_v[:, bass.ds(e, 1), bass.ds(k0 + 2 * half, 2), :]
                                     .rearrange("p a k n -> p (a k) n"), rounds)

                    two(0, moe_gate_v, slice(0, WB), 7 * i)
                    two(2, moe_up_v, slice(0, WB), 7 * i)
                    with sp.Fori(1, 7) as j:
                        n = 7 * i + j - 1
                        two(4, moe_gate_v, bass.ds(j * WB, WB), n)
                        two(6, moe_up_v, bass.ds(j * WB, WB), n)
                        down(8, j * 4 - 4, n)
                    down(4, 24, 7 * i + 6)
                for u in range(2):
                    moe_load(u, moe_gate_v[:, 0, 4 * u:4 * u + 4, 0:WB], 7 * n_tasks)
            if level < 5:
                sp.wait_ge(x_new, 4 * (level + 1))
                sp.dma_start(out_v, x[:, :, :]).then_inc(s_out, 16)
            else:
                sp.wait_ge(fin_done, 1)
                sp.dma_start(out_v, fin_o).then_inc(s_out, 16)
            sp.wait_ge(s_out, 16)

        @block.scalar
        def _(act):
            C = Chain(act, "act_chain")
            def row(group, at, src):
                act.dma_start(vrow[at:at + src.shape[0], group, :], src).then_inc(s_vrow, 16)

            def as_rows(v):
                return v.rearrange("(c p) -> c p", p=P)

            row(0, V_MIX, as_rows(I["ln_mix_g"][0]))
            row(0, V_FFN, as_rows(I["ln_ffn_g"][0]))
            row(0, V_CB, as_rows(I["conv_b"][0]))
            row(0, V_CW, I["conv_w"][0].rearrange("w (c p) -> (w c) p", p=P))
            row(0, V_BGK, as_rows(I["b_gk"][0]))
            row(0, V_G2, as_rows(I["gla_norm_g"][0]))
            for at, name in ((V_QG, "q_norm_g"), (V_KG, "k_norm_g")):
                for half in range(2):
                    act.dma_start(vrow[at:at + 1, 0, half * DH:(half + 1) * DH], I[name]).then_inc(s_vrow, 16)
            row(1, V_POOL - P, as_rows(I["pool_norm_w_2"][0]))
            row(1, V_DENSE - P, as_rows(I["dense_norm_w_2"][0]))
            row(1, V_SSD - P, as_rows(I["ssd_norm_w_2"][0]))
            row(1, V_MOE - P, as_rows(I["moe_norm_w_2"][0]))
            row(1, V_GN - P, as_rows(I["ssd_gate_norm_w_2"][0]))
            row(1, V_SCB - P, as_rows(I["ssd_conv_b_2"][0]))
            row(2, 0, I["ssd_conv_w_2"][0].rearrange("w (c p) -> (w c) p", p=P))
            for dst, name in ((sinks, "sinks"), (dt_bias, "ssd_dt_bias_2"), (a_log, "ssd_a_log_2"),
                              (d_skip, "ssd_d_2")):
                act.dma_start(dst, I[name].to_broadcast([P, dst.shape[1]])).then_inc(s_rowv, 16)
            act.dma_start(wr[:, :, :], rows(I["moe_w_router_2"][0])).then_inc(s_small, 16)
            act.dma_start(wgk, I["w_gk_up"][0]).then_inc(s_small, 16)

            norm_act(act, "mix", C)
            act.wait_ge(s_vecT, 1)
            nc.scalar.activation(vec[:, 0:VA_N], ps[7][:, 0:VA_N], ACT.Copy)
            nc.scalar.activation(vec[:, P:P + VB_N], ps[7][:, P:P + VB_N], ACT.Copy)
            nc.scalar.activation(vec[:, 2 * P:3 * P], ps[7][:, 2 * P:3 * P], ACT.Copy).then_inc(s_vec, 1)
            act.wait_ge(s_vec, 1)
            turn_act(act, "mix", chunks_of(a0_hi), DC, lambda c: V_MIX + c)

            u0 = UNIT["in"]
            for u in range(2):
                split_hi(act, u0 + u)

            def in_block(b, rounds, cols, n=WB):
                for u in (u0 + 2 * b + 2, u0 + 2 * b + 3):
                    split_hi(act, u, rounds)
                act.wait_ge(unit_used, used(u0 + 2 * b + 1, rounds))
                nc.scalar.activation(z[:, 0, cols], ps[2 * (b % 3)][:, 0:n], ACT.Copy).then_inc(z_act, 1)

            with act.Fori(0, 3) as i:
                for b in range(3):
                    in_block(b, i, bass.ds(i * 3 * WB + b * WB, WB))
            for b in range(9, 12):
                n = min(WB, IN_W - b * WB)
                in_block(b, 0, slice(b * WB, b * WB + n), n)

            act.wait_ge(z_dve, 12)
            nc.scalar.activation(z[:, :, C_RB:C_RB + VB], z[:, :, C_RB:C_RB + VB], ACT.Silu).then_inc(gl_r, 1)
            act.wait_ge(at_ss, 1)
            nc.scalar.activation(stat[:, 28:48], stat[:, 8:28], ACT.Sqrt, scale=1.0 / DH, bias=EPS).then_inc(at_sd, 1)
            C.link(nc.scalar.mul(vec[:, V_QG:V_QG + 1], vec[:, V_QG:V_QG + 1], DH ** -0.5))
            act.wait_ge(at_T, 1)
            for c in range(5):
                g = V_QG if c < 4 else V_KG
                last = nc.scalar.activation(at_qkT[:, c, :], ps[c // 2][:, (c % 2) * S:(c % 2 + 1) * S], ACT.Copy,
                                            scale=vec[:, g:g + 1])
            last.then_inc(at_c, 1)
            for step in range(4):
                w = P if step < 2 else S
                act.wait_ge(at_m, step + 1)
                C.link(nc.scalar.activation(stat[:, 52:56], stat[:, 52:56], ACT.Exp))
                nc.scalar.activation(at_s[:, :, 0:w], at_s[:, :, 0:w], ACT.Exp).then_inc(at_e, 1)
                nb = w // P
                for k in range(nb):
                    act.wait_ge(at_pt, (step if step < 2 else 2 * step - 2) + k + 1)
                    nc.scalar.activation(at_pT[:, 4 * k:4 * k + 4, :],
                                         ps[5 + k][:, :].rearrange("p (c s) -> p c s", c=4),
                                         ACT.Copy).then_inc(at_pc, 1)
            turn_act(act, "ya", chunks_of(a1_hi), 4, None)

            act.wait_ge(gl_T, 1)
            for t in range(T):
                nc.scalar.mul(g_q[:, t, :, :], ps[t][:, :].rearrange("p (h i) -> p h i", h=HB), DKB ** -0.5)
                nc.scalar.activation(g_k[:, t, :, :], ps[2 + t][:, :].rearrange("p (h i) -> p h i", h=HB), ACT.Copy)
            nc.scalar.activation(g_lrT[0:GKR, :, :], ps[4][0:GKR, 0:S].rearrange("p (t i) -> p t i", t=T),
                                 ACT.Copy).then_inc(gl_c, 1)
            act.wait_ge(gl_y, 1)
            C.link(nc.scalar.activation(g_qe, g_e, ACT.Abs))
            C.link(nc.scalar.activation(g_qe, g_qe, ACT.Exp, scale=-1.0))
            nc.scalar.activation(g_qe, g_qe, ACT.Ln, bias=1.0).then_inc(gl_l, 1)
            nc.scalar.activation(z[:, :, C_GA:C_GA + 2 * D], z[:, :, C_GA:C_GA + 2 * D], ACT.Sigmoid).then_inc(br_g, 1)
            for n in range(T * LEVELS):
                act.wait_ge(gl_d, n + 1)
                nc.scalar.activation(g_f[n % 4], g_f[n % 4], ACT.Exp, scale=1.0 / GATE_NORM).then_inc(gl_e, 1)
            act.wait_ge(gl_i, 1)
            nc.scalar.activation(g_e[:, 0], g_e[:, 0], ACT.Exp, scale=1.0 / GATE_NORM)
            act.wait_ge(gl_a, T * LEVELS + 2)
            nc.scalar.activation(g_e[:, 1], g_b[:, 1], ACT.Exp, scale=1.0 / GATE_NORM).then_inc(gl_x, 1)
            act.wait_ge(gl_kT, 1)
            nc.scalar.activation(g_kdT, ps[4][:, :].rearrange("p (h i) -> p h i", h=HB), ACT.Copy).then_inc(gl_kc, 1)
            act.wait_ge(gl_s, 1)
            for k in range(2):
                last = nc.scalar.activation(g_s0[:, 2 * k:2 * k + 2, :],
                                            ps[5 + k][:, :].rearrange("p (h e) -> p h e", h=2), ACT.Copy)
            last.then_inc(gl_sc, 1)
            act.wait_ge(gl_o, 1)
            for t in range(T):
                for hh in range(HB):
                    last = nc.scalar.activation(junk[:, hh * DVB:(hh + 1) * DVB],
                                                ps[4 + 2 * t + hh // 2][:, (hh % 2) * DVB:(hh % 2 + 1) * DVB],
                                                ACT.Square, accum_out=stat[:, 8 + 4 * t + hh:9 + 4 * t + hh])
                C.link(last)
            nc.scalar.activation(stat[:, 28:36], stat[:, 8:16], ACT.Sqrt, scale=1.0 / DVB, bias=EPS).then_inc(gl_sd, 1)
            turn_act(act, "yb", chunks_of(a0_hi), DC, lambda c: V_G2 + c % 2)

            u0 = UNIT["wa"]
            for u in range(2, 12):
                split_hi(act, u0 + u)
                if u == 7:
                    turn_act(act, "merged", chunks_of(a1_hi), DC, None)

            def ffn(f):
                u0 = UNIT[f"ffn{f}"]
                norm_act(act, f"ffn{f}", C)
                turn_act(act, f"ffn{f}", chunks_of(a0_hi), DC, lambda c: (V_FFN if f == 0 else V_DENSE) + c)

                def first_tap(i, nf=4):
                    for fc in range(nf):
                        last = nc.scalar.activation(f_acc[:, fc, :], ps[fc // 2][:, (fc % 2) * S:(fc % 2 + 1) * S],
                                                    ACT.Identity, scale=taps[:, 2, fc:fc + 1],
                                                    bias=taps[:, 4, fc:fc + 1])
                        if fc % 2 == 1:
                            last.then_inc(f_tap, 1)

                def step(us, rounds, gate_unit, i, nf=4, dst=0, hi=True):
                    split_hi(act, us[0], rounds)
                    split_hi(act, us[1], rounds)
                    act.wait_ge(unit_used, used(gate_unit, rounds))
                    if f == 0:
                        act.wait_ge(f_vec, i + 1)
                        first_tap(i, nf)
                    for u in us[2:4]:
                        split_hi(act, u, rounds)
                    if f == 0:
                        act.wait_ge(f_conv, i + 1)
                        nc.scalar.activation(f_sg[:, 0:nf, :], f_acc[:, 0:nf, :], ACT.Silu).then_inc(f_silu, 1)
                    else:
                        for k in range(nf // 2):
                            last = nc.scalar.activation(f_sg[:, 2 * k:2 * k + 2, :],
                                                        ps[k][:, :].rearrange("p (c s) -> p c s", c=2), ACT.Silu)
                        last.then_inc(f_silu, 1)
                    for u in us[4:]:
                        split_hi(act, u, rounds)
                    act.wait_ge(f_mult, 6 * f + i + 1)
                    nc.scalar.activation(a1_hi[:, dst:dst + nf, :], f_p[:, 0:nf, :], ACT.Copy).then_inc(f_hi, 1)

                step([u0 + 2, u0 + 3, u0 + 4, u0 + 5], 0, u0 + 1, 0)
                with act.Fori(0, 4) as i:
                    step([u0 + 6 + k for k in range(6)], i, u0 + 5, i + 1)
                step([u0 + 30, u0 + 31], 0, u0 + 29, 5, 2, 4)
                for u in range(32, 35):
                    split_hi(act, u0 + u)

            if level >= 1:
                ffn(0)
            if level >= 2:
                norm_act(act, "pool", C)
                for b in range(4):
                    act.wait_ge(pl_T, b + 1)
                    for c in (2 * b, 2 * b + 1):
                        last = nc.scalar.activation(p_hT[:, c, :], ps[b][:, (c % 2) * S:(c % 2 + 1) * S], ACT.Copy,
                                                    scale=vec[:, V_POOL + c:V_POOL + c + 1])
                    last.then_inc(pl_c, 1)
                split_hi(act, UNIT["ffn1"] + 1)
                act.wait_ge(pl_p, 1)
                nc.scalar.activation(a1_hi[:, :, :], p_out, ACT.Copy).then_inc(pl_hi, 1)
            if level >= 3:
                ffn(1)
            if level >= 4:
                D0, X0, Z0, O0 = UNIT["dt"], UNIT["xbc"], UNIT["z"], UNIT["sout"]
                norm_act(act, "ssd", C)
                turn_act(act, "ssd", chunks_of(a0_hi), DC, lambda c: V_SSD + c)
                split_hi(act, X0 + 1)
                act.wait_ge(gl_g, 1)
                nc.scalar.activation(ea[:, 0:NH], a_log, ACT.Exp)
                act.wait_ge(sd_y, 1)
                C.link(nc.scalar.activation(lg2, lgt, ACT.Abs))
                C.link(nc.scalar.activation(lg2, lg2, ACT.Exp, scale=-1.0))
                nc.scalar.activation(lg2, lg2, ACT.Ln, bias=1.0).then_inc(sd_l, 1)
                split_hi(act, X0 + 2)

                def conv_block(b, rounds, blk, chunk):
                    split_hi(act, X0 + 2 * b + 3, rounds)
                    act.wait_ge(unit_used, used(X0 + 2 * b + 1, rounds))
                    act.wait_ge(c_vec, blk + 1)
                    for fc in range(4):
                        last = nc.scalar.activation(c_acc[:, fc, :], ps[2 * (b % 3) + fc // 2][:, (fc % 2) * S:(fc % 2 + 1) * S],
                                                    ACT.Identity, scale=taps[:, 3, fc:fc + 1],
                                                    bias=taps[:, 4, fc:fc + 1])
                        if fc % 2 == 1:
                            last.then_inc(c_tap, 1)
                    split_hi(act, X0 + 2 * b + 4, rounds)
                    act.wait_ge(c_conv, blk + 1)
                    nc.scalar.activation(chunk, c_acc, ACT.Silu).then_inc(c_silu, 1)
                    act.wait_ge(c_silu, blk + 1)

                with act.Fori(0, 2) as i:
                    for b in range(3):
                        conv_block(b, i, 3 * i + b, cv_dyn(i, b))
                for b in range(6, 8):
                    conv_block(b, 0, b, cv_at(b))
                act.wait_ge(sd_te, 1)
                nc.scalar.activation(eacs, acs, ACT.Exp)
                nc.scalar.activation(tend, tend, ACT.Exp).then_inc(sd_ex, 1)
                for r in range(0, 10, 2):
                    act.wait_ge(xt_ps, r + 1)
                    nc.scalar.activation(xt_dst(r), ps[r % 4][:, :], ACT.Copy).then_inc(xt_act, 1)
                for b in range(4):
                    split_hi(act, Z0 + 2 * b + 3)
                    split_hi(act, Z0 + 2 * b + 4)
                    act.wait_ge(unit_used, used(Z0 + 2 * b + 1))
                    for t in range(T):
                        last = nc.scalar.activation(zs[:, t, b * WB:(b + 1) * WB], ps[4 + 2 * (b % 2) + t][:, :], ACT.Silu)
                    last.then_inc(zs_done, 1)
                for k in range(2 * NG):
                    act.wait_ge(st_seg, k + 1)
                    if k >= 2:
                        act.wait_ge(st_y, k - 1)
                    g, t = k // 2, k % 2
                    for r in range(HPG):
                        hd = t * NH + HPG * g + r
                        last = nc.scalar.activation(s_ex[k % 2][:, r, :], ps[k % 2][:, r * P:(r + 1) * P], ACT.Relu,
                                                    scale=-1.0, bias=acs[:, hd:hd + 1])
                    C.link(last)
                    nc.scalar.activation(s_ex[k % 2], s_ex[k % 2], ACT.Exp, scale=-1.0).then_inc(st_ex, 1)
                    if k % 2 == 0:
                        act.wait_ge(st_s, k // 2 + 1)
                        nc.scalar.activation(s_st, ps[6][:, 0:256].rearrange("p (r e) -> p r e", r=HPG),
                                             ACT.Copy).then_inc(st_sc, 1)
                act.wait_ge(sy_gated, 1)
                for t in range(T):
                    C.link(nc.scalar.activation(ssd_junk, xs[:, t, :], ACT.Square, accum_out=ss[:, t:t + 1]))
                norm_stat(act, DI, SSM_EPS)
                turn_act(act, "y", chunks_two(a0_hi, a1_hi), 2 * DC, lambda c: V_GN + c)
                for u in range(3, 8):
                    split_hi(act, O0 + u)
            if level >= 5:
                M0 = UNIT["moe"]
                norm_act(act, "moe", C)
                for b in range(4):
                    act.wait_ge(r_T, b + 1)
                    for c in (2 * b, 2 * b + 1):
                        last = nc.scalar.activation(m_hT[:, c, :], ps[b][:, (c % 2) * S:(c % 2 + 1) * S], ACT.Copy,
                                                    scale=vec[:, V_MOE + c:V_MOE + c + 1])
                    last.then_inc(r_h, 1)
                act.wait_ge(r_m, 1)
                nc.scalar.activation(m_rt[:, 20, 0:T], m_rt[:, 20, 0:T], ACT.Exp).then_inc(r_e, 1)
                act.wait_ge(r_bc, 1)
                for k in range(2):
                    last = nc.scalar.activation(m_bc[:, 2 * k:2 * k + 2, :],
                                                ps[6 + k][:, :].rearrange("p (a s) -> p a s", a=2), ACT.Copy)
                last.then_inc(r_g, 1)
                split_hi(act, M0)
                split_hi(act, M0 + 1)

                def tokens_hi(i):
                    act.wait_ge(m_gather, i + 1)
                    for b in range(2):
                        for c in range(4 * b, 4 * b + 4):
                            last = nc.scalar.activation(a0_hi[:, c, 0:P], ps[b][:, (c % 4) * P:(c % 4 + 1) * P],
                                                        ACT.Copy, scale=vec[:, V_MOE + c:V_MOE + c + 1])
                        last.then_inc(m_ahi, 1)

                def product_hi(n):
                    act.wait_ge(m_tr, n + 1)
                    nc.scalar.activation(a1_hi[:, 0:4, 0:P], ps[0][:, :].rearrange("p (c s) -> p c s", c=4),
                                         ACT.Copy).then_inc(m_phi, 1)

                tokens_hi(0)
                n_tasks = act.value_load(tasks[0:1, 15:16], min_val=1, max_val=MAX_TASKS)
                with act.Fori(0, n_tasks) as i:
                    split_hi(act, M0 + 2, 7 * i)
                    split_hi(act, M0 + 3, 7 * i)
                    act.wait_ge(unit_used, used(M0 + 1, 7 * i))
                    nc.scalar.activation(m_sg, ps[2][:, :], ACT.Silu).then_inc(m_silu, 1)
                    split_hi(act, M0 + 4, 7 * i)
                    split_hi(act, M0 + 5, 7 * i)
                    with act.Fori(1, 7) as j:
                        n = 7 * i + j
                        split_hi(act, M0, n)
                        split_hi(act, M0 + 1, n)
                        act.wait_ge(unit_used, RAW * n + M0)
                        act.wait_ge(m_mult, n)
                        nc.scalar.activation(m_sg, ps[2][:, :], ACT.Silu).then_inc(m_silu, 1)
                        product_hi(n - 1)
                        for u in range(2, 6):
                            split_hi(act, M0 + u, n)
                    n = 7 * i + 6
                    product_hi(n)
                    split_hi(act, M0, n + 1)
                    split_hi(act, M0 + 1, n + 1)
                    act.wait_ge(unit_used, RAW * n + (M0 + 6))
                    for k in range(2):
                        last = nc.scalar.activation(m_y[:, k * 512:(k + 1) * 512], ps[4 + k][:, :], ACT.Copy)
                    last.then_inc(m_y_done, 1)
                    tokens_hi(i + 1)
                act.wait_ge(x_new, 4 * n_tasks + UPD["ssd"])
                norm_act(act, "final", C)

        @block.vector
        def _(dve):
            C = Chain(dve, "dve_chain")
            norm_dve(dve, "mix", C)
            dve.wait_ge(s_vec, 1)
            turn_dve(dve, "mix", chunks_of(a0_hi), chunks_of(a0_lo), DC, lambda c: V_MIX + c)

            u0 = UNIT["in"]
            for u in range(2):
                split_lo(dve, u0 + u)

            def in_block(b, rounds, cols, n=WB):
                for u in (u0 + 2 * b + 2, u0 + 2 * b + 3):
                    split_lo(dve, u, rounds)
                dve.wait_ge(unit_used, used(u0 + 2 * b + 1, rounds))
                nc.vector.tensor_copy(z[:, 1, cols], ps[2 * (b % 3) + 1][:, 0:n]).then_inc(z_dve, 1)

            with dve.Fori(0, 3) as i:
                for b in range(3):
                    in_block(b, i, bass.ds(i * 3 * WB + b * WB, WB))
            for b in range(9, 12):
                n = min(WB, IN_W - b * WB)
                in_block(b, 0, slice(b * WB, b * WB + n), n)

            dve.wait_ge(z_act, 12)
            dve.wait_ge(z_dve, 12)
            dve.wait_ge(s_rowv, 64)
            C.link(nc.vector.tensor_tensor(at_sq, z[:, :, 0:640], z[:, :, 0:640], ALU.mult))
            nc.vector.tensor_reduce(stat[:, 8:28].rearrange("p (t h) -> p t h", t=T),
                                    at_sq.rearrange("p t (h d) -> p t h d", d=DH), AX.X, ALU.add).then_inc(at_ss, 1)
            dve.wait_ge(at_sd, 1)
            C.link(nc.vector.reciprocal(stat[:, 28:48], stat[:, 28:48]))
            for t in range(T):
                r = stat[:, 28 + 10 * t:38 + 10 * t]
                for j in range(HKV):
                    nc.vector.tensor_tensor(at_qn[:, t, 0:QA].rearrange("p (c j d) -> p j c d", j=HKV, d=DH)[:, j],
                                            z[:, t, j * S:(j + 1) * S].rearrange("p (c d) -> p c d", d=DH),
                                            bcast(r[:, 4 * j:4 * j + 4], 2, DH), ALU.mult)
                last = nc.vector.tensor_tensor(at_qn[:, t, QA:640].rearrange("p (j d) -> p j d", d=DH),
                                               z[:, t, C_KA:C_VA].rearrange("p (j d) -> p j d", d=DH),
                                               bcast(r[:, 8:10], 2, DH), ALU.mult)
            last.then_inc(at_n, 1)
            for step in range(4):
                t, j = step // 2, step % 2
                w = P if t == 0 else S
                dve.wait_ge(at_sc, step + 1)
                if step:
                    dve.wait_ge(at_pt, 1 if step == 1 else (2 if step == 2 else 4))
                for hp in range(2):
                    C.link(nc.vector.tensor_tensor(
                        at_s[:, 2 * hp:2 * hp + 2, 0:w], ps[3 + hp][:, 0:2 * w].rearrange("p (c k) -> p c k", c=2),
                        bcast(amask[:, S - w:S], 1, 2), ALU.add))
                mx, sk, rs = stat[:, 48:52], stat[:, 52:56], stat[:, 56:60]
                C.link(nc.vector.tensor_reduce(mx, at_s[:, :, 0:w], AX.X, ALU.max))
                C.link(nc.vector.tensor_tensor(mx, mx, sinks[:, 4 * j:4 * j + 4], ALU.max))
                C.link(nc.vector.tensor_tensor(sk, sinks[:, 4 * j:4 * j + 4], mx, ALU.subtract))
                nc.vector.tensor_tensor(at_s[:, :, 0:w], at_s[:, :, 0:w], bcast(mx, 2, w),
                                        ALU.subtract).then_inc(at_m, 1)
                dve.wait_ge(at_e, step + 1)
                C.link(nc.vector.tensor_reduce(rs, at_s[:, :, 0:w], AX.X, ALU.add))
                C.link(nc.vector.tensor_tensor(rs, rs, sk, ALU.add))
                C.link(nc.vector.reciprocal(rs, rs))
                dve.wait_ge(at_o, step + 1)
                nc.vector.tensor_tensor(ya[:, t, j * S:(j + 1) * S].rearrange("p (c d) -> p c d", d=DH),
                                        ps[7][:, 0:S].rearrange("p (c d) -> p c d", d=DH),
                                        bcast(rs, 2, DH), ALU.mult).then_inc(at_y, 1)
            turn_dve(dve, "ya", chunks_of(a1_hi), chunks_of(a1_lo), 4, None)

            dve.wait_ge(gl_g, 1)
            for hh in range(HB):
                last = (nc.vector.tensor_scalar(g_e[:, :, hh, :], ps[5 + hh // 2][:, (hh % 2) * S:(hh % 2 + 1) * S]
                                               .rearrange("p (t i) -> p t i", t=T),
                                               vec[:, V_BGK + hh:V_BGK + hh + 1], None, ALU.add))
            last.then_inc(gl_y, 1)
            dve.wait_ge(gl_l, 1)
            for t in range(T):
                C.link(nc.vector.scalar_tensor_tensor(g_e[:, t], g_e[:, t], 0.0, g_qe[:, t], ALU.min, ALU.subtract))
            for t in range(T):
                for hh in range(HB):
                    last = nc.vector.tensor_tensor_scan(g_b[:, t, hh, :], ones, g_e[:, t, hh, :], 0.0,
                                                        ALU.mult, ALU.add)
            last.then_inc(gl_b, 1)
            for t in range(T):
                dve.wait_ge(gl_a, t + 1)
                nc.vector.tensor_tensor(g_acc[:, t], ps[t][:, :].rearrange("p (h i) -> p h i", h=HB),
                                        bcast(ident, 1, HB), ALU.mult).then_inc(gl_m, 1)

            def take(n):
                dve.wait_ge(gl_a, n + 3)
                dve.wait_ge(gl_m, n + 1)
                nc.vector.copy_predicated(g_acc[:, n % 2], bcast(lmask[:, n // 2, :].bitcast(mybir.dt.int16), 1, HB),
                                          ps[(n + 2) % 4][:, :].rearrange("p (h i) -> p h i", h=HB)).then_inc(gl_m, 1)

            for n in range(T * LEVELS):
                t, lv = n % 2, n // 2
                dve.wait_ge(gl_e, n + 1)
                left, right, _ = halves(g_f[n % 4], lv)
                nc.vector.tensor_tensor(left, halves(g_k[:, t], lv)[0], left, ALU.mult)
                nc.vector.tensor_tensor(right, halves(g_q[:, t], lv)[1], right, ALU.mult).then_inc(gl_p, 1)
                if n >= 2:
                    take(n - 2)
            dve.wait_ge(gl_x, 1)
            nc.vector.tensor_tensor(g_e[:, 0], g_k[:, 0], g_e[:, 0], ALU.mult)
            nc.vector.tensor_tensor(g_e[:, 1], g_q[:, 1], g_e[:, 1], ALU.mult).then_inc(gl_k, 1)
            for n in range(T * LEVELS - 2, T * LEVELS):
                take(n)
            dve.wait_ge(gl_sd, 1)
            C.link(nc.vector.reciprocal(stat[:, 28:36], stat[:, 28:36]))
            for t in range(T):
                for k in range(2):
                    last = (nc.vector.tensor_tensor(
                        g_o[:, t, k * 512:(k + 1) * 512].rearrange("p (h e) -> p h e", h=2),
                        ps[4 + 2 * t + k][:, :].rearrange("p (h e) -> p h e", h=2),
                        bcast(stat[:, 28 + 4 * t + 2 * k:30 + 4 * t + 2 * k], 2, DVB), ALU.mult))
            C.link(last)
            dve.wait_ge(gl_r, 1)
            nc.vector.tensor_tensor(g_o, g_o, z[:, :, C_RB:C_RB + VB], ALU.mult).then_inc(gl_yb, 1)
            turn_dve(dve, "yb", chunks_of(a0_hi), chunks_of(a0_lo), DC, lambda c: V_G2 + c % 2)

            u0 = UNIT["wa"]
            for u in range(2, 4):
                split_lo(dve, u0 + u)
            dve.wait_ge(br_g, 1)
            dve.wait_ge(unit_used, used(u0 + 1))
            for t in range(T):
                for half in range(2):
                    cols = slice(C_GA + half * 512, C_GA + (half + 1) * 512)
                    last = nc.vector.tensor_tensor(merged[:, t, half * 512:(half + 1) * 512], ps[4 + 2 * t + half][:, :],
                                                   z[:, t, cols], ALU.mult)
            C.link(last)
            for u in range(4, 8):
                split_lo(dve, u0 + u)
            dve.wait_ge(unit_used, used(UNIT["wb"] + 3))
            for t in range(T):
                for half in range(2):
                    at = slice(half * 512, (half + 1) * 512)
                    gb = z[:, t, C_GB + half * 512:C_GB + (half + 1) * 512]
                    C.link(nc.vector.tensor_tensor(gb, ps[2 * t + half][:, :], gb, ALU.mult))
                    last = nc.vector.tensor_tensor(merged[:, t, at], merged[:, t, at], gb, ALU.add)
            last.then_inc(br_m, 1)
            turn_dve(dve, "merged", chunks_of(a1_hi), chunks_of(a1_lo), DC, None)
            for u in range(8, 12):
                split_lo(dve, u0 + u)

            def update(u_last):
                dve.wait_ge(unit_used, used(u_last))
                for t in range(T):
                    for half in range(2):
                        at = slice(half * 512, (half + 1) * 512)
                        nc.vector.tensor_tensor(x[:, t, at], x[:, t, at], ps[4 + 2 * t + half][:, :],
                                                ALU.add).then_inc(x_new, 1)

            update(UNIT["wo"] + 3)

            def ffn(f):
                u0 = UNIT[f"ffn{f}"]
                norm_dve(dve, f"ffn{f}", C)
                turn_dve(dve, f"ffn{f}", chunks_of(a0_hi), chunks_of(a0_lo), DC,
                         lambda c: (V_FFN if f == 0 else V_DENSE) + c)

                def step(us, rounds, up_unit, i, nf=4, dst=0):
                    if f == 0:
                        for w in range(CONV_W):
                            nc.vector.tensor_copy(taps[:, w, 0:nf], vec[:, bass.ds(i * 4 + (V_CW + w * FFC), nf)])
                        nc.vector.tensor_copy(taps[:, 4, 0:nf], vec[:, bass.ds(i * 4 + V_CB, nf)]).then_inc(f_vec, 1)
                    split_lo(dve, us[0], rounds)
                    split_lo(dve, us[1], rounds)
                    if f == 0:
                        dve.wait_ge(f_vec, i + 1)
                        for tap in (1, 0):
                            sh = 2 - tap
                            for fc in range(nf):
                                if tap == 1 and fc % 2 == 0:
                                    dve.wait_ge(f_tap, i * 2 + fc // 2 + 1)
                                col = (fc % 2) * S
                                last = nc.vector.scalar_tensor_tensor(
                                    f_acc[:, fc, sh:S], ps[fc // 2][:, col:col + S - sh], taps[:, tap, fc:fc + 1],
                                    f_acc[:, fc, sh:S], ALU.mult, ALU.add)
                            if tap == 1:
                                last.then_inc(f_one, 1)
                                dve.wait_ge(f_one, i + 1)
                        last.then_inc(f_conv, 1)
                    for u in us[2:]:
                        split_lo(dve, u, rounds)
                    if f:
                        dve.wait_ge(f_lo, 6 * f + i)
                    dve.wait_ge(f_silu, 6 * f + i + 1)
                    dve.wait_ge(unit_used, used(up_unit, rounds))
                    for k in range(nf // 2):
                        last = nc.vector.tensor_tensor(f_p[:, 2 * k:2 * k + 2, :], f_sg[:, 2 * k:2 * k + 2, :],
                                                       ps[2 + k][:, :].rearrange("p (c s) -> p c s", c=2), ALU.mult)
                    last.then_inc(f_mult, 1)
                    dve.wait_ge(f_hi, 6 * f + i + 1)
                    nc.vector.tensor_tensor(a1_lo[:, dst:dst + nf, :], f_p[:, 0:nf, :],
                                            a1_hi[:, dst:dst + nf, :].bitcast(F32), ALU.subtract).then_inc(f_lo, 1)

                step([u0 + 2, u0 + 3, u0 + 4, u0 + 5], 0, u0 + 3, 0)
                with dve.Fori(0, 4) as i:
                    step([u0 + 6 + k for k in range(6)], i, u0 + 9, i + 1)
                step([u0 + 30, u0 + 31], 0, u0 + 29, 5, 2, 4)
                for u in range(32, 35):
                    split_lo(dve, u0 + u)
                update(u0 + 32)

            if level >= 1:
                ffn(0)
            if level >= 2:
                norm_dve(dve, "pool", C)
                dve.wait_ge(s_const, N_CONST)
                C.link(nc.vector.tensor_scalar(p_inv, iota_row[:, 0:16], 1.0, None, ALU.add))
                C.link(nc.vector.reciprocal(p_inv, p_inv))
                dve.wait_ge(pl_c, 4)
                for g in range(4):
                    w, src = 2 << g, p_hT[:, 2 * g:2 * g + 2, :]
                    m, flip = 1, 0
                    while m < w:
                        dst = (p_w0, p_w1)[flip]
                        C.link(nc.vector.tensor_copy(dst[:, :, 0:m], src[:, :, 0:m]))
                        C.link(nc.vector.tensor_tensor(dst[:, :, m:S], src[:, :, m:S], src[:, :, 0:S - m], ALU.add))
                        src, m, flip = dst, 2 * m, 1 - flip
                    C.link(nc.vector.tensor_tensor(src[:, :, 0:w - 1], src[:, :, 0:w - 1],
                                                   bcast(p_inv[:, 0:w - 1], 1, 2), ALU.mult))
                    C.link(nc.vector.tensor_scalar(src[:, :, w - 1:S], src[:, :, w - 1:S], 1.0 / w, None, ALU.mult))
                    C.link(nc.vector.tensor_tensor(p_out[:, 2 * g:2 * g + 2, :], src, p_hT[:, 2 * g:2 * g + 2, :],
                                                   ALU.subtract))
                nc.vector.tensor_copy(stat[:, 60:61], stat[:, 48:49]).then_inc(pl_p, 1)
                split_lo(dve, UNIT["ffn1"] + 1)
                dve.wait_ge(pl_hi, 1)
                nc.vector.tensor_tensor(a1_lo[:, :, :], p_out, a1_hi[:, :, :].bitcast(F32),
                                        ALU.subtract).then_inc(pl_lo, 1)
                dve.wait_ge(pool_in, 16)
                dve.wait_ge(unit_used, used(UNIT["pool"]))
                for t in range(T):
                    for half in range(2):
                        at = slice(half * 512, (half + 1) * 512)
                        o = p_hT.rearrange("p c s -> p (c s)")[:, (2 * t + half) * 512:(2 * t + half + 1) * 512]
                        C.link(nc.vector.tensor_tensor(o, ps[4 + 2 * t + half][:, :], p_scale[:, at], ALU.mult))
                        nc.vector.tensor_tensor(x[:, t, at], x[:, t, at], o, ALU.add).then_inc(x_new, 1)
            if level >= 3:
                ffn(1)
            if level >= 4:
                D0, X0, Z0, O0 = UNIT["dt"], UNIT["xbc"], UNIT["z"], UNIT["sout"]
                norm_dve(dve, "ssd", C)
                turn_dve(dve, "ssd", chunks_of(a0_hi), chunks_of(a0_lo), DC, lambda c: V_SSD + c)
                split_lo(dve, X0 + 1)
                dve.wait_ge(unit_used, used(D0))
                nc.vector.tensor_tensor(lgt.rearrange("p (t h) -> p t h", t=T),
                                        ps[6][:, 0:T * NH].rearrange("p (t h) -> p t h", t=T),
                                        bcast(dt_bias, 1, T), ALU.add).then_inc(sd_y, 1)
                split_lo(dve, X0 + 2)
                dve.wait_ge(sd_l, 1)
                C.link(nc.vector.scalar_tensor_tensor(dt, lgt, 0.0, lg2, ALU.max, ALU.add))
                nc.vector.scalar_tensor_tensor(dta.rearrange("p (t h) -> p t h", t=T),
                                               dt.rearrange("p (t h) -> p t h", t=T), -1.0, bcast(ea[:, 0:NH], 1, T),
                                               ALU.mult, ALU.mult).then_inc(sd_dta, 1)

                def block_taps(blk):
                    for w in range(SCONV):
                        nc.vector.tensor_copy(taps[:, w, 0:4], vec[:, bass.ds(blk * 4 + (V_SCW + w * XBCC), 4)])
                    nc.vector.tensor_copy(taps[:, 4, 0:4], vec[:, bass.ds(blk * 4 + V_SCB, 4)]).then_inc(c_vec, 1)

                def conv_block(b, rounds, blk):
                    split_lo(dve, X0 + 2 * b + 3, rounds)
                    dve.wait_ge(c_vec, blk + 1)
                    for tap, done in ((2, c_one), (1, c_two), (0, c_conv)):
                        sh = SCONV - 1 - tap
                        for fc in range(4):
                            if tap == 2 and fc % 2 == 0:
                                dve.wait_ge(c_tap, 2 * blk + fc // 2 + 1)
                            o = c_acc[:, fc, sh:S]
                            col = (fc % 2) * S
                            last = nc.vector.scalar_tensor_tensor(
                                o, ps[2 * (b % 3) + fc // 2][:, col:col + S - sh], taps[:, tap, fc:fc + 1], o,
                                ALU.mult, ALU.add)
                        last.then_inc(done, 1)
                        if tap:
                            dve.wait_ge(done, blk + 1)
                    split_lo(dve, X0 + 2 * b + 4, rounds)
                    if b < 7:
                        dve.wait_ge(c_conv, blk + 1)
                        block_taps(blk + 1)

                block_taps(0)
                with dve.Fori(0, 2) as i:
                    for b in range(3):
                        conv_block(b, i, 3 * i + b)
                for b in range(6, 8):
                    conv_block(b, 0, b)
                dve.wait_ge(sd_acs, 1)
                C.link(nc.vector.tensor_copy(acs, ps[7][:, 0:64]))
                nc.vector.tensor_tensor(tend, ps[7][:, 64:128], acs, ALU.subtract).then_inc(sd_te, 1)
                for r in range(1, 10, 2):
                    dve.wait_ge(xt_ps, r + 1)
                    nc.vector.tensor_copy(xt_dst(r), ps[r % 4][:, :]).then_inc(xt_dve, 1)
                for u in range(3, 11):
                    split_lo(dve, Z0 + u)
                dve.wait_ge(sd_ex, 1)

                def accumulate(k):
                    g, t = k // 2, k % 2
                    heads = slice(t * NH + HPG * g, t * NH + HPG * (g + 1))
                    xv = xs[:, t, g * 256:(g + 1) * 256].rearrange("p (r e) -> p r e", r=HPG)
                    dve.wait_ge(st_y, k + 1)
                    dve.wait_ge(st_skip, k + 1)
                    before = ps[7][:, 0:256].rearrange("p (r e) -> p r e", r=HPG)
                    if t:
                        nc.vector.tensor_tensor(before, before, bcast(eacs[:, heads], 2, HD), ALU.mult)
                    last = nc.vector.tensor_tensor(xv, xv, ps[4 + k % 2][:, 0:256].rearrange("p (r e) -> p r e", r=HPG),
                                                   ALU.add)
                    if t:
                        C.link(last)
                        last = nc.vector.tensor_tensor(xv, xv, before, ALU.add)
                    last.then_inc(st_acc, 1)

                for k in range(2 * NG):
                    dve.wait_ge(st_seg, k + 1)
                    if k:
                        dve.wait_ge(st_w, k)
                    nc.vector.tensor_tensor(s_cb, ps[2 + k % 2][:, 0:P], upper, ALU.mult).then_inc(st_cb, 1)
                    dve.wait_ge(st_ex, k + 1)
                    dve.wait_ge(st_cb, k + 1)
                    nc.vector.tensor_tensor(s_ex[k % 2], s_ex[k % 2], bcast(s_cb, 1, HPG), ALU.mult).then_inc(st_w, 1)
                    if k:
                        accumulate(k - 1)
                accumulate(2 * NG - 1)
                dve.wait_ge(st_acc, 2 * NG)
                dve.wait_ge(zs_done, 4)
                nc.vector.tensor_tensor(xs, xs, zs, ALU.mult).then_inc(sy_gated, 1)
                dve.wait_ge(sq_sum, 6)
                C.link(nc.vector.reciprocal(rstd, sd))
                for t in range(T):
                    last = nc.vector.tensor_scalar(xs[:, t, :], xs[:, t, :], rstd[:, t:t + 1], None, ALU.mult)
                last.then_inc(sy_done, 1)
                turn_dve(dve, "y", chunks_two(a0_hi, a1_hi), chunks_two(a0_lo, a1_lo), 2 * DC, lambda c: V_GN + c)
                for u in range(3, 8):
                    split_lo(dve, O0 + u)
                update(O0 + 7)
            if level >= 5:
                M0 = UNIT["moe"]
                norm_dve(dve, "moe", C)
                R = [m_rt[:, k, :] for k in range(20)]
                R3 = [v.rearrange("p (t e) -> p t e", t=T) for v in R]
                lg, eq, oh1, l2, oh2, sl, pr, fc_ = R3[0:8]
                iota_e = iota_row[:, 0:NE]
                iota_b, m1, m2, i1, i2 = R[8][:, 0:NE], R[9][:, 0:T], R[10][:, 0:T], R[11][:, 0:T], R[12][:, 0:T]
                pos = [R[13][:, 0:T], R[13][:, T:2 * T]]
                gate = [R[14][:, 0:T], R[14][:, T:2 * T]]
                nb, end, start = R[15][:, 0:NE], R[16][:, 0:NE], R[17][:, 0:NE]
                slot_id = R[18][:, 0:1]
                e21 = m_rt[:, 20, 0:T]

                dve.wait_ge(r_lg, 1)
                C.link(nc.vector.tensor_copy(R[0], ps[4][:, 0:T * NE]))
                C.link(nc.vector.tensor_scalar(iota_b, iota_e, 64.0, None, ALU.add))
                for src, mx, idx, oh in ((lg, m1, i1, oh1), (l2, m2, i2, oh2)):
                    C.link(nc.vector.tensor_reduce(mx, src, AX.X, ALU.max))
                    C.link(nc.vector.tensor_tensor(eq, src, bcast(mx, 2, NE), ALU.is_equal))
                    for t in range(T):
                        last = nc.vector.scalar_tensor_tensor(fc_[:, t], eq[:, t], -64.0, iota_b, ALU.mult, ALU.add)
                    C.link(last)
                    C.link(nc.vector.tensor_reduce(idx, fc_, AX.X, ALU.min))
                    C.link(nc.vector.tensor_tensor(oh, bcast(iota_e, 1, T), bcast(idx, 2, NE), ALU.is_equal))
                    if oh is oh1:
                        C.link(nc.vector.scalar_tensor_tensor(R[3], R[2], -3e38, R[0], ALU.mult, ALU.add))
                C.link(nc.vector.tensor_tensor(R[5], R[2], R[4], ALU.add))
                nc.vector.tensor_tensor(e21, m2, m1, ALU.subtract).then_inc(r_m, 1)
                dve.wait_ge(r_e, 1)
                C.link(nc.vector.tensor_scalar(gate[0], e21, 1.0, None, ALU.add))
                C.link(nc.vector.reciprocal(gate[0], gate[0]))
                C.link(nc.vector.tensor_tensor(gate[1], e21, gate[0], ALU.mult))
                dve.wait_ge(r_rank, 1)
                count = ps[5][:, 2 * NE:3 * NE]
                C.link(nc.vector.tensor_scalar(nb, count, 0.5, None, ALU.is_gt))
                C.link(nc.vector.tensor_scalar(start, count, P + 0.5, None, ALU.is_gt))
                C.link(nc.vector.tensor_tensor(nb, nb, start, ALU.add))
                C.link(nc.vector.tensor_tensor_scan(end, ones[:, 0:NE], nb, 0.0, ALU.mult, ALU.add))
                C.link(nc.vector.tensor_tensor(start, end, nb, ALU.subtract))
                C.link(nc.vector.tensor_scalar(start, start, float(P), -1.0, ALU.mult, ALU.add))
                C.link(nc.vector.tensor_tensor(m_sg[0:1, 0:16 * NE].rearrange("p (i e) -> p i e", e=NE),
                                               bcast(end[0:1, :], 1, 16), bcast(iota_row[0:1, 0:16], 2, NE),
                                               ALU.is_le))
                C.link(nc.vector.tensor_reduce(m_sg[0:1, 256:272], m_sg[0:1, 0:16 * NE].rearrange("p (i e) -> p i e", e=NE),
                                               AX.X, ALU.add))
                C.link(nc.vector.tensor_scalar(m_sg[0:1, 256:272], m_sg[0:1, 256:272], NE - 1.0, None, ALU.min))
                C.link(nc.vector.tensor_copy(m_sg[0:1, 271:272], end[0:1, NE - 1:NE]))
                nc.vector.tensor_copy(tasks[0:1, :], m_sg[0:1, 256:272]).then_inc(r_tab, 1)
                for t in range(T):
                    last = nc.vector.tensor_tensor(sl[:, t], ps[5][:, t * NE:(t + 1) * NE], start, ALU.add)
                C.link(last)
                for c, oh in enumerate((oh1, oh2)):
                    C.link(nc.vector.tensor_tensor(pr, oh, sl, ALU.mult))
                    C.link(nc.vector.tensor_reduce(pos[c], pr, AX.X, ALU.add))
                for n, v in enumerate(pos + gate):
                    for t in range(T):
                        last = nc.vector.tensor_scalar(m_y[:, (2 * n + t) % 8 * P:((2 * n + t) % 8 + 1) * P], ident,
                                                       v[:, t:t + 1], None, ALU.mult)
                last.then_inc(r_diag, 1)
                C.link(nc.vector.tensor_copy(slot_id, iota_col))
                split_lo(dve, M0)
                split_lo(dve, M0 + 1)

                def pick():
                    for t in range(T):
                        nc.vector.tensor_scalar(m_pt[:, t, :], iota_row, pos[0][:, t:t + 1], None, ALU.is_equal)
                    for t in range(T):
                        last = nc.vector.tensor_scalar(m_p[:, t, :], iota_row, pos[1][:, t:t + 1], None, ALU.is_equal)
                    return last

                def pick_sum():
                    return nc.vector.tensor_tensor(m_p, m_p, m_pt, ALU.add)

                def tokens_lo(i):
                    for b in range(2):
                        dve.wait_ge(m_ahi, 2 * i + b + 1)
                        for c in range(4 * b, 4 * b + 4):
                            last = nc.vector.scalar_tensor_tensor(
                                a0_lo[:, c, 0:P], ps[b][:, (c % 4) * P:(c % 4 + 1) * P],
                                vec[:, V_MOE + c:V_MOE + c + 1], a0_hi[:, c, 0:P].bitcast(F32), ALU.mult, ALU.subtract)
                    last.then_inc(m_alo, 1)

                def product_lo(n):
                    dve.wait_ge(m_phi, n + 1)
                    nc.vector.tensor_tensor(a1_lo[:, 0:4, 0:P], ps[0][:, :].rearrange("p (c s) -> p c s", c=4),
                                            a1_hi[:, 0:4, 0:P].bitcast(F32), ALU.subtract).then_inc(m_plo, 1)

                def product(n, up_used):
                    dve.wait_ge(m_silu, n + 1)
                    dve.wait_ge(unit_used, up_used)
                    nc.vector.tensor_tensor(m_act, m_sg, ps[3][:, :], ALU.mult).then_inc(m_mult, 1)

                C.link(pick())
                pick_sum().then_inc(m_pk, 1)
                dve.wait_ge(m_pk, 1)
                tokens_lo(0)
                dve.wait_ge(r_g, 1)
                n_tasks = dve.value_load(tasks[0:1, 15:16], min_val=1, max_val=MAX_TASKS)
                L = Chain(dve, "task_chain")
                PER = 5
                with dve.Fori(0, n_tasks) as i:
                    L.again(i, PER)
                    split_lo(dve, M0 + 2, 7 * i)
                    split_lo(dve, M0 + 3, 7 * i)
                    L.link(nc.vector.tensor_scalar(m_gt, m_bc[:, 0, :], slot_id, None, ALU.is_equal))
                    L.link(nc.vector.tensor_tensor(m_gt, m_gt, m_bc[:, 2, :], ALU.mult))
                    L.link(nc.vector.scalar_tensor_tensor(m_gt2, m_bc[:, 1, :], slot_id, m_bc[:, 3, :],
                                                          ALU.is_equal, ALU.mult))
                    nc.vector.tensor_tensor(m_gt, m_gt, m_gt2, ALU.add).then_inc(m_gt_done, 1)
                    nc.vector.tensor_scalar(slot_id, slot_id, float(P), None, ALU.add)
                    L.link(nc.vector.tensor_scalar(R[13][:, 0:2 * T], R[13][:, 0:2 * T], float(P), None, ALU.subtract))
                    L.link(pick())
                    pick_sum().then_inc(m_pk, 1)
                    split_lo(dve, M0 + 4, 7 * i)
                    split_lo(dve, M0 + 5, 7 * i)
                    product(7 * i, used(M0 + 3, 7 * i))
                    with dve.Fori(1, 7) as j:
                        n = 7 * i + j
                        split_lo(dve, M0, n)
                        split_lo(dve, M0 + 1, n)
                        product_lo(n - 1)
                        for u in range(2, 6):
                            split_lo(dve, M0 + u, n)
                        product(n, used(M0 + 1, n))
                    n = 7 * i + 6
                    product_lo(n)
                    split_lo(dve, M0, n + 1)
                    split_lo(dve, M0 + 1, n + 1)
                    tokens_lo(i + 1)
                    dve.wait_ge(m_scat, i + 1)
                    for t in range(T):
                        for half in range(2):
                            at = slice(half * 512, (half + 1) * 512)
                            nc.vector.tensor_tensor(x[:, t, at], x[:, t, at], ps[SCAT[2 * t + half]][:, :],
                                                    ALU.add).then_inc(x_new, 1)
                    L.close()
                norm_dve(dve, "final", C)
                dve.wait_ge(pool_in, 32)
                for t in range(T):
                    last = nc.vector.scalar_tensor_tensor(fin_o[:, t, :], x[:, t, :], rstd[:, t:t + 1], fin_w,
                                                          ALU.mult, ALU.mult)
                last.then_inc(fin_done, 1)

        @block.tensor
        def _(pe):
            pe.wait_ge(s_const, N_CONST)
            pe.wait_ge(s_vrow, 16 * 17)
            nc.tensor.transpose(ps[7][:, 0:VA_N], vrow[0:VA_N, 0, :], ident[0:VA_N, 0:VA_N])
            nc.tensor.transpose(ps[7][:, P:P + VB_N], vrow[0:VB_N, 1, :], ident[0:VB_N, 0:VB_N])
            nc.tensor.transpose(ps[7][:, 2 * P:3 * P], vrow[:, 2, :], ident).then_inc(s_vecT, 1)
            pe.wait_ge(h_ready, 1)
            turn_pe(pe, "mix", h, DC)

            pe.wait_ge(turn_lo, TURN["mix"] + 4)
            u0 = UNIT["in"]
            for b in range(3):
                mm_rows(pe, u0 + 2 * b, ps[2 * b:2 * b + 2])
            with pe.Fori(1, 3) as i:
                for b in range(3):
                    pe.wait_ge(z_act, 3 * i + (b - 2))
                    pe.wait_ge(z_dve, 3 * i + (b - 2))
                    mm_rows(pe, u0 + 2 * b, ps[2 * b:2 * b + 2], i)
            for b in range(9, 12):
                pe.wait_ge(z_act, b - 2)
                pe.wait_ge(z_dve, b - 2)
                mm_rows(pe, u0 + 2 * b, ps[2 * (b % 3):2 * (b % 3) + 2], 0, min(WB, IN_W - b * WB))

            pe.wait_ge(at_n, 1)
            for c in range(5):
                for t in range(T):
                    at = (c % 2) * S + t * P
                    last = nc.tensor.transpose(ps[c // 2][:, at:at + P], at_qn[:, t, c * P:(c + 1) * P], ident)
            last.then_inc(at_T, 1)
            pe.wait_ge(at_c, 1)
            for step in range(4):
                t, j = step // 2, step % 2
                w = P if t == 0 else S
                rowsj = slice(j * DH, (j + 1) * DH)
                if step:
                    pe.wait_ge(at_m, step)
                for c in range(4):
                    last = nc.tensor.matmul(ps[3 + c // 2][:, (c % 2) * w:(c % 2 + 1) * w],
                                            at_qkT[rowsj, c, t * P:(t + 1) * P], at_qkT[rowsj, 4, 0:w],
                                            start=True, stop=True)
                last.then_inc(at_sc, 1)
                pe.wait_ge(at_e, step + 1)
                for k in range(w // P):
                    for c in range(4):
                        last = nc.tensor.transpose(ps[5 + k][:, c * P:(c + 1) * P], at_s[:, c, k * P:(k + 1) * P], ident)
                    last.then_inc(at_pt, 1)
                pe.wait_ge(at_pc, (step + 1 if step < 2 else 2 * step))
                if step:
                    pe.wait_ge(at_y, step)
                for c in range(4):
                    for k in range(w // P):
                        last = nc.tensor.matmul(ps[7][:, c * DH:(c + 1) * DH], at_pT[:, 4 * k + c, :],
                                                z[:, k, C_VA + j * DH:C_VA + (j + 1) * DH],
                                                start=(k == 0), stop=(k == w // P - 1))
                last.then_inc(at_o, 1)
            pe.wait_ge(at_y, 4)
            turn_pe(pe, "ya", ya, 4)

            pe.wait_ge(turn_lo, TURN["ya"] + 2)
            for t in range(T):
                for hh in range(HB):
                    for kk in range(2):
                        nc.tensor.transpose(ps[2 * kk + t][:, hh * P:(hh + 1) * P],
                                            z[:, t, C_QB + kk * QKB + hh * P:C_QB + kk * QKB + (hh + 1) * P], ident)
            for t in range(T):
                last = nc.tensor.transpose(ps[4][0:GKR, t * P:(t + 1) * P], z[:, t, C_GK:C_GK + GKR], ident)
            last.then_inc(gl_T, 1)
            pe.wait_ge(gl_c, 1)
            pe.wait_ge(s_small, 32)
            for hh in range(HB):
                last = nc.tensor.matmul(ps[5 + hh // 2][:, (hh % 2) * S:(hh % 2 + 1) * S], wgk[:, hh * P:(hh + 1) * P],
                                        g_lrT[0:GKR, :, :].rearrange("p t i -> p (t i)"), start=True, stop=True)
            last.then_inc(gl_g, 1)
            for t in range(T):
                for hh in range(HB):
                    last = nc.tensor.matmul(ps[t][:, hh * P:(hh + 1) * P], g_k[:, t, hh, :], g_q[:, t, hh, :],
                                            start=True, stop=True)
                last.then_inc(gl_a, 1)
            for n in range(T * LEVELS):
                pe.wait_ge(gl_p, n + 1)
                if n >= 2:
                    pe.wait_ge(gl_m, n - 1)
                for hh in range(HB):
                    last = nc.tensor.matmul(ps[(n + 2) % 4][:, hh * P:(hh + 1) * P], g_f[n % 4][:, hh, :],
                                            g_f[n % 4][:, hh, :], start=True, stop=True)
                last.then_inc(gl_a, 1)
            pe.wait_ge(gl_k, 1)
            for hh in range(HB):
                last = nc.tensor.transpose(ps[4][:, hh * P:(hh + 1) * P], g_e[:, 0, hh, :], ident)
            last.then_inc(gl_kT, 1)
            pe.wait_ge(gl_kc, 1)
            for hh in range(HB):
                last = nc.tensor.matmul(ps[5 + hh // 2][:, (hh % 2) * DVB:(hh % 2 + 1) * DVB], g_kdT[:, hh, :],
                                        z[:, 0, C_VB + hh * DVB:C_VB + (hh + 1) * DVB], start=True, stop=True)
            last.then_inc(gl_s, 1)
            pe.wait_ge(gl_m, T * LEVELS + 2)
            pe.wait_ge(gl_sc, 1)
            for t in range(T):
                for hh in range(HB):
                    o = ps[4 + 2 * t + hh // 2][:, (hh % 2) * DVB:(hh % 2 + 1) * DVB]
                    last = nc.tensor.matmul(o, g_acc[:, t, hh, :], z[:, t, C_VB + hh * DVB:C_VB + (hh + 1) * DVB],
                                            start=True, stop=(t == 0))
                    if t:
                        last = nc.tensor.matmul(o, g_e[:, 1, hh, :], g_s0[:, hh, :], start=False, stop=True)
            last.then_inc(gl_o, 1)
            pe.wait_ge(gl_yb, 1)
            turn_pe(pe, "yb", g_o, DC)

            for k in range(2):
                mm_down(pe, UNIT["wa"] + k, a1_hi[:, 2 * k:2 * k + 2], a1_lo[:, 2 * k:2 * k + 2], ps[4:8], k == 0, k == 1)
            pe.wait_ge(turn_lo, TURN["yb"] + 4)
            for k in range(4):
                mm_down(pe, UNIT["wb"] + k, a0_hi[:, 2 * k:2 * k + 2], a0_lo[:, 2 * k:2 * k + 2], ps[0:4], k == 0, k == 3)
            pe.wait_ge(br_m, 1)
            turn_pe(pe, "merged", merged, DC)
            pe.wait_ge(turn_lo, TURN["merged"] + 4)
            for k in range(4):
                mm_down(pe, UNIT["wo"] + k, a1_hi[:, 2 * k:2 * k + 2], a1_lo[:, 2 * k:2 * k + 2], ps[4:8], k == 0, k == 3)

            def two_to_a_bank(b0):
                return [ps[b0 + f // 2][:, (f % 2) * S:(f % 2 + 1) * S] for f in range(4)]

            def ffn(f):
                u0 = UNIT[f"ffn{f}"]
                pe.wait_ge(h_ready, 2 + 2 * f)
                turn_pe(pe, f"ffn{f}", h, DC)
                pe.wait_ge(turn_lo, TURN[f"ffn{f}"] + 4)
                gate, up = two_to_a_bank(0), two_to_a_bank(2)

                def down(u, i, first, last, rounds=0):
                    if first is not None:
                        pe.wait_ge(f_lo, 6 * f + i + 1)
                    mm_down(pe, u, a1_hi[:, 0:2], a1_lo[:, 0:2], ps[4:8], first is True, False, rounds)
                    mm_down(pe, u + 1, a1_hi[:, 2:4], a1_lo[:, 2:4], ps[4:8], False, False, rounds)

                def gate_free(i):
                    pe.wait_ge(f_conv, i) if f == 0 else pe.wait_ge(f_silu, 6 * f + i)

                mm_cols(pe, u0, gate)
                mm_cols(pe, u0 + 2, up)
                def body(i, rounds, first):
                    gate_free(i + 1)
                    mm_cols(pe, u0 + 4, gate, rounds)
                    down(u0 + 6, i, first, False, rounds)
                    pe.wait_ge(f_mult, 6 * f + i + 1)
                    mm_cols(pe, u0 + 8, up, rounds)

                body(0, 0, True)
                with pe.Fori(1, 4) as i:
                    body(i, i, False)
                gate_free(5)
                pe.wait_ge(f_mult, 6 * f + 5)
                mm_cols(pe, u0 + 28, [gate[0], gate[1], up[0], up[1]])
                down(u0 + 30, 4, False, False)
                pe.wait_ge(f_lo, 6 * f + 6)
                mm_down(pe, u0 + 32, a1_hi[:, 4:6], a1_lo[:, 4:6], ps[4:8], False, True)

            if level >= 1:
                ffn(0)
            if level >= 2:
                pe.wait_ge(h_ready, 3)
                for b in range(4):
                    for c in (2 * b, 2 * b + 1):
                        for t in range(T):
                            at = (c % 2) * S + t * P
                            last = nc.tensor.transpose(ps[b][:, at:at + P], h[:, t, c * P:(c + 1) * P], ident)
                    last.then_inc(pl_T, 1)
                u = UNIT["pool"]
                pe.wait_ge(lo_done, u + 1)
                pe.wait_ge(pl_lo, 1)
                for t in range(T):
                    for g in range(4):
                        for k in range(2):
                            c = 2 * g + k
                            cols = slice(c * 256, (c + 1) * 256)
                            last = mm3(ps[4 + 2 * t + g // 2][:, (g % 2) * 256:(g % 2 + 1) * 256],
                                       a1_hi[:, c, t * P:(t + 1) * P], a1_lo[:, c, t * P:(t + 1) * P],
                                       w_hi[:, u % SPL, cols], w_lo[:, u % SPL, cols], k == 0, k == 1)
                last.then_inc(unit_used, 1)
            if level >= 3:
                ffn(1)
            if level >= 4:
                D0, X0, Z0, O0 = UNIT["dt"], UNIT["xbc"], UNIT["z"], UNIT["sout"]
                pe.wait_ge(h_ready, 5)
                turn_pe(pe, "ssd", h, DC)
                pe.wait_ge(turn_lo, TURN["ssd"] + 4)
                pe.wait_ge(lo_done, D0 + 1)
                for t in range(T):
                    for kc in range(DC):
                        cols = slice(kc * NH, (kc + 1) * NH)
                        last = mm3(ps[6][:, t * NH:(t + 1) * NH], a0_hi[:, kc, t * P:(t + 1) * P],
                                   a0_lo[:, kc, t * P:(t + 1) * P], w_hi[:, D0 % SPL, cols], w_lo[:, D0 % SPL, cols],
                                   kc == 0, kc == DC - 1)
                last.then_inc(unit_used, 1)
                pairs = [two_to_a_bank(2 * b) for b in range(3)]
                for b in range(3):
                    mm_cols(pe, X0 + 2 * b, pairs[b])
                with pe.Fori(1, 2) as i:
                    for b in range(3):
                        pe.wait_ge(c_conv, 3 * i + (b - 2))
                        mm_cols(pe, X0 + 2 * b, pairs[b], i)
                for b in range(6, 8):
                    pe.wait_ge(c_conv, b - 2)
                    mm_cols(pe, X0 + 2 * b, pairs[b % 3])
                pe.wait_ge(sd_dta, 1)
                nc.tensor.matmul(ps[7][:, 0:64], upper, dta, start=True, stop=True)
                nc.tensor.matmul(ps[7][:, 64:128], ones, dta, start=True, stop=True).then_inc(sd_acs, 1)
                pe.wait_ge(c_silu, 8)
                for r in range(10):
                    if r >= 4:
                        pe.wait_ge(xt_dve if r % 2 else xt_act, (r - 4) // 2 + 1)
                    t, c0 = (r // 4, 4 * (r % 4)) if r < 8 else (0, 16 + 4 * (r - 8))
                    for c in range(4):
                        last = nc.tensor.transpose(ps[r % 4][:, c * P:(c + 1) * P], cv[:, c0 + c, t * P:(t + 1) * P], ident)
                    last.then_inc(xt_ps, 1)
                pe.wait_ge(sd_te, 1)
                for b in range(4):
                    if b >= 2:
                        pe.wait_ge(zs_done, b - 1)
                    mm_rows(pe, Z0 + 2 * b, ps[4 + 2 * (b % 2):6 + 2 * (b % 2)])
                pe.wait_ge(xt_act, 5)
                pe.wait_ge(xt_dve, 5)
                pe.wait_ge(zs_done, 4)

                def tile_weights(k):
                    g, t = k // 2, k % 2
                    if k >= 2:
                        pe.wait_ge(st_ex, k - 1)
                        pe.wait_ge(st_cb, k - 1)
                    for r in range(HPG):
                        hd = t * NH + HPG * g + r
                        nc.tensor.matmul(ps[k % 2][:, r * P:(r + 1) * P], dta[:, hd:hd + 1].to_broadcast([P, P]), upper,
                                         start=True, stop=True)
                    nc.tensor.matmul(ps[2 + k % 2][:, 0:P], cv[:, 16 + g, t * P:(t + 1) * P],
                                     cv[:, 24 + g, t * P:(t + 1) * P], start=True, stop=True).then_inc(st_seg, 1)

                def tile_output(k):
                    g, t = k // 2, k % 2
                    pe.wait_ge(st_xd, 3 * g + (2 if t == 0 else 3))
                    if t:
                        pe.wait_ge(st_sc, g + 1)
                        if g:
                            pe.wait_ge(st_acc, k - 1)
                        nc.tensor.matmul(ps[7][:, 0:256], cv[:, 24 + g, P:S], s_st.rearrange("p r e -> p (r e)"),
                                         start=True, stop=True)
                    else:
                        nc.tensor.matmul(ps[6][:, 0:256], s_b0[:, g, :], s_xe.rearrange("p r e -> p (r e)"),
                                         start=True, stop=True).then_inc(st_s, 1)
                    pe.wait_ge(st_w, k + 1)
                    if k >= 2:
                        pe.wait_ge(st_acc, k - 1)
                    for r in range(HPG):
                        last = nc.tensor.matmul(ps[4 + k % 2][:, r * HD:(r + 1) * HD], s_ex[k % 2][:, r, :], s_xd[k % 2][:, r, :],
                                                start=True, stop=True)
                    last.then_inc(st_y, 1)

                tile_weights(0)
                tile_weights(1)
                for k in range(2 * NG):
                    tile_output(k)
                    if k + 2 < 2 * NG:
                        tile_weights(k + 2)
                pe.wait_ge(sy_done, 1)
                turn_pe(pe, "y", xs, 2 * DC)
                pe.wait_ge(turn_lo, TURN["y"] + 8)
                for k in range(8):
                    hi, lo = (a0_hi, a0_lo) if k < 4 else (a1_hi, a1_lo)
                    at = slice(2 * (k % 4), 2 * (k % 4) + 2)
                    mm_down(pe, O0 + k, hi[:, at], lo[:, at], ps[4:8], k == 0, k == 7)
            if level >= 5:
                M0 = UNIT["moe"]
                pe.wait_ge(h_ready, 6)
                for b in range(4):
                    for c in (2 * b, 2 * b + 1):
                        for t in range(T):
                            at = (c % 2) * S + t * P
                            last = nc.tensor.transpose(ps[b][:, at:at + P], h[:, t, c * P:(c + 1) * P], ident)
                    last.then_inc(r_T, 1)
                pe.wait_ge(r_h, 4)
                for t in range(T):
                    for c in range(DC):
                        last = nc.tensor.matmul(ps[4][:, t * NE:(t + 1) * NE], m_hT[:, c, t * P:(t + 1) * P], wr[:, c, :],
                                                start=(c == 0), stop=(c == DC - 1))
                last.then_inc(r_lg, 1)
                pe.wait_ge(r_m, 1)
                sel = m_rt[:, 5, :]
                nc.tensor.matmul(ps[5][:, 0:NE], upper, sel[:, 0:NE], start=True, stop=True)
                nc.tensor.matmul(ps[5][:, NE:2 * NE], upper, sel[:, NE:2 * NE], start=True, stop=False)
                nc.tensor.matmul(ps[5][:, NE:2 * NE], ones, sel[:, 0:NE], start=False, stop=True)
                nc.tensor.matmul(ps[5][:, 2 * NE:3 * NE], ones, sel[:, 0:NE], start=True, stop=False)
                nc.tensor.matmul(ps[5][:, 2 * NE:3 * NE], ones, sel[:, NE:2 * NE], start=False,
                                 stop=True).then_inc(r_rank, 1)
                pe.wait_ge(r_diag, 1)
                for n in range(4):
                    for t in range(T):
                        last = nc.tensor.matmul(ps[6 + n // 2][:, (n % 2) * S + t * P:(n % 2) * S + (t + 1) * P], ones,
                                                m_y[:, (2 * n + t) * P:(2 * n + t + 1) * P], start=True, stop=True)
                last.then_inc(r_bc, 1)

                def gather(i):
                    pe.wait_ge(m_pk, i + 1)
                    for c in range(DC):
                        for t in range(T):
                            last = nc.tensor.matmul(ps[c // 4][:, (c % 4) * P:(c % 4 + 1) * P],
                                                    h[:, t, c * P:(c + 1) * P], m_p[:, t, :],
                                                    start=(t == 0), stop=(t == T - 1))
                    last.then_inc(m_gather, 1)

                def project(u, bank, rounds):
                    for half in range(2):
                        pe.wait_ge(lo_done, RAW * rounds + (M0 + u + half + 1))
                        slot = (M0 + u + half) % SPL
                        for k in range(4):
                            kc = 4 * half + k
                            cols = slice(k * WB, (k + 1) * WB)
                            last = mm3(bank[:, :], a0_hi[:, kc, 0:P], a0_lo[:, kc, 0:P], w_hi[:, slot, cols],
                                       w_lo[:, slot, cols], kc == 0, kc == DC - 1)
                        last.then_inc(unit_used, 1)

                def turn_product(n):
                    pe.wait_ge(m_mult, n + 1)
                    for c in range(4):
                        last = nc.tensor.transpose(ps[0][:, c * P:(c + 1) * P], m_act[:, c * P:(c + 1) * P], ident)
                    last.then_inc(m_tr, 1)

                def down(u, n, rounds, first, last):
                    pe.wait_ge(m_plo, n + 1)
                    for half in range(2):
                        mm_down(pe, M0 + u + half, a1_hi[:, 2 * half:2 * half + 2], a1_lo[:, 2 * half:2 * half + 2],
                                ps[4:6], first and half == 0, last and half == 1, rounds, tiles=1)

                gather(0)
                pe.wait_ge(r_tab, 1)
                n_tasks = pe.value_load(tasks[0:1, 15:16], min_val=1, max_val=MAX_TASKS)
                with pe.Fori(0, n_tasks) as i:
                    pe.wait_ge(m_alo, i + 1)
                    pe.wait_ge(x_new, 4 * i + UPD["ssd"])
                    project(0, ps[2], 7 * i)
                    project(2, ps[3], 7 * i)

                    def body(n, first):
                        pe.wait_ge(m_silu, n)
                        project(4 - RAW, ps[2], n)
                        turn_product(n - 1)
                        project(6 - RAW, ps[3], n)
                        down(8 - RAW, n - 1, n, first, False)

                    body(7 * i + 1, True)
                    with pe.Fori(2, 7) as j:
                        body(7 * i + j, False)
                    n = 7 * i + 6
                    turn_product(n)
                    down(4, n, n, False, True)
                    gather(i + 1)
                    pe.wait_ge(m_y_done, i + 1)
                    pe.wait_ge(m_gt_done, i + 1)
                    for t in range(T):
                        for half in range(2):
                            last = nc.tensor.matmul(ps[SCAT[2 * t + half]][:, :], m_gt[:, t * P:(t + 1) * P],
                                                    m_y[:, half * 512:(half + 1) * 512], start=True, stop=True)
                    last.then_inc(m_scat, 1)


STOP = "all"
_INS = ["x", "ln_mix_g", "w_in", "q_norm_g", "k_norm_g", "sinks", "w_gk_up", "b_gk", "gla_norm_g", "w_branch_a",
        "w_branch_b", "w_out", "ln_ffn_g", "w_ffn_in", "conv_w", "conv_b", "w_ffn_out", "pool_norm_w_2", "pool_w_2",
        "pool_scale_2", "dense_norm_w_2", "dense_w_gate_2", "dense_w_up_2", "dense_w_down_2", "ssd_norm_w_2",
        "ssd_w_in_2", "ssd_conv_w_2", "ssd_conv_b_2", "ssd_dt_bias_2", "ssd_a_log_2", "ssd_d_2",
        "ssd_gate_norm_w_2", "ssd_w_out_2", "moe_norm_w_2", "moe_w_router_2", "moe_w_gate_2", "moe_w_up_2",
        "moe_w_down_2", "final_norm_w_2"]


def kernel(**inputs):
    import numpy as _np
    import concourse.bacc as _bacc
    from concourse import mybir as _mybir
    from concourse.bass_utils import run_bass_kernel_spmd as _run

    nc = _bacc.Bacc("TRN2", target_bir_lowering=False, num_devices=1)
    arrays, aps = {}, {}
    for name in _INS:
        a = _np.ascontiguousarray(inputs[name])
        arrays[f"in_{name}_dram"] = a
        aps[name] = nc.dram_tensor(f"in_{name}_dram", a.shape, _mybir.dt.from_np(a.dtype), kind="ExternalInput").ap()
    out = nc.dram_tensor("out_0_dram", (1, S, D), _mybir.dt.from_np(_np.dtype("float32")), kind="ExternalOutput").ap()
    block_kernel(nc, aps, out, stop=STOP)
    r = _run(nc, [arrays], core_ids=[0])
    return r.results[0]["out_0_dram"]
```

```python
import concourse.bass as bass
from concourse import mybir
from contextlib import ExitStack

F32 = mybir.dt.float32
F32R = mybir.dt.float32r
BF16 = mybir.dt.bfloat16
I32 = mybir.dt.int32
ALU = mybir.AluOpType
ACT = mybir.ActivationFunctionType
AX = mybir.AxisListType

P = 128
S = 256
T = S // P
D = 1024
DC = D // P
EPS, SSM_EPS = 1e-6, 1e-5

QA, KVA, QKB, VB, GKR = 512, 128, 512, 1024, 16
DH, HKV, GQ = 64, 2, 4
HB, DKB, DVB = 4, 128, 256
GATE_NORM = 16.0
C_KA, C_VA, C_QB = QA, QA + KVA, QA + 2 * KVA
C_KB, C_VB = C_QB + QKB, C_QB + 2 * QKB
C_RB = C_VB + VB
C_GK = C_RB + VB
C_GA = C_GK + GKR
C_GB = C_GA + D
IN_W = C_GB + D
FF = 2816
FFC = FF // P
CONV_W = 3

DI, BC, NH, NG, HPG, HD = 2048, 1024, 32, 8, 4, 64
XBC = DI + 2 * BC
XBCC = XBC // P
SCONV = 4

NE, FE = 8, 3584
MAX_TASKS = NE + (2 * S - NE) // P

UC = 2048
RAW, SPL = 6, 3
WB = 512


def schedule():
    first, at = {}, 0
    for name, n in (("in", 24), ("wa", 2), ("wb", 4), ("wo", 4), ("ffn0", 33), ("pool", 1), ("ffn1", 33),
                    ("dt", 1), ("xbc", 16), ("z", 8), ("sout", 8), ("moe", 0)):
        first[name] = at
        at += n
    return first


UNIT = schedule()
MOE_UNITS = 42

TURNS = (("mix", 4), ("ya", 2), ("yb", 4), ("merged", 4), ("ffn0", 4), ("pooled", 4), ("ffn1", 4), ("ssd", 4),
         ("y", 8))
TURN = {}
_at = 0
for _name, _n in TURNS:
    TURN[_name] = _at
    _at += _n


def bcast(ap, axis, n):
    a = ap.unsqueeze(axis)
    shape = list(a.shape)
    shape[axis] = n
    return a.to_broadcast(shape)


def block_kernel(nc, I, out, stop="all"):
    ctx = ExitStack()
    with ctx:
        def sb(name, shape, dt=F32):
            return ctx.enter_context(nc.sbuf_tensor(name, shape, dt))

        def sem(name):
            return ctx.enter_context(nc.semaphore(name))

        def rows(w):
            return w.rearrange("(k p) n -> p k n", p=P)

        w_in_v = rows(I["w_in"][0])
        wa_v, wb_v, wo_v = rows(I["w_branch_a"][0]), rows(I["w_branch_b"][0]), rows(I["w_out"][0])
        ffn_in_v = rows(I["w_ffn_in"][0])
        ffn_gate_v = (ffn_in_v[:, :, 0:FF], rows(I["dense_w_gate_2"][0]))
        ffn_up_v = (ffn_in_v[:, :, FF:2 * FF], rows(I["dense_w_up_2"][0]))
        ffn_down_v = (rows(I["w_ffn_out"][0]), rows(I["dense_w_down_2"][0]))
        pool_v = I["pool_w_2"][0].rearrange("g (k p) n -> p (g k) n", p=P)
        ssd_in_v, ssd_out_v = rows(I["ssd_w_in_2"][0]), rows(I["ssd_w_out_2"][0])
        moe_gate_v = I["moe_w_gate_2"][0].rearrange("e (k p) n -> p e k n", p=P)
        moe_up_v = I["moe_w_up_2"][0].rearrange("e (k p) n -> p e k n", p=P)
        moe_down_v = I["moe_w_down_2"][0].rearrange("e (k p) n -> p e k n", p=P)
        x_v = I["x"][0].rearrange("(t p) d -> p t d", p=P)
        out_v = out[0].rearrange("(t p) d -> p t d", p=P)

        raw = sb("raw", [P, RAW, UC])
        w_hi = sb("w_hi", [P, SPL, UC], F32R)
        w_lo = sb("w_lo", [P, SPL, UC], F32R)
        a0_hi = sb("a0_hi", [P, DC, S], F32R)
        a0_lo = sb("a0_lo", [P, DC, S], F32R)
        a1_hi = sb("a1_hi", [P, DC, S], F32R)
        a1_lo = sb("a1_lo", [P, DC, S], F32R)
        x = sb("x_res", [P, T, D])
        arena = sb("arena", [P, 15496])
        vec = sb("vec", [P, 3 * P])
        cst = sb("cst", [P, 7 * P + 1])
        lmask = sb("lmask", [P, 7, P], BF16)
        rowv = sb("rowv", [P, 8 + 3 * NH])
        stat = sb("stat", [P, 64])
        sm = sb("sm", [P, 9, T * NH])
        taps = sb("taps", [P, SCONV + 1, 4])
        wr = sb("wr", [P, DC, NE])
        tasks = sb("tasks", [1, 16], I32)

        ident, upper, lower, ones = (cst[:, k * P:(k + 1) * P] for k in range(4))
        amask = cst[:, 4 * P:6 * P]
        iota_row, iota_col = cst[:, 6 * P:7 * P], cst[:, 7 * P:7 * P + 1]
        wgk = sm[0:GKR, 0:8, :].rearrange("p a b -> p (a b)")
        sinks, dt_bias, a_log, d_skip = rowv[:, 0:8], rowv[:, 8:40], rowv[:, 40:72], rowv[:, 72:104]
        ss, sd, rstd = stat[:, 0:2], stat[:, 2:4], stat[:, 4:6]

        def region(at, *dims):
            n = 1
            for d in dims:
                n *= d
            v = arena[:, at:at + n]
            if len(dims) == 2:
                v = v.rearrange("p (a b) -> p a b", a=dims[0])
            if len(dims) == 3:
                v = v.rearrange("p (a b c) -> p a b c", a=dims[0], b=dims[1])
            return v

        V_MIX, V_FFN, V_CB, V_CW, V_BGK, V_G2, V_QG, V_KG, VA_N = 0, 8, 16, 38, 104, 108, 110, 111, 112
        V_POOL, V_DENSE, V_SSD, V_MOE, V_GN, V_SCB = (P + n for n in (0, 8, 16, 24, 32, 48))
        VB_N = 80
        V_SCW = 2 * P

        TMP = 11808
        z = region(0, T, IN_W)
        h = region(TMP, T, D)
        junk = region(TMP + T * D, D)
        vrow = region(0, 3, P)

        ps = [ctx.enter_context(nc.psum_tensor(f"ps{b}", [P, 512], F32)) for b in range(8)]

        raw_full = [sem(f"raw_full{k}") for k in range(RAW)]
        hi_done, lo_done, unit_used = sem("hi_done"), sem("lo_done"), sem("unit_used")
        s_x, s_vrow, s_rowv, s_small = sem("s_x"), sem("s_vrow"), sem("s_rowv"), sem("s_small")
        s_const, s_out = sem("s_const"), sem("s_out")
        s_vecT, s_vec = sem("s_vecT"), sem("s_vec")
        x_new, sq_sum, h_ready = sem("x_new"), sem("sq_sum"), sem("h_ready")
        turned, turn_hi, turn_lo = sem("turned"), sem("turn_hi"), sem("turn_lo")
        z_act, z_dve = sem("z_act"), sem("z_dve")

        N_CONST = 10 + 4 * 7

        class Chain:

            def __init__(self, eng, name, rounds=0, per=0):
                self.eng, self.sem, self.n, self.base, self.per = eng, sem(name), 0, rounds, per

            def link(self, ins):
                self.n += 1
                ins.then_inc(self.sem, 1)
                self.eng.wait_ge(self.sem, self.base * self.per + self.n)

            def again(self, rounds, per):
                self.n, self.base, self.per = 0, rounds, per

            def close(self):
                assert self.n == self.per, (self.n, self.per)

        block = ctx.enter_context(nc.Block())

        PHASES = ["mix", "ffn0", "pool", "ffn1", "ssd", "all"]
        level = PHASES.index(stop)

        UPD = {"mix": 4, "ffn0": 8, "pool": 12, "ffn1": 16, "ssd": 20}

        def used(u, rounds=0):
            return RAW * rounds + u + 1

        def load(sp, u, src, rounds=0, part=None):
            if u >= RAW:
                sp.wait_ge(lo_done, RAW * rounds + u - RAW + 1)
            k, n = src.shape[-2], src.shape[-1]
            dst = raw[:, u % RAW, 0:k * n].rearrange("p (k n) -> p k n", k=k) if part is None else part
            return sp.dma_start(dst, src).then_inc(raw_full[u % RAW], 16)

        LAST = [UNIT["ffn0"], UNIT["pool"], UNIT["ffn1"], UNIT["dt"], UNIT["moe"], UNIT["moe"] + 1000][level]

        def split_hi(act, u, rounds=0):
            if u >= LAST:
                return
            act.wait_ge(raw_full[u % RAW], 16 * rounds + 16 * (u // RAW + 1))
            if u >= SPL:
                act.wait_ge(unit_used, RAW * rounds + u - SPL + 1)
            nc.scalar.activation(w_hi[:, u % SPL, :], raw[:, u % RAW, :], ACT.Copy).then_inc(hi_done, 1)

        def split_lo(dve, u, rounds=0):
            if u >= LAST:
                return
            dve.wait_ge(hi_done, RAW * rounds + u + 1)
            nc.vector.tensor_tensor(w_lo[:, u % SPL, :], raw[:, u % RAW, :], w_hi[:, u % SPL, :].bitcast(F32),
                                    ALU.subtract).then_inc(lo_done, 1)

        def mm3(o, lh, ll, rh, rl, start, stop):
            nc.tensor.matmul(o, lh, rh, start=start, stop=False, skip_group_check=True)
            nc.tensor.matmul(o, lh, rl, start=False, stop=False, skip_group_check=True)
            return nc.tensor.matmul(o, ll, rh, start=False, stop=stop, skip_group_check=True)

        def mm_rows(pe, u, banks, rounds=0, n=WB, halves=(0, 1), turn=None):
            for half in halves:
                if turn:
                    pe.wait_ge(turn_lo, TURN[turn] + 2 * half + 2)
                pe.wait_ge(lo_done, RAW * rounds + u + half + 1)
                slot = (u + half) % SPL
                for k in range(4):
                    kc = 4 * half + k
                    for t in range(T):
                        cols = slice(k * n, (k + 1) * n)
                        last = mm3(banks[t][:, 0:n], a0_hi[:, kc, t * P:(t + 1) * P], a0_lo[:, kc, t * P:(t + 1) * P],
                                   w_hi[:, slot, cols], w_lo[:, slot, cols], kc == 0, kc == DC - 1)
                last.then_inc(unit_used, 1)

        def mm_cols(pe, u, outs, rounds=0, n=WB, turn=None):
            for half in range(2):
                if turn:
                    pe.wait_ge(turn_lo, TURN[turn] + 2 * half + 2)
                pe.wait_ge(lo_done, RAW * rounds + u + half + 1)
                slot = (u + half) % SPL
                for k in range(4):
                    kc = 4 * half + k
                    for f in range(n // P):
                        cols = slice(k * n + f * P, k * n + (f + 1) * P)
                        last = mm3(outs[f], w_hi[:, slot, cols], w_lo[:, slot, cols], a0_hi[:, kc, :], a0_lo[:, kc, :],
                                   kc == 0 and f % 2 == 0, kc == DC - 1)
                last.then_inc(unit_used, 1)

        def mm_down(pe, u, src_hi, src_lo, banks, first, last_one, rounds=0, tiles=T, nk=2):
            pe.wait_ge(lo_done, RAW * rounds + u + 1)
            slot = u % SPL
            for k in range(nk):
                for t in range(tiles):
                    lh, ll = src_hi[:, k, t * P:(t + 1) * P], src_lo[:, k, t * P:(t + 1) * P]
                    for half in range(2):
                        cols = slice(k * D + half * 512, k * D + (half + 1) * 512)
                        mm = mm3(banks[2 * t + half][:, :], lh, ll, w_hi[:, slot, cols], w_lo[:, slot, cols],
                                 first and k == 0, last_one and k == nk - 1)
            mm.then_inc(unit_used, 1)

        def norm_stat(act, width, eps):
            nc.scalar.activation(sd, ss, ACT.Sqrt, scale=1.0 / width, bias=eps).then_inc(sq_sum, 1)

        NORMS = ["mix", "ffn0", "pool", "ffn1", "ssd", "moe", "final"]

        def norm_act(act, name, chain):
            n = NORMS.index(name)
            if name == "mix":
                act.wait_ge(s_x, 16)
            for t in range(T):
                if name not in ("mix", "final"):
                    act.wait_ge(x_new, 4 * n - 2 + 2 * t)
                chain.link(nc.scalar.activation(junk, x[:, t, :], ACT.Square, accum_out=ss[:, t:t + 1]))
            norm_stat(act, D, EPS)

        def norm_dve(dve, name, chain):
            n = NORMS.index(name)
            dve.wait_ge(sq_sum, n + 1 + (1 if name in ("moe", "final") else 0))
            chain.link(nc.vector.reciprocal(rstd, sd))
            if name == "final":
                return
            nc.vector.tensor_scalar(h[:, 0, :], x[:, 0, :], rstd[:, 0:1], None, ALU.mult)
            nc.vector.tensor_scalar(h[:, 1, :], x[:, 1, :], rstd[:, 1:2], None, ALU.mult).then_inc(h_ready, 1)

        def turn_pe(pe, name, src, chunks):
            for b in range(chunks // 2):
                g = TURN[name] + b
                if b >= 4:
                    pe.wait_ge(turn_lo, g - 3)
                for c in (2 * b, 2 * b + 1):
                    for t in range(T):
                        at = (c % 2) * S + t * P
                        last = nc.tensor.transpose(ps[b % 4][:, at:at + P], src[:, t, c * P:(c + 1) * P], ident)
                last.then_inc(turned, 1)

        def turn_act(act, name, dst_hi, chunks, gain):
            for b in range(chunks // 2):
                act.wait_ge(turned, TURN[name] + b + 1)
                if gain is None:
                    last = nc.scalar.activation(dst_hi(2 * b, 2), ps[b % 4][:, :].rearrange("p (c s) -> p c s", c=2),
                                                ACT.Copy)
                else:
                    for c in (2 * b, 2 * b + 1):
                        g = gain(c)
                        last = nc.scalar.activation(dst_hi(c, 1), ps[b % 4][:, (c % 2) * S:(c % 2 + 1) * S], ACT.Copy,
                                                    scale=vec[:, g:g + 1])
                last.then_inc(turn_hi, 1)

        def turn_dve(dve, name, dst_hi, dst_lo, chunks, gain):
            for b in range(chunks // 2):
                dve.wait_ge(turn_hi, TURN[name] + b + 1)
                if gain is None:
                    last = nc.vector.tensor_tensor(dst_lo(2 * b, 2), ps[b % 4][:, :].rearrange("p (c s) -> p c s", c=2),
                                                   dst_hi(2 * b, 2).bitcast(F32), ALU.subtract)
                else:
                    for c in (2 * b, 2 * b + 1):
                        g = gain(c)
                        last = nc.vector.scalar_tensor_tensor(dst_lo(c, 1), ps[b % 4][:, (c % 2) * S:(c % 2 + 1) * S],
                                                              vec[:, g:g + 1], dst_hi(c, 1).bitcast(F32),
                                                              ALU.mult, ALU.subtract)
                last.then_inc(turn_lo, 1)

        def chunks_of(buf):
            def at(c, n):
                return buf[:, c, :] if n == 1 else buf[:, c:c + n, :]
            return at

        def chunks_two(b0, b1):
            def at(c, n):
                buf, c = (b0, c) if c < DC else (b1, c - DC)
                return buf[:, c, :] if n == 1 else buf[:, c:c + n, :]
            return at

        at_sq, at_qkT = region(TMP, T, 640), region(TMP, 5, S)
        at_qn = region(TMP + 1280, T, 640)
        at_s = [z[:, 1, 0:512], z[:, 0, 0:512], region(TMP + 1280, 4 * S), region(TMP + 2304, 4 * S)]
        AT_BANKS = ((4,), (5,), (6, 7), (4, 5))
        AT_OUT = (4, 6)
        at_max, at_neg, at_sink = ([stat[:, c + 4 * k:c + 4 * k + 4] for k in range(4)] for c in (8, 24, 40))
        at_sum, at_nsink = at_max, stat[:, 56:64]

        def at_width(step):
            return P if step < 2 else S

        ya = z[:, :, 0:QA]
        def tiles(v):
            return v.rearrange("p t (h i) -> p t h i", h=HB)
        g_b, g_acc, g_e = tiles(z[:, :, C_QB:C_QB + 512]), tiles(z[:, :, C_KB:C_KB + 512]), tiles(z[:, :, 0:512])
        g_q, g_k = region(TMP, T, HB, P), region(TMP + 1024, T, HB, P)
        g_qe = region(TMP + 2048, T, HB, P)
        g_lrT = region(TMP + 3072, T, P)
        g_f = (g_e[:, 0], g_e[:, 1], g_qe[:, 0], g_qe[:, 1])
        LEVELS = 7

        def halves(v, lv):
            m = 64 >> lv
            pairs = v.rearrange("p h (b r) -> p (h b) r", r=2 * m)
            return pairs[:, :, 0:m], pairs[:, :, m:2 * m], pairs[:, :, m - 1:m].to_broadcast([P, HB * P // (2 * m), m])

        g_kdT = region(TMP + 2048, HB, P)
        g_s0 = region(TMP + 2560, HB, DVB)
        g_o = region(TMP, T, D)
        merged = z[:, :, C_QB:C_QB + D]
        f_acc, f_sg, f_p = region(0, 4, S), region(1024, 4, S), region(2048, 4, S)
        p_band, p_inv, p_tmp, p_scale = region(3072, 4, 3 * P), region(4608, 4, P), region(5120, 4 * WB), region(8192, D)
        cv = region(0, XBCC, S)
        zs = region(0, T, DI)
        xs = region(8192, T, DI)
        s_b0 = region(12288, NG, P)
        s_ex, s_cb = (region(13312, HPG, P), region(13824, HPG, P)), region(14336, P)
        s_xd, s_xe, s_st = (region(14464, HPG, HD), region(14720, HPG, HD)), region(14976, HPG, HD), region(15232, HPG, HD)
        ssd_junk = region(13312, DI)
        (dt, dta, acs, eacs, tend, ea, dskip2, lgt, lg2) = (sm[:, k, :] for k in range(9))
        c_acc = region(13312, 4, S)

        def cv_at(b):
            return cv[:, 4 * b:4 * b + 4, :]

        def cv_dyn(i, b):
            return arena[:, bass.ds(i * (12 * S) + 4 * b * S, 4 * S)].rearrange("p (c s) -> p c s", c=4)

        def xt_dst(r):
            if r < 8:
                return xs[:, r // 4, (r % 4) * 512:(r % 4 + 1) * 512]
            return s_b0[:, 4 * (r - 8):4 * (r - 8) + 4, :].rearrange("p g n -> p (g n)")

        SCAT = (0, 1, 6, 7)
        m_hT = region(0, DC, S)
        m_p, m_pt = region(2048, T, P), region(2304, T, P)
        m_gt, m_gt2 = region(2560, S), region(2816, S)
        m_bc = region(3072, 4, S)
        m_sg, m_act, m_y = region(4096, 512), region(4608, 512), region(5120, D)
        m_rt = region(6144, 24, T * NE)
        m_128 = m_rt[:, 19, 0:1]
        fin_w = region(8192, D)
        fin_o = region(9216, T, D)

        at_ss, at_sd, at_n, at_T, at_c = (sem("at_" + k) for k in ("ss", "sd", "n", "T", "c"))
        at_sc, at_m, at_e, at_pt, at_pc, at_o, at_y = (sem("at_" + k) for k in ("sc", "m", "e", "pt", "pc", "o", "y"))
        gl_T, gl_c, gl_g, gl_y, gl_l, gl_b = (sem("gl_" + k) for k in ("T", "c", "g", "y", "l", "b"))
        gl_d, gl_e, gl_p, gl_a, gl_m = (sem("gl_" + k) for k in ("d", "e", "p", "a", "m"))
        gl_i, gl_x, gl_k, gl_kT, gl_kc, gl_s, gl_sc, gl_o, gl_ss, gl_sd, gl_r, gl_on, gl_yb = (
            sem("gl_" + k) for k in ("i", "x", "k", "kT", "kc", "s", "sc", "o", "ss", "sd", "r", "on", "yb"))
        br_g, br_a, br_m = sem("br_g"), sem("br_a"), sem("br_m")
        f_one, f_tap, f_conv, f_silu, f_mult, f_hi, f_lo, f_vec = (
            sem("f_" + k) for k in ("one", "tap", "conv", "silu", "mult", "hi", "lo", "vec"))

        pl_band, pl_ready = sem("pl_band"), sem("pl_ready")
        fin_done = sem("fin_done")
        sd_y, sd_l, sd_dta, sd_acs, sd_te, sd_ex = (sem("sd_" + k) for k in ("y", "l", "dta", "acs", "te", "ex"))
        c_vec, c_tap, c_one, c_two, c_conv, c_silu = (sem("c_" + k) for k in ("vec", "tap", "one", "two", "conv", "silu"))
        xt_ps, xt_act, xt_dve, zs_done = sem("xt_ps"), sem("xt_act"), sem("xt_dve"), sem("zs_done")
        st_skip, st_xd, st_seg, st_ex, st_cb, st_w, st_y, st_s, st_sc, st_acc = (
            sem("st_" + k) for k in ("skip", "xd", "seg", "ex", "cb", "w", "y", "s", "sc", "acc"))
        sy_gated, sy_done = sem("sy_gated"), sem("sy_done")
        r_T, r_h, r_lg, r_m, r_e, r_g, r_rank, r_tab, r_diag, r_bc = (
            sem("r_" + k) for k in ("T", "h", "lg", "m", "e", "g", "rank", "tab", "diag", "bc"))
        m_pk, m_gather, m_ahi, m_alo, m_silu, m_mult, m_tr, m_phi, m_plo, m_y_done, m_scat = (
            sem("m_" + k) for k in ("p", "gather", "ahi", "alo", "silu", "mult", "tr", "phi", "plo", "y", "scat"))
        up_tail = sem("up_tail")
        pool_in = sem("pool_in")

        @block.gpsimd
        def _(pool):
            n = [0]

            def link(ins):
                n[0] += 1
                ins.then_inc(s_const, 1)
                pool.wait_ge(s_const, n[0])

            link(nc.gpsimd.memset(cst[:, 0:3 * P], 0.0))
            link(nc.gpsimd.memset(ones, 1.0))
            link(nc.gpsimd.memset(amask, 0.0))
            link(nc.gpsimd.affine_select(out=ident, in_=ident, compare_op=ALU.not_equal, fill=1.0, base=0,
                                         pattern=[[-1, P]], channel_multiplier=1))
            link(nc.gpsimd.affine_select(out=upper, in_=upper, compare_op=ALU.is_gt, fill=1.0, base=0,
                                         pattern=[[-1, P]], channel_multiplier=1))
            link(nc.gpsimd.affine_select(out=lower, in_=lower, compare_op=ALU.is_ge, fill=1.0, base=0,
                                         pattern=[[1, P]], channel_multiplier=-1))
            link(nc.gpsimd.affine_select(out=amask[:, 0:P], in_=amask[:, 0:P], compare_op=ALU.is_gt, fill=-3e38, base=0,
                                         pattern=[[1, P]], channel_multiplier=-1))
            link(nc.gpsimd.affine_select(out=amask[:, P:S], in_=amask[:, P:S], compare_op=ALU.is_ge, fill=-3e38, base=0,
                                         pattern=[[-1, P]], channel_multiplier=1))
            link(nc.gpsimd.iota(iota_row, pattern=[[1, P]], base=0, channel_multiplier=0,
                                allow_small_or_imprecise_dtypes=True))
            link(nc.gpsimd.iota(iota_col, pattern=[[0, 1]], base=0, channel_multiplier=1,
                                allow_small_or_imprecise_dtypes=True))
            for lv in range(7):
                m = 64 >> lv
                link(nc.gpsimd.memset(lmask[:, lv, :], 0.0))
                right = lmask[:, lv, :].rearrange("p (b r) -> p b r", r=2 * m)[:, :, m:2 * m]
                link(nc.gpsimd.memset(right, 1.0))
                link(nc.gpsimd.affine_select(out=right, in_=right, compare_op=ALU.is_ge, fill=0.0, base=0,
                                             pattern=[[-2 * m, P // (2 * m)], [0, m]], channel_multiplier=1))
                link(nc.gpsimd.affine_select(out=right, in_=right, compare_op=ALU.is_ge, fill=0.0, base=m - 1,
                                             pattern=[[2 * m, P // (2 * m)], [0, m]], channel_multiplier=-1))
            pool.wait_ge(gl_b, 1)
            for n in range(T * LEVELS):
                if n >= 4:
                    pool.wait_ge(gl_a, n - 1)
                left, right, middle = halves(g_b[:, n % 2], n // 2)
                to_left, to_right, _ = halves(g_f[n % 4], n // 2)
                nc.gpsimd.tensor_tensor(to_left, middle, left, ALU.subtract)
                nc.gpsimd.tensor_tensor(to_right, right, middle, ALU.subtract).then_inc(gl_d, 1)
            pool.wait_ge(gl_a, T * LEVELS + 1)
            nc.gpsimd.tensor_tensor(g_e[:, 0], g_b[:, 0, :, P - 1:P].to_broadcast([P, HB, P]), g_b[:, 0],
                                    ALU.subtract).then_inc(gl_i, 1)
            if level >= PHASES.index("pool"):
                pool.wait_ge(x_new, UPD["mix"])
                K = Chain(pool, "band_chain")
                for g in range(4):
                    w = 2 << g
                    first, across, second = (p_band[:, g, k * P:(k + 1) * P] for k in range(3))
                    nc.gpsimd.memset(first, 1.0)
                    K.link(nc.gpsimd.memset(p_band[:, g, P:3 * P], 1.0 / w))
                    for v in (first, second):
                        K.link(nc.gpsimd.affine_select(out=v, in_=v, compare_op=ALU.is_ge, fill=0.0, base=0,
                                                       pattern=[[1, P]], channel_multiplier=-1))
                        K.link(nc.gpsimd.affine_select(out=v, in_=v, compare_op=ALU.is_ge, fill=0.0, base=w - 1,
                                                       pattern=[[-1, P]], channel_multiplier=1))
                    nc.gpsimd.affine_select(out=across, in_=across, compare_op=ALU.is_ge, fill=0.0, base=w - 1 - P,
                                            pattern=[[-1, P]], channel_multiplier=1)
                    nc.gpsimd.affine_select(out=second, in_=second, compare_op=ALU.not_equal, fill=1.0 / w - 1.0, base=0,
                                            pattern=[[-1, P]], channel_multiplier=1).then_inc(pl_band, 1)
                pool.wait_ge(x_new, UPD["ffn0"])
                pool.dma_start(p_scale, I["pool_scale_2"].to_broadcast([P, D])).then_inc(pool_in, 16)
            if level >= 4:
                pool.wait_ge(sd_dta, 1)
                pool.wait_ge(sd_ex, 1)
                pool.wait_ge(xt_act, 5)
                pool.wait_ge(xt_dve, 5)
                pool.wait_ge(s_rowv, 64)
                for k in range(2 * NG):
                    g, t = k // 2, k % 2
                    heads = slice(t * NH + HPG * g, t * NH + HPG * (g + 1))
                    xv = xs[:, t, g * 256:(g + 1) * 256].rearrange("p (r e) -> p r e", r=HPG)
                    if k >= 2:
                        pool.wait_ge(st_y, k - 1)
                    nc.gpsimd.tensor_tensor(s_xd[k % 2], xv, bcast(dt[:, heads], 2, HD), ALU.mult).then_inc(st_xd, 1)
                    pool.wait_ge(st_xd, 3 * g + (1 if t == 0 else 3))
                    if t == 0:
                        if g:
                            pool.wait_ge(st_s, g)
                        nc.gpsimd.tensor_tensor(s_xe, s_xd[0], bcast(tend[:, heads], 2, HD), ALU.mult).then_inc(st_xd, 1)
                    nc.gpsimd.tensor_tensor(xv, xv, bcast(d_skip[:, HPG * g:HPG * (g + 1)], 2, HD),
                                            ALU.mult).then_inc(st_skip, 1)
            if level >= PHASES.index("all"):
                pool.wait_ge(x_new, UPD["ssd"])
                pool.dma_start(fin_w, I["final_norm_w_2"].unsqueeze(0).to_broadcast([P, D])).then_inc(pool_in, 16)
                slots = m_rt[:, 13, 0:2 * T]
                slot_id = m_rt[:, 18, 0:1]
                pool.wait_ge(m_pk, 1)
                pool.wait_ge(r_g, 1)
                n_tasks = pool.value_load(tasks[0:1, 15:16], min_val=1, max_val=MAX_TASKS)
                L = Chain(pool, "task_chain")
                with pool.Fori(0, n_tasks) as i:
                    L.again(i, 3)
                    pool.wait_ge(x_new, 4 * i + UPD["ssd"])
                    nc.gpsimd.tensor_tensor(slots, slots, m_128.to_broadcast([P, 2 * T]), ALU.subtract)
                    nc.gpsimd.tensor_scalar(m_gt, m_bc[:, 0, :], slot_id, None, ALU.is_equal)
                    L.link(nc.gpsimd.tensor_scalar(m_gt2, m_bc[:, 1, :], slot_id, None, ALU.is_equal))
                    nc.gpsimd.tensor_tensor(m_gt, m_gt, m_bc[:, 2, :], ALU.mult)
                    L.link(nc.gpsimd.tensor_tensor(m_gt2, m_gt2, m_bc[:, 3, :], ALU.mult))
                    nc.gpsimd.tensor_tensor(m_gt, m_gt, m_gt2, ALU.add)
                    pool.wait_ge(m_gather, i + 1)
                    nc.gpsimd.tensor_tensor(slot_id, slot_id, m_128, ALU.add)
                    for t in range(T):
                        nc.gpsimd.tensor_scalar(m_pt[:, t, :], iota_row, slots[:, t:t + 1], None, ALU.is_equal)
                    for t in range(T):
                        last = nc.gpsimd.tensor_scalar(m_p[:, t, :], iota_row, slots[:, T + t:T + t + 1], None,
                                                       ALU.is_equal)
                    L.link(last)
                    nc.gpsimd.tensor_tensor(m_p, m_p, m_pt, ALU.add).then_inc(m_pk, 1)
                    L.close()


        @block.sync
        def _(sp):
            sp.dma_start(x[:, :, :], x_v).then_inc(s_x, 16)

            def in_block(u, cols, n=WB, rounds=0):
                for half in range(2):
                    load(sp, u + half, w_in_v[:, 4 * half:4 * half + 4, cols], rounds)

            u0 = UNIT["in"]
            for b in range(3):
                in_block(u0 + 2 * b, slice(b * WB, (b + 1) * WB))
            with sp.Fori(1, 3) as i:
                for b in range(3):
                    for half in range(2):
                        u = u0 + 2 * b + half
                        sp.wait_ge(lo_done, RAW * i + u - RAW + 1)
                        sp.dma_start(raw[:, u % RAW, :].rearrange("p (k n) -> p k n", k=4),
                                     w_in_v[:, 4 * half:4 * half + 4, bass.ds((3 * i + b) * WB, WB)]
                                     ).then_inc(raw_full[u % RAW], 16)
            for b in range(9, 12):
                n = min(WB, IN_W - b * WB)
                in_block(u0 + 2 * b, slice(b * WB, b * WB + n), n)
            for name, src, n in (("wa", wa_v, 2), ("wb", wb_v, 4), ("wo", wo_v, 4)):
                for k in range(n):
                    load(sp, UNIT[name] + k, src[:, 2 * k:2 * k + 2, :])

            def ffn(f):
                u0 = UNIT[f"ffn{f}"]
                gate, up, down = ffn_gate_v[f], ffn_up_v[f], ffn_down_v[f]

                def two(u, src, cols, rounds=0):
                    for half in range(2):
                        load(sp, u + half, src[:, 4 * half:4 * half + 4, cols], rounds)

                two(u0, gate, slice(0, WB))
                two(u0 + 2, up, slice(0, WB))
                with sp.Fori(0, 4) as i:
                    two(u0 + 4, gate, bass.ds(i * WB + WB, WB), i)
                    for half in range(2):
                        load(sp, u0 + 6 + half, down[:, bass.ds(4 * i + 2 * half, 2), :], i)
                    two(u0 + 8, up, bass.ds(i * WB + WB, WB), i)
                views = [raw[:, (u0 + 28 + half) % RAW, :].rearrange("p (k n) -> p k n", k=4) for half in range(2)]
                for half in range(2):
                    sp.wait_ge(lo_done, u0 + 28 + half - RAW + 1)
                    sp.dma_start(views[half][:, :, 256:512], up[:, 4 * half:4 * half + 4, 5 * WB:FF]
                                 ).then_inc(up_tail, 16)
                sp.wait_ge(up_tail, 32 * (f + 1))
                for half in range(2):
                    load(sp, u0 + 28 + half, gate[:, 4 * half:4 * half + 4, 5 * WB:FF],
                         part=views[half][:, :, 0:256])
                for k in range(3):
                    load(sp, u0 + 30 + k, down[:, 16 + 2 * k:18 + 2 * k, :])

            if level >= 1:
                ffn(0)
            if level >= 2:
                load(sp, UNIT["pool"], pool_v)
            if level >= 3:
                ffn(1)
            if level >= 4:
                load(sp, UNIT["dt"], ssd_in_v[:, :, DI + XBC:DI + XBC + NH])
                u0 = UNIT["xbc"]
                with sp.Fori(0, 2) as i:
                    for b in range(3):
                        for half in range(2):
                            load(sp, u0 + 2 * b + half,
                                 ssd_in_v[:, 4 * half:4 * half + 4, bass.ds(i * 3 * WB + DI + b * WB, WB)], i)
                for b in range(6, 8):
                    for half in range(2):
                        load(sp, u0 + 2 * b + half,
                             ssd_in_v[:, 4 * half:4 * half + 4, DI + b * WB:DI + (b + 1) * WB])
                for b in range(4):
                    for half in range(2):
                        load(sp, UNIT["z"] + 2 * b + half,
                             ssd_in_v[:, 4 * half:4 * half + 4, b * WB:(b + 1) * WB])
                for k in range(8):
                    load(sp, UNIT["sout"] + k, ssd_out_v[:, 2 * k:2 * k + 2, :])
            if level >= 5:
                M0 = UNIT["moe"]
                sp.wait_ge(r_tab, 1)
                n_tasks = sp.value_load(tasks[0:1, 15:16], min_val=1, max_val=MAX_TASKS)

                def moe_load(u, src, rounds):
                    sp.wait_ge(lo_done, RAW * rounds + (M0 + u - RAW + 1))
                    sp.dma_start(raw[:, (M0 + u) % RAW, :].rearrange("p (k n) -> p k n", k=src.shape[-2]),
                                 src).then_inc(raw_full[(M0 + u) % RAW], 16)

                with sp.Fori(0, n_tasks) as i:
                    e = sp.value_load(tasks[0:1, bass.ds(i, 1)], min_val=0, max_val=NE - 1)

                    def two(u, src, cols, rounds):
                        for half in range(2):
                            moe_load(u + half, src[:, bass.ds(e, 1), 4 * half:4 * half + 4, cols]
                                     .rearrange("p a k n -> p (a k) n"), rounds)

                    def down(u, k0, rounds):
                        for half in range(2):
                            moe_load(u + half, moe_down_v[:, bass.ds(e, 1), bass.ds(k0 + 2 * half, 2), :]
                                     .rearrange("p a k n -> p (a k) n"), rounds)

                    two(0, moe_gate_v, slice(0, WB), 7 * i)
                    two(2, moe_up_v, slice(0, WB), 7 * i)
                    with sp.Fori(1, 7) as j:
                        n = 7 * i + j - 1
                        two(4, moe_gate_v, bass.ds(j * WB, WB), n)
                        two(6, moe_up_v, bass.ds(j * WB, WB), n)
                        down(8, j * 4 - 4, n)
                    down(4, 24, 7 * i + 6)
                for u in range(2):
                    moe_load(u, moe_gate_v[:, 0, 4 * u:4 * u + 4, 0:WB], 7 * n_tasks)
            if level < 5:
                sp.wait_ge(x_new, 4 * (level + 1))
                sp.dma_start(out_v, x[:, :, :]).then_inc(s_out, 16)
            else:
                sp.wait_ge(fin_done, 1)
                sp.dma_start(out_v, fin_o).then_inc(s_out, 16)
            sp.wait_ge(s_out, 16)

        @block.scalar
        def _(act):
            C = Chain(act, "act_chain")
            def row(group, at, src):
                act.dma_start(vrow[at:at + src.shape[0], group, :], src).then_inc(s_vrow, 16)

            def as_rows(v):
                return v.rearrange("(c p) -> c p", p=P)

            row(0, V_MIX, as_rows(I["ln_mix_g"][0]))
            row(0, V_FFN, as_rows(I["ln_ffn_g"][0]))
            row(0, V_CB, as_rows(I["conv_b"][0]))
            row(0, V_CW, I["conv_w"][0].rearrange("w (c p) -> (w c) p", p=P))
            row(0, V_BGK, as_rows(I["b_gk"][0]))
            row(0, V_G2, as_rows(I["gla_norm_g"][0]))
            for at, name in ((V_QG, "q_norm_g"), (V_KG, "k_norm_g")):
                for half in range(2):
                    act.dma_start(vrow[at:at + 1, 0, half * DH:(half + 1) * DH], I[name]).then_inc(s_vrow, 16)
            row(1, V_POOL - P, as_rows(I["pool_norm_w_2"][0]))
            row(1, V_DENSE - P, as_rows(I["dense_norm_w_2"][0]))
            row(1, V_SSD - P, as_rows(I["ssd_norm_w_2"][0]))
            row(1, V_MOE - P, as_rows(I["moe_norm_w_2"][0]))
            row(1, V_GN - P, as_rows(I["ssd_gate_norm_w_2"][0]))
            row(1, V_SCB - P, as_rows(I["ssd_conv_b_2"][0]))
            row(2, 0, I["ssd_conv_w_2"][0].rearrange("w (c p) -> (w c) p", p=P))
            for dst, name in ((sinks, "sinks"), (dt_bias, "ssd_dt_bias_2"), (a_log, "ssd_a_log_2"),
                              (d_skip, "ssd_d_2")):
                act.dma_start(dst, I[name].to_broadcast([P, dst.shape[1]])).then_inc(s_rowv, 16)
            act.dma_start(wr[:, :, :], rows(I["moe_w_router_2"][0])).then_inc(s_small, 16)
            act.dma_start(wgk, I["w_gk_up"][0]).then_inc(s_small, 16)

            norm_act(act, "mix", C)
            act.wait_ge(s_vecT, 1)
            nc.scalar.activation(vec[:, 0:VA_N], ps[7][:, 0:VA_N], ACT.Copy)
            nc.scalar.activation(vec[:, P:P + VB_N], ps[7][:, P:P + VB_N], ACT.Copy)
            nc.scalar.activation(vec[:, 2 * P:3 * P], ps[7][:, 2 * P:3 * P], ACT.Copy).then_inc(s_vec, 1)
            act.wait_ge(s_vec, 1)
            turn_act(act, "mix", chunks_of(a0_hi), DC, lambda c: V_MIX + c)

            u0 = UNIT["in"]
            for u in range(2):
                split_hi(act, u0 + u)

            def in_block(b, rounds, cols, n=WB):
                for u in (u0 + 2 * b + 2, u0 + 2 * b + 3):
                    split_hi(act, u, rounds)
                act.wait_ge(unit_used, used(u0 + 2 * b + 1, rounds))
                nc.scalar.activation(z[:, 0, cols], ps[2 * (b % 3)][:, 0:n], ACT.Copy).then_inc(z_act, 1)

            with act.Fori(0, 2) as i:
                for b in range(3):
                    in_block(b, i, bass.ds(i * 3 * WB + b * WB, WB))

            def at_copy_turned():
                act.wait_ge(at_T, 1)
                for c in range(5):
                    g = V_QG if c < 4 else V_KG
                    last = nc.scalar.activation(at_qkT[:, c, :], ps[4 + c // 2][:, (c % 2) * S:(c % 2 + 1) * S], ACT.Copy,
                                                scale=vec[:, g:g + 1])
                last.then_inc(at_c, 1)

            def at_exp(step):
                w = at_width(step)
                act.wait_ge(at_m, step + 1)
                nc.scalar.activation(at_sink[step], at_sink[step], ACT.Exp)
                for c in range(4):
                    s = at_s[step][:, c * w:(c + 1) * w]
                    last = nc.scalar.activation(s, s, ACT.Exp, bias=at_neg[step][:, c:c + 1],
                                                accum_out=at_sum[step][:, c:c + 1])
                last.then_inc(at_e, 1)

            def at_copy_weights(step):
                act.wait_ge(at_pt, step + 1)
                for k in range(at_width(step) // P):
                    last = nc.scalar.activation(at_s[step][:, k * 512:(k + 1) * 512], ps[AT_BANKS[step][k]][:, :], ACT.Copy)
                last.then_inc(at_pc, 1)

            for v in range(12, 24):
                split_hi(act, u0 + v + 2)
                if v == 12:
                    act.wait_ge(at_ss, 1)
                    nc.scalar.activation(stat[:, 28:48], stat[:, 8:28], ACT.Sqrt, scale=1.0 / DH, bias=EPS).then_inc(at_sd, 1)
                    C.link(nc.scalar.mul(vec[:, V_QG:V_QG + 1], vec[:, V_QG:V_QG + 1], DH ** -0.5))
                if v == 13:
                    at_copy_turned()
                if v == 16:
                    at_exp(0)
                    at_exp(1)
                if v == 17:
                    at_copy_weights(0)
                    at_copy_weights(1)
                    at_exp(2)
                if v == 18:
                    at_copy_weights(2)
                if v == 21:
                    at_exp(3)
                if v == 22:
                    at_copy_weights(3)
                if v % 2:
                    b = v // 2
                    n = min(WB, IN_W - b * WB)
                    act.wait_ge(unit_used, used(u0 + v))
                    nc.scalar.activation(z[:, 0, b * WB:b * WB + n], ps[2 * (b % 2)][:, 0:n], ACT.Copy).then_inc(z_act, 1)
            act.wait_ge(z_dve, 12)
            nc.scalar.activation(z[:, :, C_RB:C_RB + VB], z[:, :, C_RB:C_RB + VB], ACT.Silu).then_inc(gl_r, 1)
            turn_act(act, "ya", chunks_of(a1_hi), 4, None)

            act.wait_ge(gl_T, 1)
            for t in range(T):
                nc.scalar.mul(g_q[:, t, :, :], ps[t][:, :].rearrange("p (h i) -> p h i", h=HB), DKB ** -0.5)
                nc.scalar.activation(g_k[:, t, :, :], ps[2 + t][:, :].rearrange("p (h i) -> p h i", h=HB), ACT.Copy)
            nc.scalar.activation(g_lrT[0:GKR, :, :], ps[4][0:GKR, 0:S].rearrange("p (t i) -> p t i", t=T),
                                 ACT.Copy).then_inc(gl_c, 1)
            act.wait_ge(gl_y, 1)
            C.link(nc.scalar.activation(g_qe, g_e, ACT.Abs))
            C.link(nc.scalar.activation(g_qe, g_qe, ACT.Exp, scale=-1.0))
            nc.scalar.activation(g_qe, g_qe, ACT.Ln, bias=1.0).then_inc(gl_l, 1)
            nc.scalar.activation(z[:, :, C_GA:C_GA + 2 * D], z[:, :, C_GA:C_GA + 2 * D], ACT.Sigmoid).then_inc(br_g, 1)
            for n in range(T * LEVELS):
                act.wait_ge(gl_d, n + 1)
                nc.scalar.activation(g_f[n % 4], g_f[n % 4], ACT.Exp, scale=1.0 / GATE_NORM).then_inc(gl_e, 1)
            act.wait_ge(gl_i, 1)
            nc.scalar.activation(g_e[:, 0], g_e[:, 0], ACT.Exp, scale=1.0 / GATE_NORM)
            act.wait_ge(gl_a, T * LEVELS + 2)
            nc.scalar.activation(g_e[:, 1], g_b[:, 1], ACT.Exp, scale=1.0 / GATE_NORM).then_inc(gl_x, 1)
            act.wait_ge(gl_kT, 1)
            nc.scalar.activation(g_kdT, ps[4][:, :].rearrange("p (h i) -> p h i", h=HB), ACT.Copy).then_inc(gl_kc, 1)
            act.wait_ge(gl_s, 1)
            for k in range(2):
                last = nc.scalar.activation(g_s0[:, 2 * k:2 * k + 2, :],
                                            ps[5 + k][:, :].rearrange("p (h e) -> p h e", h=2), ACT.Copy)
            last.then_inc(gl_sc, 1)
            act.wait_ge(gl_o, 1)
            for t in range(T):
                for hh in range(HB):
                    last = nc.scalar.activation(junk[:, hh * DVB:(hh + 1) * DVB],
                                                ps[4 + 2 * t + hh // 2][:, (hh % 2) * DVB:(hh % 2 + 1) * DVB],
                                                ACT.Square, accum_out=stat[:, 8 + 4 * t + hh:9 + 4 * t + hh])
                C.link(last)
            nc.scalar.activation(stat[:, 28:36], stat[:, 8:16], ACT.Sqrt, scale=1.0 / DVB, bias=EPS).then_inc(gl_sd, 1)
            turn_act(act, "yb", chunks_of(a0_hi), DC, lambda c: V_G2 + c % 2)

            u0 = UNIT["wa"]
            for u in range(2, 12):
                split_hi(act, u0 + u)
                if u == 7:
                    turn_act(act, "merged", chunks_of(a1_hi), DC, None)

            def ffn(f):
                u0 = UNIT[f"ffn{f}"]
                norm_act(act, f"ffn{f}", C)
                turn_act(act, f"ffn{f}", chunks_of(a0_hi), DC, lambda c: (V_FFN if f == 0 else V_DENSE) + c)

                def first_tap(i, nf=4):
                    for fc in range(nf):
                        last = nc.scalar.activation(f_acc[:, fc, :], ps[fc // 2][:, (fc % 2) * S:(fc % 2 + 1) * S],
                                                    ACT.Identity, scale=taps[:, 2, fc:fc + 1],
                                                    bias=taps[:, 4, fc:fc + 1])
                        if fc % 2 == 1:
                            last.then_inc(f_tap, 1)

                def step(us, rounds, gate_unit, i, nf=4, dst=0, hi=True):
                    split_hi(act, us[0], rounds)
                    split_hi(act, us[1], rounds)
                    act.wait_ge(unit_used, used(gate_unit, rounds))
                    if f == 0:
                        act.wait_ge(f_vec, i + 1)
                        first_tap(i, nf)
                    for u in us[2:4]:
                        split_hi(act, u, rounds)
                    if f == 0:
                        act.wait_ge(f_conv, i + 1)
                        nc.scalar.activation(f_sg[:, 0:nf, :], f_acc[:, 0:nf, :], ACT.Silu).then_inc(f_silu, 1)
                    else:
                        for k in range(nf // 2):
                            last = nc.scalar.activation(f_sg[:, 2 * k:2 * k + 2, :],
                                                        ps[k][:, :].rearrange("p (c s) -> p c s", c=2), ACT.Silu)
                        last.then_inc(f_silu, 1)
                    for u in us[4:]:
                        split_hi(act, u, rounds)
                    act.wait_ge(f_mult, 6 * f + i + 1)
                    nc.scalar.activation(a1_hi[:, dst:dst + nf, :], f_p[:, 0:nf, :], ACT.Copy).then_inc(f_hi, 1)

                step([u0 + 2, u0 + 3, u0 + 4, u0 + 5], 0, u0 + 1, 0)
                with act.Fori(0, 4) as i:
                    step([u0 + 6 + k for k in range(6)], i, u0 + 5, i + 1)
                step([u0 + 30, u0 + 31], 0, u0 + 29, 5, 2, 4)
                for u in range(32, 35):
                    split_hi(act, u0 + u)

            if level >= 1:
                ffn(0)
            if level >= 2:
                norm_act(act, "pool", C)
                turn_act(act, "pooled", chunks_of(a1_hi), DC, lambda c: V_POOL + c)
                split_hi(act, UNIT["ffn1"] + 1)
            if level >= 3:
                ffn(1)
            if level >= 4:
                D0, X0, Z0, O0 = UNIT["dt"], UNIT["xbc"], UNIT["z"], UNIT["sout"]
                norm_act(act, "ssd", C)
                turn_act(act, "ssd", chunks_of(a0_hi), DC, lambda c: V_SSD + c)
                split_hi(act, X0 + 1)
                act.wait_ge(gl_g, 1)
                nc.scalar.activation(ea[:, 0:NH], a_log, ACT.Exp)
                act.wait_ge(sd_y, 1)
                C.link(nc.scalar.activation(lg2, lgt, ACT.Abs))
                C.link(nc.scalar.activation(lg2, lg2, ACT.Exp, scale=-1.0))
                nc.scalar.activation(lg2, lg2, ACT.Ln, bias=1.0).then_inc(sd_l, 1)
                split_hi(act, X0 + 2)

                def conv_block(b, rounds, blk, chunk):
                    split_hi(act, X0 + 2 * b + 3, rounds)
                    act.wait_ge(unit_used, used(X0 + 2 * b + 1, rounds))
                    act.wait_ge(c_vec, blk + 1)
                    for fc in range(4):
                        last = nc.scalar.activation(c_acc[:, fc, :], ps[2 * (b % 3) + fc // 2][:, (fc % 2) * S:(fc % 2 + 1) * S],
                                                    ACT.Identity, scale=taps[:, 3, fc:fc + 1],
                                                    bias=taps[:, 4, fc:fc + 1])
                        if fc % 2 == 1:
                            last.then_inc(c_tap, 1)
                    split_hi(act, X0 + 2 * b + 4, rounds)
                    act.wait_ge(c_conv, blk + 1)
                    nc.scalar.activation(chunk, c_acc, ACT.Silu).then_inc(c_silu, 1)
                    act.wait_ge(c_silu, blk + 1)

                with act.Fori(0, 2) as i:
                    for b in range(3):
                        conv_block(b, i, 3 * i + b, cv_dyn(i, b))
                for b in range(6, 8):
                    conv_block(b, 0, b, cv_at(b))
                act.wait_ge(sd_te, 1)
                nc.scalar.activation(eacs, acs, ACT.Exp)
                nc.scalar.activation(tend, tend, ACT.Exp).then_inc(sd_ex, 1)
                for r in range(0, 10, 2):
                    act.wait_ge(xt_ps, r + 1)
                    nc.scalar.activation(xt_dst(r), ps[r % 4][:, :], ACT.Copy).then_inc(xt_act, 1)
                for b in range(4):
                    split_hi(act, Z0 + 2 * b + 3)
                    split_hi(act, Z0 + 2 * b + 4)
                    act.wait_ge(unit_used, used(Z0 + 2 * b + 1))
                    for t in range(T):
                        last = nc.scalar.activation(zs[:, t, b * WB:(b + 1) * WB], ps[4 + 2 * (b % 2) + t][:, :], ACT.Silu)
                    last.then_inc(zs_done, 1)
                for k in range(2 * NG):
                    act.wait_ge(st_seg, k + 1)
                    if k >= 2:
                        act.wait_ge(st_y, k - 1)
                    g, t = k // 2, k % 2
                    for r in range(HPG):
                        hd = t * NH + HPG * g + r
                        last = nc.scalar.activation(s_ex[k % 2][:, r, :], ps[k % 2][:, r * P:(r + 1) * P], ACT.Relu,
                                                    scale=-1.0, bias=acs[:, hd:hd + 1])
                    C.link(last)
                    nc.scalar.activation(s_ex[k % 2], s_ex[k % 2], ACT.Exp, scale=-1.0).then_inc(st_ex, 1)
                    if k % 2 == 0:
                        act.wait_ge(st_s, k // 2 + 1)
                        nc.scalar.activation(s_st, ps[6][:, 0:256].rearrange("p (r e) -> p r e", r=HPG),
                                             ACT.Copy).then_inc(st_sc, 1)
                act.wait_ge(sy_gated, 1)
                for t in range(T):
                    C.link(nc.scalar.activation(ssd_junk, xs[:, t, :], ACT.Square, accum_out=ss[:, t:t + 1]))
                norm_stat(act, DI, SSM_EPS)
                turn_act(act, "y", chunks_two(a0_hi, a1_hi), 2 * DC, lambda c: V_GN + c)
                for u in range(3, 8):
                    split_hi(act, O0 + u)
            if level >= 5:
                M0 = UNIT["moe"]
                norm_act(act, "moe", C)
                for b in range(4):
                    act.wait_ge(r_T, b + 1)
                    for c in (2 * b, 2 * b + 1):
                        last = nc.scalar.activation(m_hT[:, c, :], ps[b][:, (c % 2) * S:(c % 2 + 1) * S], ACT.Copy,
                                                    scale=vec[:, V_MOE + c:V_MOE + c + 1])
                    last.then_inc(r_h, 1)
                act.wait_ge(r_m, 1)
                nc.scalar.activation(m_rt[:, 20, 0:T], m_rt[:, 20, 0:T], ACT.Exp).then_inc(r_e, 1)
                act.wait_ge(r_bc, 1)
                for k in range(2):
                    last = nc.scalar.activation(m_bc[:, 2 * k:2 * k + 2, :],
                                                ps[2 + k][:, :].rearrange("p (a s) -> p a s", a=2), ACT.Copy)
                last.then_inc(r_g, 1)
                split_hi(act, M0)
                split_hi(act, M0 + 1)

                def tokens_hi(i):
                    act.wait_ge(m_gather, i + 1)
                    for b in range(2):
                        for c in range(4 * b, 4 * b + 4):
                            last = nc.scalar.activation(a0_hi[:, c, 0:P], ps[6 + b][:, (c % 4) * P:(c % 4 + 1) * P],
                                                        ACT.Copy, scale=vec[:, V_MOE + c:V_MOE + c + 1])
                        last.then_inc(m_ahi, 1)

                def product_hi(n):
                    act.wait_ge(m_tr, n + 1)
                    nc.scalar.activation(a1_hi[:, 0:4, 0:P], ps[0][:, :].rearrange("p (c s) -> p c s", c=4),
                                         ACT.Copy).then_inc(m_phi, 1)

                tokens_hi(0)
                n_tasks = act.value_load(tasks[0:1, 15:16], min_val=1, max_val=MAX_TASKS)
                with act.Fori(0, n_tasks) as i:
                    split_hi(act, M0 + 2, 7 * i)
                    split_hi(act, M0 + 3, 7 * i)
                    act.wait_ge(unit_used, used(M0 + 1, 7 * i))
                    nc.scalar.activation(m_sg, ps[2][:, :], ACT.Silu).then_inc(m_silu, 1)
                    split_hi(act, M0 + 4, 7 * i)
                    split_hi(act, M0 + 5, 7 * i)
                    with act.Fori(1, 7) as j:
                        n = 7 * i + j
                        split_hi(act, M0, n)
                        split_hi(act, M0 + 1, n)
                        act.wait_ge(unit_used, RAW * n + M0)
                        act.wait_ge(m_mult, n)
                        nc.scalar.activation(m_sg, ps[2][:, :], ACT.Silu).then_inc(m_silu, 1)
                        product_hi(n - 1)
                        for u in range(2, 6):
                            split_hi(act, M0 + u, n)
                    n = 7 * i + 6
                    tokens_hi(i + 1)
                    product_hi(n)
                    split_hi(act, M0, n + 1)
                    split_hi(act, M0 + 1, n + 1)
                    act.wait_ge(unit_used, RAW * n + (M0 + 6))
                    for k in range(2):
                        last = nc.scalar.activation(m_y[:, k * 512:(k + 1) * 512], ps[4 + k][:, :], ACT.Copy)
                    last.then_inc(m_y_done, 1)
                act.wait_ge(x_new, 4 * n_tasks + UPD["ssd"])
                norm_act(act, "final", C)

        @block.vector
        def _(dve):
            C = Chain(dve, "dve_chain")
            norm_dve(dve, "mix", C)
            dve.wait_ge(s_vec, 1)
            turn_dve(dve, "mix", chunks_of(a0_hi), chunks_of(a0_lo), DC, lambda c: V_MIX + c)

            u0 = UNIT["in"]
            for u in range(2):
                split_lo(dve, u0 + u)

            def in_block(b, rounds, cols, n=WB):
                for u in (u0 + 2 * b + 2, u0 + 2 * b + 3):
                    split_lo(dve, u, rounds)
                dve.wait_ge(unit_used, used(u0 + 2 * b + 1, rounds))
                nc.vector.tensor_copy(z[:, 1, cols], ps[2 * (b % 3) + 1][:, 0:n]).then_inc(z_dve, 1)

            with dve.Fori(0, 2) as i:
                for b in range(3):
                    in_block(b, i, bass.ds(i * 3 * WB + b * WB, WB))

            def at_norm():
                dve.wait_ge(at_sd, 1)
                C.link(nc.vector.reciprocal(stat[:, 28:48], stat[:, 28:48]))
                for t in range(T):
                    r = stat[:, 28 + 10 * t:38 + 10 * t]
                    for j in range(HKV):
                        nc.vector.tensor_tensor(at_qn[:, t, 0:QA].rearrange("p (c j d) -> p j c d", j=HKV, d=DH)[:, j],
                                                z[:, t, j * S:(j + 1) * S].rearrange("p (c d) -> p c d", d=DH),
                                                bcast(r[:, 4 * j:4 * j + 4], 2, DH), ALU.mult)
                    last = nc.vector.tensor_tensor(at_qn[:, t, QA:640].rearrange("p (j d) -> p j d", d=DH),
                                                   z[:, t, C_KA:C_VA].rearrange("p (j d) -> p j d", d=DH),
                                                   bcast(r[:, 8:10], 2, DH), ALU.mult)
                last.then_inc(at_n, 1)

            def at_maximum(step):
                j, w = step % 2, at_width(step)
                dve.wait_ge(at_sc, step + 1)
                per = 512 // w
                for i, bank in enumerate(AT_BANKS[step]):
                    last = nc.vector.tensor_tensor(
                        at_s[step][:, i * 512:(i + 1) * 512].rearrange("p (c k) -> p c k", c=per),
                        ps[bank][:, :].rearrange("p (c k) -> p c k", c=per), bcast(amask[:, S - w:S], 1, per), ALU.add)
                C.link(last)
                C.link(nc.vector.tensor_reduce(at_max[step], at_s[step][:, 0:4 * w].rearrange("p (c k) -> p c k", c=4),
                                               AX.X, ALU.max))
                C.link(nc.vector.scalar_tensor_tensor(at_neg[step], at_max[step], -1.0, at_nsink[:, 4 * j:4 * j + 4],
                                                      ALU.mult, ALU.min))
                nc.vector.tensor_tensor(at_sink[step], sinks[:, 4 * j:4 * j + 4], at_neg[step],
                                        ALU.add).then_inc(at_m, 1)

            def at_divide(t):
                dve.wait_ge(at_o, 2 * t + 2)
                rs = stat[:, 8 + 8 * t:16 + 8 * t]
                C.link(nc.vector.tensor_tensor(rs, rs, stat[:, 40 + 8 * t:48 + 8 * t], ALU.add))
                C.link(nc.vector.reciprocal(rs, rs))
                nc.vector.tensor_tensor(ya[:, t, :].rearrange("p (h d) -> p h d", d=DH),
                                        ps[AT_OUT[t]][:, :].rearrange("p (h d) -> p h d", d=DH),
                                        bcast(rs, 2, DH), ALU.mult).then_inc(at_y, 1)

            dve.wait_ge(z_act, 2)
            dve.wait_ge(z_dve, 2)
            dve.wait_ge(s_rowv, 64)
            C.link(nc.vector.tensor_tensor(at_sq, z[:, :, 0:640], z[:, :, 0:640], ALU.mult))
            nc.vector.tensor_reduce(stat[:, 8:28].rearrange("p (t h) -> p t h", t=T),
                                    at_sq.rearrange("p t (h d) -> p t h d", d=DH), AX.X, ALU.add).then_inc(at_ss, 1)
            for v in range(12, 24):
                split_lo(dve, u0 + v + 2)
                if v == 12:
                    at_norm()
                if v == 15:
                    dve.wait_ge(at_n, 1)
                    C.link(nc.vector.tensor_scalar(at_nsink, sinks, -1.0, None, ALU.mult))
                    at_maximum(0)
                    at_maximum(1)
                if v == 16:
                    at_maximum(2)
                if v == 18:
                    at_divide(0)
                if v == 20:
                    at_maximum(3)
                if v == 23:
                    at_divide(1)
                if v % 2:
                    b = v // 2
                    n = min(WB, IN_W - b * WB)
                    dve.wait_ge(unit_used, used(u0 + v))
                    nc.vector.tensor_copy(z[:, 1, b * WB:b * WB + n], ps[2 * (b % 2) + 1][:, 0:n]).then_inc(z_dve, 1)
            turn_dve(dve, "ya", chunks_of(a1_hi), chunks_of(a1_lo), 4, None)

            dve.wait_ge(gl_g, 1)
            for hh in range(HB):
                last = (nc.vector.tensor_scalar(g_e[:, :, hh, :], ps[5 + hh // 2][:, (hh % 2) * S:(hh % 2 + 1) * S]
                                               .rearrange("p (t i) -> p t i", t=T),
                                               vec[:, V_BGK + hh:V_BGK + hh + 1], None, ALU.add))
            last.then_inc(gl_y, 1)
            dve.wait_ge(gl_l, 1)
            for t in range(T):
                C.link(nc.vector.scalar_tensor_tensor(g_e[:, t], g_e[:, t], 0.0, g_qe[:, t], ALU.min, ALU.subtract))
            for t in range(T):
                for hh in range(HB):
                    last = nc.vector.tensor_tensor_scan(g_b[:, t, hh, :], ones, g_e[:, t, hh, :], 0.0,
                                                        ALU.mult, ALU.add)
            last.then_inc(gl_b, 1)
            for t in range(T):
                dve.wait_ge(gl_a, t + 1)
                nc.vector.tensor_tensor(g_acc[:, t], ps[t][:, :].rearrange("p (h i) -> p h i", h=HB),
                                        bcast(ident, 1, HB), ALU.mult).then_inc(gl_m, 1)

            def take(n):
                dve.wait_ge(gl_a, n + 3)
                dve.wait_ge(gl_m, n + 1)
                nc.vector.copy_predicated(g_acc[:, n % 2], bcast(lmask[:, n // 2, :].bitcast(mybir.dt.int16), 1, HB),
                                          ps[(n + 2) % 4][:, :].rearrange("p (h i) -> p h i", h=HB)).then_inc(gl_m, 1)

            for n in range(T * LEVELS):
                t, lv = n % 2, n // 2
                dve.wait_ge(gl_e, n + 1)
                left, right, _ = halves(g_f[n % 4], lv)
                nc.vector.tensor_tensor(left, halves(g_k[:, t], lv)[0], left, ALU.mult)
                nc.vector.tensor_tensor(right, halves(g_q[:, t], lv)[1], right, ALU.mult).then_inc(gl_p, 1)
                if n >= 2:
                    take(n - 2)
            dve.wait_ge(gl_x, 1)
            nc.vector.tensor_tensor(g_e[:, 0], g_k[:, 0], g_e[:, 0], ALU.mult)
            nc.vector.tensor_tensor(g_e[:, 1], g_q[:, 1], g_e[:, 1], ALU.mult).then_inc(gl_k, 1)
            for n in range(T * LEVELS - 2, T * LEVELS):
                take(n)
            dve.wait_ge(gl_sd, 1)
            C.link(nc.vector.reciprocal(stat[:, 28:36], stat[:, 28:36]))
            for t in range(T):
                for k in range(2):
                    last = (nc.vector.tensor_tensor(
                        g_o[:, t, k * 512:(k + 1) * 512].rearrange("p (h e) -> p h e", h=2),
                        ps[4 + 2 * t + k][:, :].rearrange("p (h e) -> p h e", h=2),
                        bcast(stat[:, 28 + 4 * t + 2 * k:30 + 4 * t + 2 * k], 2, DVB), ALU.mult))
            C.link(last)
            dve.wait_ge(gl_r, 1)
            nc.vector.tensor_tensor(g_o, g_o, z[:, :, C_RB:C_RB + VB], ALU.mult).then_inc(gl_yb, 1)
            turn_dve(dve, "yb", chunks_of(a0_hi), chunks_of(a0_lo), DC, lambda c: V_G2 + c % 2)

            u0 = UNIT["wa"]
            for u in range(2, 4):
                split_lo(dve, u0 + u)
            dve.wait_ge(br_g, 1)
            dve.wait_ge(unit_used, used(u0 + 1))
            for t in range(T):
                for half in range(2):
                    cols = slice(C_GA + half * 512, C_GA + (half + 1) * 512)
                    last = nc.vector.tensor_tensor(merged[:, t, half * 512:(half + 1) * 512], ps[4 + 2 * t + half][:, :],
                                                   z[:, t, cols], ALU.mult)
            C.link(last)
            for u in range(4, 8):
                split_lo(dve, u0 + u)
            dve.wait_ge(unit_used, used(UNIT["wb"] + 3))
            for t in range(T):
                for half in range(2):
                    at = slice(half * 512, (half + 1) * 512)
                    gb = z[:, t, C_GB + half * 512:C_GB + (half + 1) * 512]
                    C.link(nc.vector.tensor_tensor(gb, ps[2 * t + half][:, :], gb, ALU.mult))
                    last = nc.vector.tensor_tensor(merged[:, t, at], merged[:, t, at], gb, ALU.add)
            last.then_inc(br_m, 1)
            turn_dve(dve, "merged", chunks_of(a1_hi), chunks_of(a1_lo), DC, None)
            for u in range(8, 12):
                split_lo(dve, u0 + u)

            def update(u_last):
                dve.wait_ge(unit_used, used(u_last))
                for t in range(T):
                    for half in range(2):
                        at = slice(half * 512, (half + 1) * 512)
                        nc.vector.tensor_tensor(x[:, t, at], x[:, t, at], ps[4 + 2 * t + half][:, :],
                                                ALU.add).then_inc(x_new, 1)

            update(UNIT["wo"] + 3)

            def ffn(f):
                u0 = UNIT[f"ffn{f}"]
                norm_dve(dve, f"ffn{f}", C)
                turn_dve(dve, f"ffn{f}", chunks_of(a0_hi), chunks_of(a0_lo), DC,
                         lambda c: (V_FFN if f == 0 else V_DENSE) + c)

                def step(us, rounds, up_unit, i, nf=4, dst=0):
                    if f == 0:
                        for w in range(CONV_W):
                            nc.vector.tensor_copy(taps[:, w, 0:nf], vec[:, bass.ds(i * 4 + (V_CW + w * FFC), nf)])
                        nc.vector.tensor_copy(taps[:, 4, 0:nf], vec[:, bass.ds(i * 4 + V_CB, nf)]).then_inc(f_vec, 1)
                    split_lo(dve, us[0], rounds)
                    split_lo(dve, us[1], rounds)
                    if f == 0:
                        dve.wait_ge(f_vec, i + 1)
                        for tap in (1, 0):
                            sh = 2 - tap
                            for fc in range(nf):
                                if tap == 1 and fc % 2 == 0:
                                    dve.wait_ge(f_tap, i * 2 + fc // 2 + 1)
                                col = (fc % 2) * S
                                last = nc.vector.scalar_tensor_tensor(
                                    f_acc[:, fc, sh:S], ps[fc // 2][:, col:col + S - sh], taps[:, tap, fc:fc + 1],
                                    f_acc[:, fc, sh:S], ALU.mult, ALU.add)
                            if tap == 1:
                                last.then_inc(f_one, 1)
                                dve.wait_ge(f_one, i + 1)
                        last.then_inc(f_conv, 1)
                    for u in us[2:]:
                        split_lo(dve, u, rounds)
                    if f:
                        dve.wait_ge(f_lo, 6 * f + i)
                    dve.wait_ge(f_silu, 6 * f + i + 1)
                    dve.wait_ge(unit_used, used(up_unit, rounds))
                    for k in range(nf // 2):
                        last = nc.vector.tensor_tensor(f_p[:, 2 * k:2 * k + 2, :], f_sg[:, 2 * k:2 * k + 2, :],
                                                       ps[2 + k][:, :].rearrange("p (c s) -> p c s", c=2), ALU.mult)
                    last.then_inc(f_mult, 1)
                    dve.wait_ge(f_hi, 6 * f + i + 1)
                    nc.vector.tensor_tensor(a1_lo[:, dst:dst + nf, :], f_p[:, 0:nf, :],
                                            a1_hi[:, dst:dst + nf, :].bitcast(F32), ALU.subtract).then_inc(f_lo, 1)

                step([u0 + 2, u0 + 3, u0 + 4, u0 + 5], 0, u0 + 3, 0)
                with dve.Fori(0, 4) as i:
                    step([u0 + 6 + k for k in range(6)], i, u0 + 9, i + 1)
                step([u0 + 30, u0 + 31], 0, u0 + 29, 5, 2, 4)
                for u in range(32, 35):
                    split_lo(dve, u0 + u)
                update(u0 + 32)

            if level >= 1:
                ffn(0)
            if level >= 2:
                dve.wait_ge(s_const, N_CONST)
                dve.wait_ge(pl_band, 4)
                for g in range(4):
                    last = nc.vector.tensor_scalar(p_inv[:, g, :], iota_row, 1.0, float(2 << g), ALU.add, ALU.min)
                C.link(last)
                C.link(nc.vector.reciprocal(p_inv, p_inv))
                C.link(nc.vector.tensor_tensor(p_band[:, :, 0:P], p_band[:, :, 0:P], p_inv, ALU.mult))
                nc.vector.tensor_tensor(p_band[:, :, 0:P], p_band[:, :, 0:P], bcast(ident, 1, 4),
                                        ALU.subtract).then_inc(pl_ready, 1)
                norm_dve(dve, "pool", C)
                turn_dve(dve, "pooled", chunks_of(a1_hi), chunks_of(a1_lo), DC, lambda c: V_POOL + c)
                split_lo(dve, UNIT["ffn1"] + 1)
                dve.wait_ge(pool_in, 16)
                dve.wait_ge(unit_used, used(UNIT["pool"]))
                for t in range(T):
                    for half in range(2):
                        at = slice(half * 512, (half + 1) * 512)
                        o = p_tmp[:, (2 * t + half) * 512:(2 * t + half + 1) * 512]
                        C.link(nc.vector.tensor_tensor(o, ps[4 + 2 * t + half][:, :], p_scale[:, at], ALU.mult))
                        nc.vector.tensor_tensor(x[:, t, at], x[:, t, at], o, ALU.add).then_inc(x_new, 1)
            if level >= 3:
                ffn(1)
            if level >= 4:
                D0, X0, Z0, O0 = UNIT["dt"], UNIT["xbc"], UNIT["z"], UNIT["sout"]
                norm_dve(dve, "ssd", C)
                turn_dve(dve, "ssd", chunks_of(a0_hi), chunks_of(a0_lo), DC, lambda c: V_SSD + c)
                split_lo(dve, X0 + 1)
                dve.wait_ge(unit_used, used(D0))
                nc.vector.tensor_tensor(lgt.rearrange("p (t h) -> p t h", t=T),
                                        ps[6][:, 0:T * NH].rearrange("p (t h) -> p t h", t=T),
                                        bcast(dt_bias, 1, T), ALU.add).then_inc(sd_y, 1)
                split_lo(dve, X0 + 2)
                dve.wait_ge(sd_l, 1)
                C.link(nc.vector.scalar_tensor_tensor(dt, lgt, 0.0, lg2, ALU.max, ALU.add))
                nc.vector.scalar_tensor_tensor(dta.rearrange("p (t h) -> p t h", t=T),
                                               dt.rearrange("p (t h) -> p t h", t=T), -1.0, bcast(ea[:, 0:NH], 1, T),
                                               ALU.mult, ALU.mult).then_inc(sd_dta, 1)

                def block_taps(blk):
                    for w in range(SCONV):
                        nc.vector.tensor_copy(taps[:, w, 0:4], vec[:, bass.ds(blk * 4 + (V_SCW + w * XBCC), 4)])
                    nc.vector.tensor_copy(taps[:, 4, 0:4], vec[:, bass.ds(blk * 4 + V_SCB, 4)]).then_inc(c_vec, 1)

                def conv_block(b, rounds, blk):
                    split_lo(dve, X0 + 2 * b + 3, rounds)
                    dve.wait_ge(c_vec, blk + 1)
                    for tap, done in ((2, c_one), (1, c_two), (0, c_conv)):
                        sh = SCONV - 1 - tap
                        for fc in range(4):
                            if tap == 2 and fc % 2 == 0:
                                dve.wait_ge(c_tap, 2 * blk + fc // 2 + 1)
                            o = c_acc[:, fc, sh:S]
                            col = (fc % 2) * S
                            last = nc.vector.scalar_tensor_tensor(
                                o, ps[2 * (b % 3) + fc // 2][:, col:col + S - sh], taps[:, tap, fc:fc + 1], o,
                                ALU.mult, ALU.add)
                        last.then_inc(done, 1)
                        if tap:
                            dve.wait_ge(done, blk + 1)
                    split_lo(dve, X0 + 2 * b + 4, rounds)
                    if b < 7:
                        dve.wait_ge(c_conv, blk + 1)
                        block_taps(blk + 1)

                block_taps(0)
                with dve.Fori(0, 2) as i:
                    for b in range(3):
                        conv_block(b, i, 3 * i + b)
                for b in range(6, 8):
                    conv_block(b, 0, b)
                dve.wait_ge(sd_acs, 1)
                C.link(nc.vector.tensor_copy(acs, ps[7][:, 0:64]))
                nc.vector.tensor_tensor(tend, ps[7][:, 64:128], acs, ALU.subtract).then_inc(sd_te, 1)
                for r in range(1, 10, 2):
                    dve.wait_ge(xt_ps, r + 1)
                    nc.vector.tensor_copy(xt_dst(r), ps[r % 4][:, :]).then_inc(xt_dve, 1)
                for u in range(3, 11):
                    split_lo(dve, Z0 + u)
                dve.wait_ge(sd_ex, 1)

                def accumulate(k):
                    g, t = k // 2, k % 2
                    heads = slice(t * NH + HPG * g, t * NH + HPG * (g + 1))
                    xv = xs[:, t, g * 256:(g + 1) * 256].rearrange("p (r e) -> p r e", r=HPG)
                    dve.wait_ge(st_y, k + 1)
                    dve.wait_ge(st_skip, k + 1)
                    before = ps[7][:, 0:256].rearrange("p (r e) -> p r e", r=HPG)
                    if t:
                        nc.vector.tensor_tensor(before, before, bcast(eacs[:, heads], 2, HD), ALU.mult)
                    last = nc.vector.tensor_tensor(xv, xv, ps[4 + k % 2][:, 0:256].rearrange("p (r e) -> p r e", r=HPG),
                                                   ALU.add)
                    if t:
                        C.link(last)
                        last = nc.vector.tensor_tensor(xv, xv, before, ALU.add)
                    last.then_inc(st_acc, 1)

                for k in range(2 * NG):
                    dve.wait_ge(st_seg, k + 1)
                    if k:
                        dve.wait_ge(st_w, k)
                    nc.vector.tensor_tensor(s_cb, ps[2 + k % 2][:, 0:P], upper, ALU.mult).then_inc(st_cb, 1)
                    dve.wait_ge(st_ex, k + 1)
                    dve.wait_ge(st_cb, k + 1)
                    nc.vector.tensor_tensor(s_ex[k % 2], s_ex[k % 2], bcast(s_cb, 1, HPG), ALU.mult).then_inc(st_w, 1)
                    if k:
                        accumulate(k - 1)
                accumulate(2 * NG - 1)
                dve.wait_ge(st_acc, 2 * NG)
                dve.wait_ge(zs_done, 4)
                nc.vector.tensor_tensor(xs, xs, zs, ALU.mult).then_inc(sy_gated, 1)
                dve.wait_ge(sq_sum, 6)
                C.link(nc.vector.reciprocal(rstd, sd))
                for t in range(T):
                    last = nc.vector.tensor_scalar(xs[:, t, :], xs[:, t, :], rstd[:, t:t + 1], None, ALU.mult)
                last.then_inc(sy_done, 1)
                turn_dve(dve, "y", chunks_two(a0_hi, a1_hi), chunks_two(a0_lo, a1_lo), 2 * DC, lambda c: V_GN + c)
                for u in range(3, 8):
                    split_lo(dve, O0 + u)
                update(O0 + 7)
            if level >= 5:
                M0 = UNIT["moe"]
                norm_dve(dve, "moe", C)
                R = [m_rt[:, k, :] for k in range(20)]
                R3 = [v.rearrange("p (t e) -> p t e", t=T) for v in R]
                lg, eq, oh1, l2, oh2, sl, pr, fc_ = R3[0:8]
                iota_e = iota_row[:, 0:NE]
                iota_b, m1, m2, i1, i2 = R[8][:, 0:NE], R[9][:, 0:T], R[10][:, 0:T], R[11][:, 0:T], R[12][:, 0:T]
                pos = [R[13][:, 0:T], R[13][:, T:2 * T]]
                gate = [R[14][:, 0:T], R[14][:, T:2 * T]]
                nb, end, start = R[15][:, 0:NE], R[16][:, 0:NE], R[17][:, 0:NE]
                slot_id = R[18][:, 0:1]
                e21 = m_rt[:, 20, 0:T]

                dve.wait_ge(r_lg, 1)
                C.link(nc.vector.tensor_copy(R[0], ps[4][:, 0:T * NE]))
                C.link(nc.vector.tensor_scalar(iota_b, iota_e, 64.0, None, ALU.add))
                for src, mx, idx, oh in ((lg, m1, i1, oh1), (l2, m2, i2, oh2)):
                    C.link(nc.vector.tensor_reduce(mx, src, AX.X, ALU.max))
                    C.link(nc.vector.tensor_tensor(eq, src, bcast(mx, 2, NE), ALU.is_equal))
                    for t in range(T):
                        last = nc.vector.scalar_tensor_tensor(fc_[:, t], eq[:, t], -64.0, iota_b, ALU.mult, ALU.add)
                    C.link(last)
                    C.link(nc.vector.tensor_reduce(idx, fc_, AX.X, ALU.min))
                    C.link(nc.vector.tensor_tensor(oh, bcast(iota_e, 1, T), bcast(idx, 2, NE), ALU.is_equal))
                    if oh is oh1:
                        C.link(nc.vector.scalar_tensor_tensor(R[3], R[2], -3e38, R[0], ALU.mult, ALU.add))
                C.link(nc.vector.tensor_tensor(R[5], R[2], R[4], ALU.add))
                nc.vector.tensor_tensor(e21, m2, m1, ALU.subtract).then_inc(r_m, 1)
                dve.wait_ge(r_e, 1)
                C.link(nc.vector.tensor_scalar(gate[0], e21, 1.0, None, ALU.add))
                C.link(nc.vector.reciprocal(gate[0], gate[0]))
                C.link(nc.vector.tensor_tensor(gate[1], e21, gate[0], ALU.mult))
                dve.wait_ge(r_rank, 1)
                count = ps[5][:, 2 * NE:3 * NE]
                C.link(nc.vector.tensor_scalar(nb, count, 0.5, None, ALU.is_gt))
                C.link(nc.vector.tensor_scalar(start, count, P + 0.5, None, ALU.is_gt))
                C.link(nc.vector.tensor_tensor(nb, nb, start, ALU.add))
                C.link(nc.vector.tensor_tensor_scan(end, ones[:, 0:NE], nb, 0.0, ALU.mult, ALU.add))
                C.link(nc.vector.tensor_tensor(start, end, nb, ALU.subtract))
                C.link(nc.vector.tensor_scalar(start, start, float(P), -1.0, ALU.mult, ALU.add))
                C.link(nc.vector.tensor_tensor(m_sg[0:1, 0:16 * NE].rearrange("p (i e) -> p i e", e=NE),
                                               bcast(end[0:1, :], 1, 16), bcast(iota_row[0:1, 0:16], 2, NE),
                                               ALU.is_le))
                C.link(nc.vector.tensor_reduce(m_sg[0:1, 256:272], m_sg[0:1, 0:16 * NE].rearrange("p (i e) -> p i e", e=NE),
                                               AX.X, ALU.add))
                C.link(nc.vector.tensor_scalar(m_sg[0:1, 256:272], m_sg[0:1, 256:272], NE - 1.0, None, ALU.min))
                C.link(nc.vector.tensor_copy(m_sg[0:1, 271:272], end[0:1, NE - 1:NE]))
                nc.vector.tensor_copy(tasks[0:1, :], m_sg[0:1, 256:272]).then_inc(r_tab, 1)
                for t in range(T):
                    last = nc.vector.tensor_tensor(sl[:, t], ps[5][:, t * NE:(t + 1) * NE], start, ALU.add)
                C.link(last)
                for c, oh in enumerate((oh1, oh2)):
                    C.link(nc.vector.tensor_tensor(pr, oh, sl, ALU.mult))
                    C.link(nc.vector.tensor_reduce(pos[c], pr, AX.X, ALU.add))
                for n, v in enumerate(pos + gate):
                    for t in range(T):
                        last = nc.vector.tensor_scalar(m_y[:, (2 * n + t) % 8 * P:((2 * n + t) % 8 + 1) * P], ident,
                                                       v[:, t:t + 1], None, ALU.mult)
                last.then_inc(r_diag, 1)
                nc.vector.tensor_scalar(m_128, iota_col, 0.0, float(P), ALU.mult, ALU.add)
                C.link(nc.vector.tensor_copy(slot_id, iota_col))
                split_lo(dve, M0)
                split_lo(dve, M0 + 1)

                def pick():
                    for t in range(T):
                        nc.vector.tensor_scalar(m_pt[:, t, :], iota_row, pos[0][:, t:t + 1], None, ALU.is_equal)
                    for t in range(T):
                        last = nc.vector.tensor_scalar(m_p[:, t, :], iota_row, pos[1][:, t:t + 1], None, ALU.is_equal)
                    return last

                def pick_sum():
                    return nc.vector.tensor_tensor(m_p, m_p, m_pt, ALU.add)

                def tokens_lo(i):
                    for b in range(2):
                        dve.wait_ge(m_ahi, 2 * i + b + 1)
                        for c in range(4 * b, 4 * b + 4):
                            last = nc.vector.scalar_tensor_tensor(
                                a0_lo[:, c, 0:P], ps[6 + b][:, (c % 4) * P:(c % 4 + 1) * P],
                                vec[:, V_MOE + c:V_MOE + c + 1], a0_hi[:, c, 0:P].bitcast(F32), ALU.mult, ALU.subtract)
                    last.then_inc(m_alo, 1)

                def product_lo(n):
                    dve.wait_ge(m_phi, n + 1)
                    nc.vector.tensor_tensor(a1_lo[:, 0:4, 0:P], ps[0][:, :].rearrange("p (c s) -> p c s", c=4),
                                            a1_hi[:, 0:4, 0:P].bitcast(F32), ALU.subtract).then_inc(m_plo, 1)

                def product(n, up_used):
                    dve.wait_ge(m_silu, n + 1)
                    dve.wait_ge(unit_used, up_used)
                    nc.vector.tensor_tensor(m_act, m_sg, ps[3][:, :], ALU.mult).then_inc(m_mult, 1)

                C.link(pick())
                pick_sum().then_inc(m_pk, 1)
                dve.wait_ge(m_pk, 1)
                tokens_lo(0)
                dve.wait_ge(r_g, 1)
                n_tasks = dve.value_load(tasks[0:1, 15:16], min_val=1, max_val=MAX_TASKS)
                with dve.Fori(0, n_tasks) as i:
                    split_lo(dve, M0 + 2, 7 * i)
                    split_lo(dve, M0 + 3, 7 * i)
                    split_lo(dve, M0 + 4, 7 * i)
                    split_lo(dve, M0 + 5, 7 * i)
                    product(7 * i, used(M0 + 3, 7 * i))
                    with dve.Fori(1, 7) as j:
                        n = 7 * i + j
                        split_lo(dve, M0, n)
                        split_lo(dve, M0 + 1, n)
                        product_lo(n - 1)
                        for u in range(2, 6):
                            split_lo(dve, M0 + u, n)
                        product(n, used(M0 + 1, n))
                    n = 7 * i + 6
                    tokens_lo(i + 1)
                    product_lo(n)
                    split_lo(dve, M0, n + 1)
                    split_lo(dve, M0 + 1, n + 1)
                    dve.wait_ge(m_scat, i + 1)
                    for t in range(T):
                        for half in range(2):
                            at = slice(half * 512, (half + 1) * 512)
                            nc.vector.tensor_tensor(x[:, t, at], x[:, t, at], ps[SCAT[2 * t + half]][:, :],
                                                    ALU.add).then_inc(x_new, 1)
                norm_dve(dve, "final", C)
                dve.wait_ge(pool_in, 32)
                for t in range(T):
                    last = nc.vector.scalar_tensor_tensor(fin_o[:, t, :], x[:, t, :], rstd[:, t:t + 1], fin_w,
                                                          ALU.mult, ALU.mult)
                last.then_inc(fin_done, 1)

        @block.tensor
        def _(pe):
            pe.wait_ge(s_const, N_CONST)
            pe.wait_ge(s_vrow, 16 * 17)
            nc.tensor.transpose(ps[7][:, 0:VA_N], vrow[0:VA_N, 0, :], ident[0:VA_N, 0:VA_N])
            nc.tensor.transpose(ps[7][:, P:P + VB_N], vrow[0:VB_N, 1, :], ident[0:VB_N, 0:VB_N])
            nc.tensor.transpose(ps[7][:, 2 * P:3 * P], vrow[:, 2, :], ident).then_inc(s_vecT, 1)
            pe.wait_ge(h_ready, 1)
            turn_pe(pe, "mix", h, DC)

            u0 = UNIT["in"]
            for b in range(3):
                mm_rows(pe, u0 + 2 * b, ps[2 * b:2 * b + 2], turn="mix" if b == 0 else None)
            for b in range(3, 6):
                pe.wait_ge(z_act, b - 2)
                pe.wait_ge(z_dve, b - 2)
                mm_rows(pe, u0 + 2 * b, ps[2 * (b - 3):2 * (b - 3) + 2])

            def at_turn():
                pe.wait_ge(at_n, 1)
                pe.wait_ge(z_act, 6)
                pe.wait_ge(z_dve, 6)
                for c in range(5):
                    for t in range(T):
                        at = (c % 2) * S + t * P
                        last = nc.tensor.transpose(ps[4 + c // 2][:, at:at + P], at_qn[:, t, c * P:(c + 1) * P], ident)
                last.then_inc(at_T, 1)

            def at_scores(step):
                t, j, w = step // 2, step % 2, at_width(step)
                rowsj = slice(j * DH, (j + 1) * DH)
                if step == 0:
                    pe.wait_ge(at_c, 1)
                if step == 3:
                    pe.wait_ge(at_y, 1)
                for c in range(4):
                    bank, at = AT_BANKS[step][c * w // 512], c * w % 512
                    last = nc.tensor.matmul(ps[bank][:, at:at + w],
                                            at_qkT[rowsj, c, t * P:(t + 1) * P], at_qkT[rowsj, 4, 0:w],
                                            start=True, stop=True)
                last.then_inc(at_sc, 1)

            def at_turn_weights(step):
                w = at_width(step)
                pe.wait_ge(at_e, step + 1)
                for k in range(w // P):
                    for c in range(4):
                        last = nc.tensor.transpose(ps[AT_BANKS[step][k]][:, c * P:(c + 1) * P],
                                                   at_s[step][:, c * w + k * P:c * w + (k + 1) * P], ident)
                last.then_inc(at_pt, 1)

            def at_values(step):
                t, j, w = step // 2, step % 2, at_width(step)
                pe.wait_ge(at_pc, step + 1 if t else 2)
                for c in range(4):
                    for k in range(w // P):
                        last = nc.tensor.matmul(ps[AT_OUT[t]][:, j * S + c * DH:j * S + (c + 1) * DH],
                                                at_s[step][:, (4 * k + c) * P:(4 * k + c + 1) * P],
                                                z[:, k, C_VA + j * DH:C_VA + (j + 1) * DH],
                                                start=(k == 0), stop=(k == w // P - 1))
                last.then_inc(at_o, 1)

            for v in range(12, 24):
                b = v // 2
                if v % 2 == 0:
                    pe.wait_ge(z_act, b - 2 if b < 8 else b - 1)
                    pe.wait_ge(z_dve, b - 2 if b < 8 else b - 1)
                mm_rows(pe, u0 + 2 * b, ps[2 * (b % 2):2 * (b % 2) + 2], 0, min(WB, IN_W - b * WB), (v % 2,))
                if v == 12:
                    at_turn()
                if v == 14:
                    at_scores(0)
                    at_scores(1)
                if v == 15:
                    at_scores(2)
                if v == 16:
                    at_turn_weights(0)
                    at_turn_weights(1)
                if v == 17:
                    at_values(0)
                    at_values(1)
                    at_turn_weights(2)
                if v == 18:
                    at_values(2)
                if v == 19:
                    at_scores(3)
                if v == 21:
                    at_turn_weights(3)
                if v == 22:
                    at_values(3)
            pe.wait_ge(at_y, 2)
            pe.wait_ge(z_act, 12)
            pe.wait_ge(z_dve, 12)
            turn_pe(pe, "ya", ya, 4)

            pe.wait_ge(turn_lo, TURN["ya"] + 2)
            for t in range(T):
                for hh in range(HB):
                    for kk in range(2):
                        nc.tensor.transpose(ps[2 * kk + t][:, hh * P:(hh + 1) * P],
                                            z[:, t, C_QB + kk * QKB + hh * P:C_QB + kk * QKB + (hh + 1) * P], ident)
            for t in range(T):
                last = nc.tensor.transpose(ps[4][0:GKR, t * P:(t + 1) * P], z[:, t, C_GK:C_GK + GKR], ident)
            last.then_inc(gl_T, 1)
            pe.wait_ge(gl_c, 1)
            pe.wait_ge(s_small, 32)
            for hh in range(HB):
                last = nc.tensor.matmul(ps[5 + hh // 2][:, (hh % 2) * S:(hh % 2 + 1) * S], wgk[:, hh * P:(hh + 1) * P],
                                        g_lrT[0:GKR, :, :].rearrange("p t i -> p (t i)"), start=True, stop=True)
            last.then_inc(gl_g, 1)
            for t in range(T):
                for hh in range(HB):
                    last = nc.tensor.matmul(ps[t][:, hh * P:(hh + 1) * P], g_k[:, t, hh, :], g_q[:, t, hh, :],
                                            start=True, stop=True)
                last.then_inc(gl_a, 1)
            for n in range(T * LEVELS):
                pe.wait_ge(gl_p, n + 1)
                if n >= 2:
                    pe.wait_ge(gl_m, n - 1)
                for hh in range(HB):
                    last = nc.tensor.matmul(ps[(n + 2) % 4][:, hh * P:(hh + 1) * P], g_f[n % 4][:, hh, :],
                                            g_f[n % 4][:, hh, :], start=True, stop=True)
                last.then_inc(gl_a, 1)
            pe.wait_ge(gl_k, 1)
            for hh in range(HB):
                last = nc.tensor.transpose(ps[4][:, hh * P:(hh + 1) * P], g_e[:, 0, hh, :], ident)
            last.then_inc(gl_kT, 1)
            pe.wait_ge(gl_kc, 1)
            for hh in range(HB):
                last = nc.tensor.matmul(ps[5 + hh // 2][:, (hh % 2) * DVB:(hh % 2 + 1) * DVB], g_kdT[:, hh, :],
                                        z[:, 0, C_VB + hh * DVB:C_VB + (hh + 1) * DVB], start=True, stop=True)
            last.then_inc(gl_s, 1)
            pe.wait_ge(gl_m, T * LEVELS + 2)
            pe.wait_ge(gl_sc, 1)
            for t in range(T):
                for hh in range(HB):
                    o = ps[4 + 2 * t + hh // 2][:, (hh % 2) * DVB:(hh % 2 + 1) * DVB]
                    last = nc.tensor.matmul(o, g_acc[:, t, hh, :], z[:, t, C_VB + hh * DVB:C_VB + (hh + 1) * DVB],
                                            start=True, stop=(t == 0))
                    if t:
                        last = nc.tensor.matmul(o, g_e[:, 1, hh, :], g_s0[:, hh, :], start=False, stop=True)
            last.then_inc(gl_o, 1)
            pe.wait_ge(gl_yb, 1)
            turn_pe(pe, "yb", g_o, DC)

            for k in range(2):
                mm_down(pe, UNIT["wa"] + k, a1_hi[:, 2 * k:2 * k + 2], a1_lo[:, 2 * k:2 * k + 2], ps[4:8], k == 0, k == 1)
            pe.wait_ge(turn_lo, TURN["yb"] + 4)
            for k in range(4):
                mm_down(pe, UNIT["wb"] + k, a0_hi[:, 2 * k:2 * k + 2], a0_lo[:, 2 * k:2 * k + 2], ps[0:4], k == 0, k == 3)
            pe.wait_ge(br_m, 1)
            turn_pe(pe, "merged", merged, DC)
            for k in range(4):
                pe.wait_ge(turn_lo, TURN["merged"] + k + 1)
                mm_down(pe, UNIT["wo"] + k, a1_hi[:, 2 * k:2 * k + 2], a1_lo[:, 2 * k:2 * k + 2], ps[4:8], k == 0, k == 3)

            def two_to_a_bank(b0):
                return [ps[b0 + f // 2][:, (f % 2) * S:(f % 2 + 1) * S] for f in range(4)]

            def ffn(f):
                u0 = UNIT[f"ffn{f}"]
                pe.wait_ge(h_ready, 2 + 2 * f)
                turn_pe(pe, f"ffn{f}", h, DC)
                gate, up = two_to_a_bank(0), two_to_a_bank(2)

                def down(u, i, first, last, rounds=0):
                    if first is not None:
                        pe.wait_ge(f_lo, 6 * f + i + 1)
                    mm_down(pe, u, a1_hi[:, 0:2], a1_lo[:, 0:2], ps[4:8], first is True, False, rounds)
                    mm_down(pe, u + 1, a1_hi[:, 2:4], a1_lo[:, 2:4], ps[4:8], False, False, rounds)

                def gate_free(i):
                    pe.wait_ge(f_conv, i) if f == 0 else pe.wait_ge(f_silu, 6 * f + i)

                mm_cols(pe, u0, gate, turn=f"ffn{f}")
                mm_cols(pe, u0 + 2, up)
                def body(i, rounds, first):
                    gate_free(i + 1)
                    mm_cols(pe, u0 + 4, gate, rounds)
                    down(u0 + 6, i, first, False, rounds)
                    pe.wait_ge(f_mult, 6 * f + i + 1)
                    mm_cols(pe, u0 + 8, up, rounds)

                body(0, 0, True)
                with pe.Fori(1, 4) as i:
                    body(i, i, False)
                gate_free(5)
                pe.wait_ge(f_mult, 6 * f + 5)
                mm_cols(pe, u0 + 28, [gate[0], gate[1], up[0], up[1]])
                down(u0 + 30, 4, False, False)
                pe.wait_ge(f_lo, 6 * f + 6)
                mm_down(pe, u0 + 32, a1_hi[:, 4:6], a1_lo[:, 4:6], ps[4:8], False, True)

            if level >= 1:
                ffn(0)
            if level >= 2:
                pe.wait_ge(h_ready, 3)
                pe.wait_ge(pl_ready, 1)
                for g in range(4):
                    for c in (2 * g, 2 * g + 1):
                        at = (c % 2) * S
                        nc.tensor.matmul(ps[g][:, at:at + S], h[:, 0, c * P:(c + 1) * P], p_band[:, g, 0:S],
                                         start=(c % 2 == 0), stop=False, skip_group_check=True)
                        last = nc.tensor.matmul(ps[g][:, at + P:at + S], h[:, 1, c * P:(c + 1) * P], p_band[:, g, S:3 * P],
                                                start=False, stop=True, skip_group_check=True)
                    last.then_inc(turned, 1)
                u = UNIT["pool"]
                pe.wait_ge(lo_done, u + 1)
                pe.wait_ge(turn_lo, TURN["pooled"] + 4)
                for t in range(T):
                    for g in range(4):
                        for k in range(2):
                            c = 2 * g + k
                            cols = slice(c * 256, (c + 1) * 256)
                            last = mm3(ps[4 + 2 * t + g // 2][:, (g % 2) * 256:(g % 2 + 1) * 256],
                                       a1_hi[:, c, t * P:(t + 1) * P], a1_lo[:, c, t * P:(t + 1) * P],
                                       w_hi[:, u % SPL, cols], w_lo[:, u % SPL, cols], k == 0, k == 1)
                last.then_inc(unit_used, 1)
            if level >= 3:
                ffn(1)
            if level >= 4:
                D0, X0, Z0, O0 = UNIT["dt"], UNIT["xbc"], UNIT["z"], UNIT["sout"]
                pe.wait_ge(h_ready, 5)
                turn_pe(pe, "ssd", h, DC)
                pe.wait_ge(turn_lo, TURN["ssd"] + 4)
                pe.wait_ge(lo_done, D0 + 1)
                for t in range(T):
                    for kc in range(DC):
                        cols = slice(kc * NH, (kc + 1) * NH)
                        last = mm3(ps[6][:, t * NH:(t + 1) * NH], a0_hi[:, kc, t * P:(t + 1) * P],
                                   a0_lo[:, kc, t * P:(t + 1) * P], w_hi[:, D0 % SPL, cols], w_lo[:, D0 % SPL, cols],
                                   kc == 0, kc == DC - 1)
                last.then_inc(unit_used, 1)
                pairs = [two_to_a_bank(2 * b) for b in range(3)]
                for b in range(3):
                    mm_cols(pe, X0 + 2 * b, pairs[b])
                with pe.Fori(1, 2) as i:
                    for b in range(3):
                        pe.wait_ge(c_conv, 3 * i + (b - 2))
                        mm_cols(pe, X0 + 2 * b, pairs[b], i)
                for b in range(6, 8):
                    pe.wait_ge(c_conv, b - 2)
                    mm_cols(pe, X0 + 2 * b, pairs[b % 3])
                pe.wait_ge(sd_dta, 1)
                nc.tensor.matmul(ps[7][:, 0:64], upper, dta, start=True, stop=True)
                nc.tensor.matmul(ps[7][:, 64:128], ones, dta, start=True, stop=True).then_inc(sd_acs, 1)
                pe.wait_ge(c_silu, 8)
                for r in range(10):
                    if r >= 4:
                        pe.wait_ge(xt_dve if r % 2 else xt_act, (r - 4) // 2 + 1)
                    t, c0 = (r // 4, 4 * (r % 4)) if r < 8 else (0, 16 + 4 * (r - 8))
                    for c in range(4):
                        last = nc.tensor.transpose(ps[r % 4][:, c * P:(c + 1) * P], cv[:, c0 + c, t * P:(t + 1) * P], ident)
                    last.then_inc(xt_ps, 1)
                pe.wait_ge(sd_te, 1)
                for b in range(4):
                    if b >= 2:
                        pe.wait_ge(zs_done, b - 1)
                    mm_rows(pe, Z0 + 2 * b, ps[4 + 2 * (b % 2):6 + 2 * (b % 2)])
                pe.wait_ge(xt_act, 5)
                pe.wait_ge(xt_dve, 5)
                pe.wait_ge(zs_done, 4)

                def tile_weights(k):
                    g, t = k // 2, k % 2
                    if k >= 2:
                        pe.wait_ge(st_ex, k - 1)
                        pe.wait_ge(st_cb, k - 1)
                    for r in range(HPG):
                        hd = t * NH + HPG * g + r
                        nc.tensor.matmul(ps[k % 2][:, r * P:(r + 1) * P], dta[:, hd:hd + 1].to_broadcast([P, P]), upper,
                                         start=True, stop=True)
                    nc.tensor.matmul(ps[2 + k % 2][:, 0:P], cv[:, 16 + g, t * P:(t + 1) * P],
                                     cv[:, 24 + g, t * P:(t + 1) * P], start=True, stop=True).then_inc(st_seg, 1)

                def tile_output(k):
                    g, t = k // 2, k % 2
                    pe.wait_ge(st_xd, 3 * g + (2 if t == 0 else 3))
                    if t:
                        pe.wait_ge(st_sc, g + 1)
                        if g:
                            pe.wait_ge(st_acc, k - 1)
                        nc.tensor.matmul(ps[7][:, 0:256], cv[:, 24 + g, P:S], s_st.rearrange("p r e -> p (r e)"),
                                         start=True, stop=True)
                    else:
                        nc.tensor.matmul(ps[6][:, 0:256], s_b0[:, g, :], s_xe.rearrange("p r e -> p (r e)"),
                                         start=True, stop=True).then_inc(st_s, 1)
                    pe.wait_ge(st_w, k + 1)
                    if k >= 2:
                        pe.wait_ge(st_acc, k - 1)
                    for r in range(HPG):
                        last = nc.tensor.matmul(ps[4 + k % 2][:, r * HD:(r + 1) * HD], s_ex[k % 2][:, r, :], s_xd[k % 2][:, r, :],
                                                start=True, stop=True)
                    last.then_inc(st_y, 1)

                tile_weights(0)
                tile_weights(1)
                for k in range(2 * NG):
                    tile_output(k)
                    if k + 2 < 2 * NG:
                        tile_weights(k + 2)
                pe.wait_ge(sy_done, 1)
                turn_pe(pe, "y", xs, 2 * DC)
                for k in range(8):
                    pe.wait_ge(turn_lo, TURN["y"] + k + 1)
                    hi, lo = (a0_hi, a0_lo) if k < 4 else (a1_hi, a1_lo)
                    at = slice(2 * (k % 4), 2 * (k % 4) + 2)
                    mm_down(pe, O0 + k, hi[:, at], lo[:, at], ps[4:8], k == 0, k == 7)
            if level >= 5:
                M0 = UNIT["moe"]
                pe.wait_ge(h_ready, 6)
                for b in range(4):
                    for c in (2 * b, 2 * b + 1):
                        for t in range(T):
                            at = (c % 2) * S + t * P
                            last = nc.tensor.transpose(ps[b][:, at:at + P], h[:, t, c * P:(c + 1) * P], ident)
                    last.then_inc(r_T, 1)
                pe.wait_ge(r_h, 4)
                for t in range(T):
                    for c in range(DC):
                        last = nc.tensor.matmul(ps[4][:, t * NE:(t + 1) * NE], m_hT[:, c, t * P:(t + 1) * P], wr[:, c, :],
                                                start=(c == 0), stop=(c == DC - 1))
                last.then_inc(r_lg, 1)
                pe.wait_ge(r_m, 1)
                sel = m_rt[:, 5, :]
                nc.tensor.matmul(ps[5][:, 0:NE], upper, sel[:, 0:NE], start=True, stop=True)
                nc.tensor.matmul(ps[5][:, NE:2 * NE], upper, sel[:, NE:2 * NE], start=True, stop=False)
                nc.tensor.matmul(ps[5][:, NE:2 * NE], ones, sel[:, 0:NE], start=False, stop=True)
                nc.tensor.matmul(ps[5][:, 2 * NE:3 * NE], ones, sel[:, 0:NE], start=True, stop=False)
                nc.tensor.matmul(ps[5][:, 2 * NE:3 * NE], ones, sel[:, NE:2 * NE], start=False,
                                 stop=True).then_inc(r_rank, 1)
                pe.wait_ge(r_diag, 1)
                for n in range(4):
                    for t in range(T):
                        last = nc.tensor.matmul(ps[2 + n // 2][:, (n % 2) * S + t * P:(n % 2) * S + (t + 1) * P], ones,
                                                m_y[:, (2 * n + t) * P:(2 * n + t + 1) * P], start=True, stop=True)
                last.then_inc(r_bc, 1)

                def gather(i):
                    pe.wait_ge(m_pk, i + 1)
                    for c in range(DC):
                        for t in range(T):
                            last = nc.tensor.matmul(ps[6 + c // 4][:, (c % 4) * P:(c % 4 + 1) * P],
                                                    h[:, t, c * P:(c + 1) * P], m_p[:, t, :],
                                                    start=(t == 0), stop=(t == T - 1))
                    last.then_inc(m_gather, 1)

                def project(u, bank, rounds):
                    for half in range(2):
                        pe.wait_ge(lo_done, RAW * rounds + (M0 + u + half + 1))
                        slot = (M0 + u + half) % SPL
                        for k in range(4):
                            kc = 4 * half + k
                            cols = slice(k * WB, (k + 1) * WB)
                            last = mm3(bank[:, :], a0_hi[:, kc, 0:P], a0_lo[:, kc, 0:P], w_hi[:, slot, cols],
                                       w_lo[:, slot, cols], kc == 0, kc == DC - 1)
                        last.then_inc(unit_used, 1)

                def turn_product(n):
                    pe.wait_ge(m_mult, n + 1)
                    for c in range(4):
                        last = nc.tensor.transpose(ps[0][:, c * P:(c + 1) * P], m_act[:, c * P:(c + 1) * P], ident)
                    last.then_inc(m_tr, 1)

                def down(u, n, rounds, first, last):
                    pe.wait_ge(m_plo, n + 1)
                    for half in range(2):
                        mm_down(pe, M0 + u + half, a1_hi[:, 2 * half:2 * half + 2], a1_lo[:, 2 * half:2 * half + 2],
                                ps[4:6], first and half == 0, last and half == 1, rounds, tiles=1)

                gather(0)
                pe.wait_ge(r_g, 1)
                pe.wait_ge(r_tab, 1)
                n_tasks = pe.value_load(tasks[0:1, 15:16], min_val=1, max_val=MAX_TASKS)
                with pe.Fori(0, n_tasks) as i:
                    pe.wait_ge(m_alo, i + 1)
                    project(0, ps[2], 7 * i)
                    project(2, ps[3], 7 * i)
                    pe.wait_ge(x_new, 4 * i + UPD["ssd"])

                    def body(n, first):
                        pe.wait_ge(m_silu, n)
                        project(4 - RAW, ps[2], n)
                        turn_product(n - 1)
                        project(6 - RAW, ps[3], n)
                        down(8 - RAW, n - 1, n, first, False)

                    body(7 * i + 1, True)
                    gather(i + 1)
                    with pe.Fori(2, 7) as j:
                        body(7 * i + j, False)
                    n = 7 * i + 6
                    turn_product(n)
                    down(4, n, n, False, True)
                    pe.wait_ge(m_alo, i + 2)
                    pe.wait_ge(m_y_done, i + 1)
                    pe.wait_ge(m_pk, i + 2)
                    for t in range(T):
                        for half in range(2):
                            last = nc.tensor.matmul(ps[SCAT[2 * t + half]][:, :], m_gt[:, t * P:(t + 1) * P],
                                                    m_y[:, half * 512:(half + 1) * 512], start=True, stop=True)
                    last.then_inc(m_scat, 1)


STOP = "all"
_INS = ["x", "ln_mix_g", "w_in", "q_norm_g", "k_norm_g", "sinks", "w_gk_up", "b_gk", "gla_norm_g", "w_branch_a",
        "w_branch_b", "w_out", "ln_ffn_g", "w_ffn_in", "conv_w", "conv_b", "w_ffn_out", "pool_norm_w_2", "pool_w_2",
        "pool_scale_2", "dense_norm_w_2", "dense_w_gate_2", "dense_w_up_2", "dense_w_down_2", "ssd_norm_w_2",
        "ssd_w_in_2", "ssd_conv_w_2", "ssd_conv_b_2", "ssd_dt_bias_2", "ssd_a_log_2", "ssd_d_2",
        "ssd_gate_norm_w_2", "ssd_w_out_2", "moe_norm_w_2", "moe_w_router_2", "moe_w_gate_2", "moe_w_up_2",
        "moe_w_down_2", "final_norm_w_2"]


def kernel(**inputs):
    import numpy as _np
    import concourse.bacc as _bacc
    from concourse import mybir as _mybir
    from concourse.bass_utils import run_bass_kernel_spmd as _run

    nc = _bacc.Bacc("TRN2", target_bir_lowering=False, num_devices=1)
    arrays, aps = {}, {}
    for name in _INS:
        a = _np.ascontiguousarray(inputs[name])
        arrays[f"in_{name}_dram"] = a
        aps[name] = nc.dram_tensor(f"in_{name}_dram", a.shape, _mybir.dt.from_np(a.dtype), kind="ExternalInput").ap()
    out = nc.dram_tensor("out_0_dram", (1, S, D), _mybir.dt.from_np(_np.dtype("float32")), kind="ExternalOutput").ap()
    block_kernel(nc, aps, out, stop=STOP)
    r = _run(nc, [arrays], core_ids=[0])
    return r.results[0]["out_0_dram"]
```
